# Optimizing a Trainium2 kernel written in Bass

```python
import math
import jax, jax.numpy as jnp
from jax import lax
import numpy as np

D_MODEL = 1024
BATCH = 1
SEQ = 256
DEPTH = 2

N_HEADS = 8
HEAD_DIM = 64
QK_WIDTH = 2 * N_HEADS * HEAD_DIM
V_WIDTH = N_HEADS * 2 * HEAD_DIM
Q_BLOCK = 128
ATTN_SCALE = HEAD_DIM ** -0.5
CONV_WIDTH = 31
D_FF = 3584
N_EXPERTS = 8
TOP_K = 2
PLE_DIM = 256
N_EVEN = (DEPTH + 1) // 2
N_ODD = DEPTH // 2
NORM_EPS = 1e-6
LN_EPS = 1e-5

kernel_name = 'hybrid_diffattn_conformer_moe_ple'

def rms_norm(x, g):
    xf = x.astype(jnp.float32)
    y = xf * lax.rsqrt(jnp.mean(xf * xf, axis=-1, keepdims=True) + NORM_EPS)
    return (y * g.astype(jnp.float32)).astype(x.dtype)

def layer_norm(x, g, b):
    xf = x.astype(jnp.float32)
    mu = jnp.mean(xf, axis=-1, keepdims=True)
    xc = xf - mu
    y = xc * lax.rsqrt(jnp.mean(xc * xc, axis=-1, keepdims=True) + LN_EPS)
    return (y * g.astype(jnp.float32) + b.astype(jnp.float32)).astype(x.dtype)

def diff_attention(h, w_qkv, w_o, g_q, g_k, lam_q1, lam_k1, lam_q2, lam_k2, g_sub, lambda_init):
    B, S, _ = h.shape
    qkv = h @ w_qkv
    q, k, v = jnp.split(qkv, [QK_WIDTH, 2 * QK_WIDTH], axis=-1)
    q = rms_norm(q.reshape(B, S, N_HEADS, 2, HEAD_DIM), g_q)
    k = rms_norm(k.reshape(B, S, N_HEADS, 2, HEAD_DIM), g_k)
    vf = v.reshape(B, S, N_HEADS, 2 * HEAD_DIM).astype(jnp.float32)
    f32 = jnp.float32
    lam = (jnp.exp(jnp.sum(lam_q1.astype(f32) * lam_k1.astype(f32)))
           - jnp.exp(jnp.sum(lam_q2.astype(f32) * lam_k2.astype(f32)))
           + lambda_init)
    n_blocks = S // Q_BLOCK
    q_blocks = q.reshape(B, n_blocks, Q_BLOCK, N_HEADS, 2, HEAD_DIM).transpose(1, 0, 2, 3, 4, 5)
    starts = jnp.arange(n_blocks, dtype=jnp.int32) * Q_BLOCK
    k_pos = jnp.arange(S, dtype=jnp.int32)

    def block(args):
        qi, start = args
        s = jnp.einsum('bqhcd,bkhcd->bhcqk', qi, k,
                       preferred_element_type=jnp.float32) * ATTN_SCALE
        q_pos = start + jnp.arange(Q_BLOCK, dtype=jnp.int32)
        causal = k_pos[None, :] <= q_pos[:, None]
        s = jnp.where(causal, s, -jnp.inf)
        a = jax.nn.softmax(s, axis=-1)
        a = a[:, :, 0] - lam * a[:, :, 1]
        return jnp.einsum('bhqk,bkhe->bqhe', a, vf)

    o = lax.map(block, (q_blocks, starts))
    o = o.transpose(1, 0, 2, 3, 4).reshape(B, S, N_HEADS, 2 * HEAD_DIM)
    o = rms_norm(o, g_sub) * (1.0 - lambda_init)
    return o.reshape(B, S, V_WIDTH).astype(h.dtype) @ w_o

def conformer_conv(h, w_pw1, b_pw1, w_dw, b_dw, ln_g, ln_b, w_pw2, b_pw2):
    u = h @ w_pw1 + b_pw1
    a, g = jnp.split(u, 2, axis=-1)
    u = a * jax.nn.sigmoid(g)
    u = lax.conv_general_dilated(
        u, w_dw[:, None, :].astype(u.dtype), window_strides=(1,),
        padding=[(CONV_WIDTH - 1, 0)],
        dimension_numbers=('NWC', 'WIO', 'NWC'),
        feature_group_count=D_MODEL) + b_dw
    u = jax.nn.silu(layer_norm(u, ln_g, ln_b))
    return u @ w_pw2 + b_pw2

def swiglu(h, w_gate, w_up, w_down):
    return (jax.nn.silu(h @ w_gate) * (h @ w_up)) @ w_down

def moe_swiglu(h, w_router, b_router, w_gate, w_up, w_down):
    logits = (h @ w_router).astype(jnp.float32) + b_router.astype(jnp.float32)
    top_vals, top_idx = lax.top_k(logits, TOP_K)
    top_w = jax.nn.softmax(top_vals, axis=-1)
    gates = jnp.sum(jax.nn.one_hot(top_idx, N_EXPERTS, dtype=jnp.float32)
                    * top_w[..., None], axis=-2).astype(h.dtype)
    out = jnp.zeros_like(h)
    for e in range(N_EXPERTS):
        out = out + gates[..., e:e + 1] * swiglu(h, w_gate[e], w_up[e], w_down[e])
    return out

def _normal(key, shape, scale):
    return jax.random.normal(key, shape, jnp.float32) * scale

def setup_inputs(seed: int = 0) -> dict:
    key = jax.random.key(seed)
    ks = jax.random.split(key, 34)
    D = D_MODEL
    return {
        'x': _normal(ks[0], (BATCH, SEQ, D), 1.0),
        'p': _normal(ks[1], (DEPTH, BATCH, SEQ, PLE_DIM), 1.0),
        'mix_norm_g': 1.0 + _normal(ks[2], (DEPTH, D), 0.02),
        'ffn_norm_g': 1.0 + _normal(ks[3], (DEPTH, D), 0.02),
        'attn_w_qkv': _normal(ks[4], (N_EVEN, D, 2 * QK_WIDTH + V_WIDTH), D ** -0.5),
        'attn_w_o': _normal(ks[5], (N_EVEN, V_WIDTH, D), V_WIDTH ** -0.5),
        'attn_g_q': 1.0 + _normal(ks[6], (N_EVEN, 2, HEAD_DIM), 0.02),
        'attn_g_k': 1.0 + _normal(ks[7], (N_EVEN, 2, HEAD_DIM), 0.02),
        'attn_lam_q1': _normal(ks[8], (N_EVEN, HEAD_DIM), 0.1),
        'attn_lam_k1': _normal(ks[9], (N_EVEN, HEAD_DIM), 0.1),
        'attn_lam_q2': _normal(ks[10], (N_EVEN, HEAD_DIM), 0.1),
        'attn_lam_k2': _normal(ks[11], (N_EVEN, HEAD_DIM), 0.1),
        'attn_g_sub': 1.0 + _normal(ks[12], (N_EVEN, 2 * HEAD_DIM), 0.02),
        'conv_w_pw1': _normal(ks[13], (N_ODD, D, 2 * D), D ** -0.5),
        'conv_b_pw1': _normal(ks[14], (N_ODD, 2 * D), 0.02),
        'conv_w_dw': _normal(ks[15], (N_ODD, CONV_WIDTH, D), CONV_WIDTH ** -0.5),
        'conv_b_dw': _normal(ks[16], (N_ODD, D), 0.02),
        'conv_ln_g': 1.0 + _normal(ks[17], (N_ODD, D), 0.02),
        'conv_ln_b': _normal(ks[18], (N_ODD, D), 0.02),
        'conv_w_pw2': _normal(ks[19], (N_ODD, D, D), D ** -0.5),
        'conv_b_pw2': _normal(ks[20], (N_ODD, D), 0.02),
        'ffn_w_gate': _normal(ks[21], (N_EVEN, D, D_FF), D ** -0.5),
        'ffn_w_up': _normal(ks[22], (N_EVEN, D, D_FF), D ** -0.5),
        'ffn_w_down': _normal(ks[23], (N_EVEN, D_FF, D), D_FF ** -0.5),
        'moe_w_router': _normal(ks[24], (N_ODD, D, N_EXPERTS), D ** -0.5),
        'moe_b_router': _normal(ks[25], (N_ODD, N_EXPERTS), 0.01),
        'moe_w_gate': _normal(ks[26], (N_ODD, N_EXPERTS, D, D_FF), D ** -0.5),
        'moe_w_up': _normal(ks[27], (N_ODD, N_EXPERTS, D, D_FF), D ** -0.5),
        'moe_w_down': _normal(ks[28], (N_ODD, N_EXPERTS, D_FF, D), D_FF ** -0.5),
        'ple_w_proj': _normal(ks[29], (DEPTH, PLE_DIM, D), PLE_DIM ** -0.5),
        'ple_norm_g': 1.0 + _normal(ks[30], (DEPTH, D), 0.02),
        'ple_gate_norm_g': 1.0 + _normal(ks[31], (DEPTH, D), 0.02),
        'ple_w_gate': _normal(ks[32], (DEPTH, D, D), D ** -0.5),
    }

def reference(x, p, mix_norm_g, ffn_norm_g, attn_w_qkv, attn_w_o, attn_g_q, attn_g_k,
              attn_lam_q1, attn_lam_k1, attn_lam_q2, attn_lam_k2, attn_g_sub,
              conv_w_pw1, conv_b_pw1, conv_w_dw, conv_b_dw, conv_ln_g, conv_ln_b,
              conv_w_pw2, conv_b_pw2, ffn_w_gate, ffn_w_up, ffn_w_down,
              moe_w_router, moe_b_router, moe_w_gate, moe_w_up, moe_w_down,
              ple_w_proj, ple_norm_g, ple_gate_norm_g, ple_w_gate):
    for i in range(DEPTH):
        j = i // 2
        h = rms_norm(x, mix_norm_g[i])
        if i % 2 == 0:
            lambda_init = 0.8 - 0.6 * math.exp(-0.3 * i)
            x = x + diff_attention(h, attn_w_qkv[j], attn_w_o[j], attn_g_q[j], attn_g_k[j],
                                   attn_lam_q1[j], attn_lam_k1[j], attn_lam_q2[j],
                                   attn_lam_k2[j], attn_g_sub[j], lambda_init)
        else:
            x = x + conformer_conv(h, conv_w_pw1[j], conv_b_pw1[j], conv_w_dw[j], conv_b_dw[j],
                                   conv_ln_g[j], conv_ln_b[j], conv_w_pw2[j], conv_b_pw2[j])
        h = rms_norm(x, ffn_norm_g[i])
        if i % 2 == 0:
            x = x + swiglu(h, ffn_w_gate[j], ffn_w_up[j], ffn_w_down[j])
        else:
            x = x + moe_swiglu(h, moe_w_router[j], moe_b_router[j],
                               moe_w_gate[j], moe_w_up[j], moe_w_down[j])
        e = rms_norm(p[i] @ ple_w_proj[i], ple_norm_g[i])
        gate = jax.nn.sigmoid(rms_norm(x, ple_gate_norm_g[i]) @ ple_w_gate[i])
        x = x + gate * e
    return x


_drawn_inputs = setup_inputs


def setup_inputs(seed=0):
    import zlib

    import numpy as np

    out = dict(_drawn_inputs(seed))
    spreads = {}
    factors = {'attn_g_q': 3.215,
     'attn_g_k': 2.838,
     'attn_lam_k1': 5.923,
     'attn_lam_q2': 8.0,
     'attn_g_sub': 8.185,
     'conv_b_pw1': 16.524,
     'conv_b_dw': 9.254,
     'conv_ln_b': 18.328,
     'conv_b_pw2': 11.808,
     'moe_b_router': 12.682,
     'ple_norm_g': 46.787,
     'ple_gate_norm_g': 30.373,
     'ffn_norm_g': 4.997,
     'conv_ln_g': 48.831}
    for name, (base, spread) in spreads.items():
        noise = np.random.default_rng([zlib.crc32(name.encode()), seed]).standard_normal(out[name].shape)
        drawn = base * np.exp(spread * noise) if base else spread * noise
        out[name] = __import__('jax').numpy.asarray(drawn.astype(out[name].dtype))
    for name, factor in factors.items():
        out[name] = (out[name] * factor).astype(out[name].dtype)
    return out
```

```python
from contextlib import ExitStack

import concourse.bass as bass
from concourse import mybir

F32 = mybir.dt.float32
F32R = mybir.dt.float32r
I32 = mybir.dt.int32
ACT = mybir.ActivationFunctionType
ALU = mybir.AluOpType
AX = mybir.AxisListType.X

P = 128
CW = 512
UNIT = 2 * CW
N_CONSTS = 18
RING = 14
SPLIT = 4


def program(nc, x, p, mix_norm_g, ffn_norm_g, attn_w_qkv, attn_w_o, attn_g_q, attn_g_k,
            attn_lam_q1, attn_lam_k1, attn_lam_q2, attn_lam_k2, attn_g_sub,
            conv_w_pw1, conv_b_pw1, conv_w_dw, conv_b_dw, conv_ln_g, conv_ln_b,
            conv_w_pw2, conv_b_pw2, ffn_w_gate, ffn_w_up, ffn_w_down,
            moe_w_router, moe_b_router, moe_w_gate, moe_w_up, moe_w_down,
            ple_w_proj, ple_norm_g, ple_gate_norm_g, ple_w_gate, out):
    _, S, D = x.shape
    T = S // P
    KT = D // P
    FF = ffn_w_gate.shape[2]
    STEPS = FF // CW
    NE = moe_w_router.shape[2]
    H = attn_w_o.shape[1] // P
    HD = P // 2
    TAPS = conv_w_dw.shape[1]
    NQKV = attn_w_qkv.shape[2] // CW
    NO = D // CW
    MAXJOBS = NE + (2 * S) // (P + 1)
    NCOL = MAXJOBS + 1
    LAM0 = 0.2
    assert (T, KT, STEPS, NE, H, NQKV, NO) == (2, 8, 7, 8, 8, 6, 2) and 3 * STEPS * 2 % RING == 0
    EPS, LN_EPS = 1e-6, 1e-5
    NEG = -1e30

    U_QKV = 0
    U_WO = U_QKV + 4 * NQKV
    U_FFN = U_WO + 4 * NO
    JOB = 3 * STEPS * 4
    U_PROJ0 = U_FFN + JOB
    U_GATE0 = U_PROJ0 + 2
    U_PW1 = U_GATE0 + 4 * NO
    U_PW2 = U_PW1 + 16
    U_MOE = U_PW2 + 4 * NO
    U_PROJ1 = U_MOE
    U_GATE1 = U_PROJ1 + 2
    U_END = U_GATE1 + 4 * NO
    C_QKV, C_WO, C_GATE0, C_PW1, C_PW2, C_GATE1 = 0, 6, 8, 10, 14, 16

    wqkv, wo = attn_w_qkv[0], attn_w_o[0]
    wpw1, wpw2 = conv_w_pw1[0], conv_w_pw2[0]

    with ExitStack() as ctx:
        def sb(name, shape, dt=F32, to=ctx):
            return to.enter_context(nc.sbuf_tensor(name, shape, dt))

        def sem(name):
            return ctx.enter_context(nc.semaphore(name))

        ring = sb("weight_ring", [P, RING, 2 * UNIT])
        whi = sb("weight_hi", [P, SPLIT, UNIT], F32R)
        wlo = sb("weight_lo", [P, SPLIT, UNIT], F32R)
        xres = sb("residual", [P, T, D])
        xn = sb("normed", [P, T, D])
        ident = sb("identity", [P, P])
        iota = sb("iota", [P, P])
        upper = sb("strict_upper", [P, P])
        ones = sb("ones", [P, P])
        vecs = sb("column_vectors", [P, 96])
        taps = sb("conv_taps", [P, TAPS * KT])
        mask = sb("causal_mask", [P, 3 * P])
        small = sb("small", [P, 160])
        wr = sb("router_raw", [P, KT, NE])
        wrhi = sb("router_hi", [P, KT, NE], F32R)
        wrlo = sb("router_lo", [P, KT, NE], F32R)
        rbias = sb("router_bias", [P, NE])
        jpos = sb("job_positions", [P, T, NCOL])
        jgate = sb("job_gates", [P, T, NCOL])
        jtab = sb("job_table", [1, 16], I32)
        with ExitStack() as o:
            ahi = sb("act_hi", [P, KT, S], F32R, o)
            alo = sb("act_lo", [P, KT, S], F32R, o)
        with ExitStack() as o:
            prob = sb("prob", [P, 2, 2, 3 * P], to=o)
            amix = sb("mixed_prob", [P, 2, 3 * P], to=o)
            amixT = sb("mixed_prob_T", [P, 2, 3 * P], to=o)
        sb("act_region", [P, 2 * KT * S])
        with ExitStack() as o:
            v_sb = sb("values", [P, T, D], to=o)
            qT = sb("q_T", [P, H, S], to=o)
            kT = sb("k_T", [P, H, S], to=o)
            lamv = sb("lambda_vectors", [P, 4, HD], to=o)
        with ExitStack() as o:
            sg = sb("silu_gate", [P, T, CW], to=o)
            hid = sb("hidden", [P, T, CW], to=o)
            hThi = sb("hidden_T_hi", [P, T, CW], F32R, o)
            hTlo = sb("hidden_T_lo", [P, T, CW], F32R, o)
            ysb = sb("expert_out", [P, D], to=o)
            sel = sb("one_hot", [P, T, P], to=o)
            selg = sb("one_hot_gated", [P, T, P], to=o)
            selT = sb("one_hot_gated_T", [P, S], to=o)
        with ExitStack() as o:
            cT = sb("conv_in_T", [P, KT, TAPS - 1 + S], to=o)
            cy = sb("conv_out_T", [P, KT, S], to=o)
            csq = sb("conv_square", [P, KT, S], to=o)
        with ExitStack() as o:
            emb = sb("embedding", [P, T, D], to=o)
            pnat = sb("p_rows", [P, T, 2 * P], to=o)
            pThi = sb("p_T_hi", [P, 2, S], F32R, o)
            pTlo = sb("p_T_lo", [P, 2, S], F32R, o)
            gbc = sb("norm_row", [P, D], to=o)
            sgm = sb("gate_sigmoid", [P, T, CW], to=o)
        sb("stage_region", [P, KT * (TAPS - 1 + S) + 2 * KT * S])

        ps = ctx.enter_context(nc.psum_tensor("psum", [P, 8, CW], F32))

        eps, lneps = small[:, 0:1], small[:, 1:2]
        ssq, std, rstd = small[:, 2:4], small[:, 4:6], small[:, 6:8]
        hsq, hstd, hrstd = small[:, 8:24], small[:, 24:40], small[:, 40:56]
        neglam, lamsum, lamexp = small[:, 56:57], small[:, 57:59], small[:, 59:61]
        gsub = small[:, 61:62]
        mx, nmx = small[:, 64:72], small[:, 72:80]
        psum_e, pinv = small[:, 80:88], small[:, 88:96]
        logits = small[:, 96:112].rearrange("p (t e) -> p t e", t=T)

        V_MIX, V_FFN, V_PLEG, V_BPW1, V_BDW, V_LNG, V_LNB, V_GQ, V_GK, V_GSUB = \
            0, 16, 32, 48, 64, 72, 80, 88, 89, 90
        NV = 91
        TAPROWS = TAPS * KT // 2
        stage_v = kT[0:NV, 0, 0:P]
        stage_t = [kT[0:TAPROWS, 1, 0:P], kT[0:TAPROWS, 2, 0:P]]

        piece_in = [sem(f"piece_in{i}") for i in range(RING)]
        hi_done = sem("hi_done")
        lo_done = sem("lo_done")
        unit_used = sem("unit_used")
        consts_in = sem("consts_in")
        x_in = sem("x_in")
        p_in = sem("p_in")
        g_in = sem("g_in")
        b_in = sem("b_in")
        masks_done = sem("masks_done")
        pool_seq = sem("pool_seq")
        vecsT_ready = sem("vecsT_ready")
        vecs_done = sem("vecs_done")
        wr_done = sem("wr_done")
        lam_part = sem("lam_part")
        ssq_a = sem("ssq_a")
        ssq_d = sem("ssq_d")
        std_done = sem("std_done")
        xn_done = sem("xn_done")
        x_done = sem("x_done")
        tp_ready = sem("tp_ready")
        ahi_done = sem("ahi_done")
        alo_done = sem("alo_done")
        chunk_free = sem("chunk_free")
        qk_sq = sem("qk_sq")
        qk_ssq = sem("qk_ssq")
        qk_std = sem("qk_std")
        qk_n = sem("qk_n")
        qkT_ready = sem("qkT_ready")
        qkT_done = sem("qkT_done")
        v_done = sem("v_done")
        s_ready = sem("scores_ready")
        sm_done = sem("masked_done")
        exp_done = sem("exp_done")
        am_done = sem("mixed_done")
        amT_ready = sem("mixedT_ready")
        amT_done = sem("mixedT_done")
        o_ready = sem("o_ready")
        o_done = sem("o_done")
        on_step = sem("o_norm_step")
        silu_done = sem("silu_done")
        h_done = sem("h_done")
        hT_ready = sem("hT_ready")
        hThi_done = sem("hThi_done")
        hTlo_done = sem("hTlo_done")
        pT_ready = sem("pT_ready")
        pThi_done = sem("pThi_done")
        pTlo_done = sem("pTlo_done")
        e_sq = sem("e_sq")
        e_std = sem("e_std")
        e_done = sem("e_done")
        sgm_done = sem("sgm_done")
        glu_sig = sem("glu_sig")
        glu_done = sem("glu_done")
        conv_done = sem("conv_done")
        mean_ready = sem("mean_ready")
        mean_done = sem("mean_done")
        cent_done = sem("centred_done")
        csq_done = sem("csq_done")
        var_ready = sem("var_ready")
        cstd_done = sem("cstd_done")
        cn_done = sem("conv_normed_done")
        cs_done = sem("conv_silu_done")
        log_ready = sem("logits_ready")
        r_step = sem("router_exp")
        rm_done = sem("route_mask_done")
        cnt_ready = sem("counts_ready")
        tab_done = sem("job_table_done")
        hg_done = sem("h_rows_done")
        sel_done = sem("one_hot_done")
        xe_ready = sem("gather_ready")
        xehi_done = sem("gather_hi_done")
        xelo_done = sem("gather_lo_done")
        selT_ready = sem("one_hot_T_ready")
        selT_done = sem("one_hot_T_done")
        y0_done = sem("y0_done")
        y1_done = sem("y1_done")
        sc_ready = sem("scatter_ready")
        sc_done = sem("scatter_added")
        dve_seq = sem("dve_seq")
        act_seq = sem("act_seq")
        stored = sem("stored")

        def after(n, per, j):
            return n if j is None else j * per + n

        class Splitter:

            def __init__(self, one):
                self.next, self.one, self.j = 0, one, None

            def to(self, n):
                while self.next < n:
                    self.one(self.next, self.j)
                    self.next += 1

        class Order:

            def __init__(self, eng, s):
                self.eng, self.s, self.n = eng, s, 0

            def add(self, ins):
                ins.then_inc(self.s, 1)
                self.n += 1
                return self.n

            def wait(self, n):
                self.eng.wait_ge(self.s, n)

            def step(self, ins):
                self.wait(self.add(ins))

        def raw(u):
            return ring[:, (u // 2) % RING, (u % 2) * UNIT:(u % 2 + 1) * UNIT]

        block = ctx.enter_context(nc.Block())

        @block.sync
        def _(sp):
            def load(piece, src, j, kt=4):
                slot = piece % RING
                if piece >= RING:
                    sp.wait_ge(lo_done, after(2 * (piece - RING) + 2, JOB, j))
                dst = ring[:, slot, :].rearrange("p (t n) -> p t n", t=kt)
                sp.dma_start(dst, src).then_inc(piece_in[slot], 16)

            def columns(first, w, chunk, j=None):
                for k in range(2):
                    load(first + k, w[k * 4 * P:(k + 1) * 4 * P, chunk * CW:(chunk + 1) * CW]
                         .rearrange("(t p) n -> p t n", p=P), j)

            def feed_forward(first, wg, wu, wd, j=None):
                def rows(at, s):
                    for half in range(2):
                        load(at + half, wd[s * CW:(s + 1) * CW, half * CW:(half + 1) * CW]
                             .rearrange("(t p) n -> p t n", p=P), j)
                at = first
                for s in range(STEPS):
                    columns(at, wg, s, j)
                    at += 2
                    if s:
                        rows(at, s - 1)
                        at += 2
                    columns(at, wu, s, j)
                    at += 2
                rows(at, STEPS - 1)

            sp.dma_start(xres[:, :, :], x[0].rearrange("(t p) d -> p t d", p=P)).then_inc(x_in, 16)
            for c in range(NQKV):
                columns((U_QKV + 4 * c) // 2, wqkv, c)
            for c in range(NO):
                columns((U_WO + 4 * c) // 2, wo, c)
            feed_forward(U_FFN // 2, ffn_w_gate[0], ffn_w_up[0], ffn_w_down[0])
            load(U_PROJ0 // 2, ple_w_proj[0].rearrange("(t p) n -> p t n", p=P), None, 2)
            for c in range(NO):
                columns((U_GATE0 + 4 * c) // 2, ple_w_gate[0], c)
            for i, c in enumerate((0, 2, 1, 3)):
                columns((U_PW1 + 4 * i) // 2, wpw1, c)
            for c in range(NO):
                columns((U_PW2 + 4 * c) // 2, wpw2, c)
            feed_forward(U_MOE // 2, moe_w_gate[0, 0], moe_w_up[0, 0], moe_w_down[0, 0])
            sp.wait_ge(tab_done, 1)
            jobs = sp.snap(sp.value_load(jtab[0:1, NCOL:NCOL + 1], min_val=NE, max_val=MAXJOBS))
            with sp.Fori(1, jobs) as j:
                e = sp.snap(sp.value_load(jtab[0:1, bass.ds(j, 1)], min_val=0, max_val=NE - 1))
                feed_forward(U_MOE // 2, *(w[0, bass.ds(e, 1), :, :].rearrange("a k n -> (a k) n")
                                           for w in (moe_w_gate, moe_w_up, moe_w_down)), j)
            load(U_PROJ1 // 2, ple_w_proj[1].rearrange("(t p) n -> p t n", p=P), jobs, 2)
            for c in range(NO):
                columns((U_GATE1 + 4 * c) // 2, ple_w_gate[1], c, jobs)
            for c in range(NO):
                sp.wait_ge(x_done, 6 + c)
                sp.dma_start(out[0].rearrange("(t p) d -> p t d", p=P)[:, :, c * CW:(c + 1) * CW],
                             xres[:, :, c * CW:(c + 1) * CW]).then_inc(stored, 16)
            sp.wait_ge(stored, 32)

        @block.gpsimd
        def _(pool):
            pool.memset(ident[:, :], 0.0).then_inc(pool_seq, 1)
            pool.memset(mask[:, :], 0.0).then_inc(pool_seq, 1)
            pool.memset(ones[:, :], 1.0).then_inc(pool_seq, 1)
            pool.wait_ge(pool_seq, 3)
            pool.affine_select(out=ident[:, :], in_=ident[:, :], compare_op=ALU.not_equal, fill=1.0,
                               base=0, pattern=[[-1, P]], channel_multiplier=1).then_inc(masks_done, 1)
            for at in (0, 2 * P):
                pool.affine_select(out=mask[:, at:at + P], in_=mask[:, at:at + P], compare_op=ALU.is_ge,
                                   fill=NEG, base=0, pattern=[[-1, P]],
                                   channel_multiplier=1).then_inc(masks_done, 1)
            pool.affine_select(out=upper[:, :], in_=ones[:, :], compare_op=ALU.is_gt, fill=0.0,
                               base=0, pattern=[[1, P]], channel_multiplier=-1).then_inc(masks_done, 1)
            pool.iota(iota[:, :], pattern=[[1, P]], base=0, channel_multiplier=0,
                      allow_small_or_imprecise_dtypes=True).then_inc(masks_done, 1)

            def embedding_inputs(i, updates):
                pool.wait_ge(x_done, updates)
                pool.dma_start(pnat[:, :, :], p[i, 0].rearrange("(t p) d -> p t d", p=P)).then_inc(p_in, 16)
                pool.dma_start(gbc[:, :], ple_norm_g[i:i + 1, :].broadcast_to([P, D])).then_inc(p_in, 16)

            embedding_inputs(0, 2)
            pool.wait_ge(cs_done, KT)
            pool.dma_start(cT[:, 0:4, 0:2 * P], conv_b_pw2[0:1, :].rearrange("a (c n) -> a c n", c=4)
                           .broadcast_to([P, 4, 2 * P])).then_inc(b_in, 16)
            pool.wait_ge(x_done, 4)
            pool.dma_start(ysb[:, :], ffn_norm_g[1:2, :].broadcast_to([P, D])).then_inc(g_in, 16)
            embedding_inputs(1, 5)

        @block.tensor
        def _(pe):
            def wait_unit(u, j):
                pe.wait_ge(lo_done, after(u + 1, JOB, j))

            def three(dst, ahi_, alo_, bhi_, blo_, first, last, **kw):
                pe.matmul(dst, ahi_, bhi_, start=first, stop=False, **kw)
                pe.matmul(dst, ahi_, blo_, start=False, stop=False, **kw)
                return pe.matmul(dst, alo_, bhi_, start=False, stop=last, **kw)

            def linear_unit(u, i, banks, tiles, j=None):
                wait_unit(u, j)
                s = u % SPLIT
                for k in range(2):
                    kt = 2 * i + k
                    cols = slice(k * CW, (k + 1) * CW)
                    for t in range(tiles):
                        rows = slice(t * P, (t + 1) * P)
                        last = three(ps[:, banks + t, :], ahi[:, kt, rows], alo[:, kt, rows],
                                     whi[:, s, cols], wlo[:, s, cols], kt == 0, kt == KT - 1)
                last.then_inc(unit_used, 1)

            def transpose_rows():
                for b in range(4):
                    for k in range(2):
                        for t in range(T):
                            kt = 2 * b + k
                            at = k * S + t * P
                            last = pe.transpose(ps[:, b, at:at + P], xn[:, t, kt * P:(kt + 1) * P],
                                                ident[:, :])
                    last.then_inc(tp_ready, 1)

            def norm_transpose(r):
                pe.wait_ge(xn_done, 2 * (r + 1))
                transpose_rows()

            def linear(u0, c0, chunks, stage):
                for c in range(chunks):
                    if c0 + c >= 2:
                        pe.wait_ge(chunk_free, c0 + c - 1)
                    for i in range(4):
                        if c == 0:
                            pe.wait_ge(alo_done, 4 * stage + i + 1)
                        linear_unit(u0 + 4 * c + i, i, 2 * ((c0 + c) % 2), T)

            def hidden_transpose(n, tiles, j):
                pe.wait_ge(h_done, after(n, STEPS, j))
                for t in range(tiles):
                    for k in range(4):
                        last = pe.transpose(ps[:, 2 // (3 - tiles) + t, k * P:(k + 1) * P],
                                            hid[:, t, k * P:(k + 1) * P], ident[:, :])
                last.then_inc(hT_ready, 1)

            def down(u, n, s, tiles, j):
                pe.wait_ge(hTlo_done, after(n, STEPS, j))
                for i in range(4):
                    half = i // 2
                    wait_unit(u + i, j)
                    for k in range(2):
                        kt = 2 * (i % 2) + k
                        cols = slice(k * CW, (k + 1) * CW)
                        for t in range(tiles):
                            last = three(ps[:, 4 + 2 * t + half, :], hThi[:, t, kt * P:(kt + 1) * P],
                                         hTlo[:, t, kt * P:(kt + 1) * P], whi[:, (u + i) % SPLIT, cols],
                                         wlo[:, (u + i) % SPLIT, cols], s == 0 and kt == 0,
                                         s == STEPS - 1 and kt == 3)
                    last.then_inc(unit_used, 1)

            def feed_forward(u0, n0, tiles, j, side):
                u, up = u0, 2 // (3 - tiles)
                for s in range(STEPS):
                    n = n0 + s
                    if n:
                        pe.wait_ge(silu_done, after(n, STEPS, j))
                    for i in range(4):
                        linear_unit(u + i, i, 0, tiles, j)
                        if i == 1 and s:
                            hidden_transpose(n, tiles, j)
                    u += 4
                    if s:
                        down(u, n, s - 1, tiles, j)
                        u += 4
                    side(s)
                    if s == 0 and n:
                        pe.wait_ge(hTlo_done, after(n, STEPS, j))
                    for i in range(4):
                        linear_unit(u + i, i, up, tiles, j)
                    u += 4
                side(STEPS)
                hidden_transpose(n0 + STEPS, tiles, j)
                side(STEPS + 1)
                down(u, n0 + STEPS, STEPS - 1, tiles, j)

            pe.wait_ge(consts_in, 16 * N_CONSTS)
            pe.wait_ge(masks_done, 5)
            pe.transpose(ps[:, 0, 0:NV], stage_v, ident[0:NV, 0:NV])
            pe.transpose(ps[:, 0, P:P + TAPROWS], stage_t[0], ident[0:TAPROWS, 0:TAPROWS])
            pe.transpose(ps[:, 0, 2 * P:2 * P + TAPROWS], stage_t[1],
                         ident[0:TAPROWS, 0:TAPROWS]).then_inc(vecsT_ready, 1)

            pe.wait_ge(vecs_done, 1)
            norm_transpose(0)
            for c in range(NQKV):
                if c >= 2:
                    pe.wait_ge(chunk_free, c - 1)
                for i in range(4):
                    if c == 0:
                        pe.wait_ge(alo_done, i + 1)
                    if c < 2:
                        pe.wait_ge(alo_done, 4)
                    linear_unit(U_QKV + 4 * c + i, i, 2 * (c % 2), T)
                    if i == 1 and 1 <= c <= 4:
                        pe.wait_ge(qk_n, c)
                        if c >= 2:
                            pe.wait_ge(qkT_done, c - 1)
                        for t in range(T):
                            for h in range(4):
                                last = pe.transpose(ps[:, 4 + t, h * P:(h + 1) * P],
                                                    xn[:, t, h * P:(h + 1) * P], ident[:, :])
                        last.then_inc(qkT_ready, 1)

            def scores(h):
                if h >= 2:
                    pe.wait_ge(sm_done, h - 1)
                for c in range(2):
                    rows = slice(c * HD, (c + 1) * HD)
                    b = 2 * (h % 2) + c
                    pe.matmul(ps[:, b, 0:P], qT[rows, h, 0:P], kT[rows, h, 0:P], start=True, stop=True)
                    last = pe.matmul(ps[:, b, P:3 * P], qT[rows, h, P:S], kT[rows, h, 0:S],
                                     start=True, stop=True)
                last.then_inc(s_ready, 1)

            pe.wait_ge(qkT_done, 4)
            pe.wait_ge(v_done, 2)
            scores(0)
            scores(1)
            for h in range(H):
                pe.wait_ge(am_done, h + 1)
                if h >= 2:
                    pe.wait_ge(amT_done, h - 1)
                for k in range(3):
                    last = pe.transpose(ps[:, 4 + h % 2, k * P:(k + 1) * P],
                                        amix[:, h % 2, k * P:(k + 1) * P], ident[:, :])
                last.then_inc(amT_ready, 1)
                if h + 2 < H:
                    scores(h + 2)
                pe.wait_ge(amT_done, h + 1)
                if h >= 2:
                    pe.wait_ge(o_done, h - 1)
                b, e = 6 + h % 2, slice(h * P, (h + 1) * P)
                pe.matmul(ps[:, b, 0:P], amixT[:, h % 2, 0:P], v_sb[:, 0, e], start=True, stop=True)
                pe.matmul(ps[:, b, P:S], amixT[:, h % 2, P:2 * P], v_sb[:, 0, e], start=True, stop=False)
                pe.matmul(ps[:, b, P:S], amixT[:, h % 2, 2 * P:3 * P], v_sb[:, 1, e],
                          start=False, stop=True).then_inc(o_ready, 1)
            pe.wait_ge(on_step, 3)
            transpose_rows()
            pe.wait_ge(alo_done, 8)
            linear(U_WO, C_WO, NO, 1)

            norm_transpose(1)
            pe.wait_ge(alo_done, 12)
            feed_forward(U_FFN, 0, T, None, lambda place: None)

            def embedding(i, u_proj, u_gate, c0, r, stage, j):
                pe.wait_ge(p_in, 32 * (i + 1))
                for k in range(2):
                    for t in range(T):
                        last = pe.transpose(ps[:, 0, k * S + t * P:k * S + (t + 1) * P],
                                            pnat[:, t, k * P:(k + 1) * P], ident[:, :])
                last.then_inc(pT_ready, 1)
                pe.wait_ge(pTlo_done, i + 1)
                for k in range(2):
                    wait_unit(u_proj + k, j)
                    s = (u_proj + k) % SPLIT
                    for t in range(T):
                        for half in range(2):
                            rows, cols = slice(t * P, (t + 1) * P), slice(half * CW, (half + 1) * CW)
                            last = three(ps[:, 4 + 2 * t + half, :], pThi[:, k, rows], pTlo[:, k, rows],
                                         whi[:, s, cols], wlo[:, s, cols], k == 0, k == 1)
                    last.then_inc(unit_used, 1)
                norm_transpose(r)
                pe.wait_ge(alo_done, 4 * (stage + 1))
                for c in range(NO):
                    for n in range(4):
                        linear_unit(u_gate + 4 * c + n, n, 2 * ((c0 + c) % 2), T, j)

            pe.wait_ge(x_done, 2)
            embedding(0, U_PROJ0, U_GATE0, C_GATE0, 2, 3, None)

            norm_transpose(3)
            pe.wait_ge(alo_done, 20)
            for c in range(4):
                pe.wait_ge(chunk_free, C_PW1 + c - 1)
                for i in range(4):
                    u = U_PW1 + 4 * c + i
                    wait_unit(u, None)
                    for k in range(2):
                        kt = 2 * i + k
                        for b in range(4):
                            cols = slice(k * CW + b * P, k * CW + (b + 1) * P)
                            bank, at = 2 * (c % 2) + b // 2, (b % 2) * S
                            last = three(ps[:, bank, at:at + S], whi[:, u % SPLIT, cols],
                                         wlo[:, u % SPLIT, cols], ahi[:, kt, :], alo[:, kt, :],
                                         kt == 0 and b % 2 == 0, kt == KT - 1, skip_group_check=True)
                    last.then_inc(unit_used, 1)
            for (wait, src, bank, done) in ((conv_done, cy, 4, mean_ready), (csq_done, csq, 5, var_ready)):
                for b in range(KT):
                    pe.wait_ge(wait, b + 1 if wait is conv_done else 1)
                    last = pe.matmul(ps[:, bank, 0:S], ones[:, :], src[:, b, :], start=b == 0, stop=b == KT - 1)
                last.then_inc(done, 1)
            linear(U_PW2, C_PW2, NO, 5)

            norm_transpose(4)
            pe.wait_ge(alo_done, 28)
            for t in range(T):
                rows = slice(t * P, (t + 1) * P)
                for kt in range(KT):
                    for a, b in ((ahi, wrhi), (ahi, wrlo), (alo, wrhi), (alo, wrlo)):
                        last = pe.matmul(ps[:, 4 + t, 0:NE], a[:, kt, rows], b[:, kt, :],
                                         start=kt == 0 and a is ahi and b is wrhi,
                                         stop=kt == KT - 1 and a is alo and b is wrlo)
            last.then_inc(log_ready, 1)
            pe.wait_ge(rm_done, 1)
            m = small[:, 112:128].rearrange("p (t e) -> p t e", t=T)
            pe.matmul(ps[:, 6, 0:NE], upper[:, :], m[:, 0, :], start=True, stop=True)
            pe.matmul(ps[:, 6, NE:2 * NE], ones[:, :], m[:, 0, :], start=True, stop=False)
            pe.matmul(ps[:, 6, NE:2 * NE], upper[:, :], m[:, 1, :], start=False, stop=True)
            pe.matmul(ps[:, 6, 2 * NE:3 * NE], ones[:, :], m[:, 0, :], start=True, stop=False)
            pe.matmul(ps[:, 6, 2 * NE:3 * NE], ones[:, :], m[:, 1, :], start=False,
                      stop=True).then_inc(cnt_ready, 1)

            def gather(bank, j):
                for k in range(4):
                    kt = 4 * (bank - 2) + k
                    for t in range(T):
                        last = pe.matmul(ps[:, bank, k * P:(k + 1) * P], xn[:, t, kt * P:(kt + 1) * P],
                                         sel[:, t, :], start=t == 0, stop=t == T - 1)
                last.then_inc(xe_ready, 1)

            pe.wait_ge(hg_done, 1)
            pe.wait_ge(sel_done, 1)
            gather(2, None)
            gather(3, None)
            pe.wait_ge(tab_done, 1)
            jobs = pe.snap(pe.value_load(jtab[0:1, NCOL:NCOL + 1], min_val=NE, max_val=MAXJOBS))
            with pe.Fori(0, jobs) as j:
                def side(place):
                    if place == 2:
                        for t in range(T):
                            last = pe.transpose(ps[:, 3, t * P:(t + 1) * P], selg[:, t, :], ident[:, :])
                        last.then_inc(selT_ready, 1)
                    if place == STEPS:
                        pe.wait_ge(selT_done, j + 1)
                        pe.wait_ge(sel_done, j + 2)
                        gather(2, j)
                    if place == STEPS + 1:
                        gather(3, j)

                pe.wait_ge(xelo_done, 2 * j + 2)
                feed_forward(U_MOE, STEPS, 1, j, side)
                pe.wait_ge(y0_done, j + 1)
                for k in range(4):
                    half, t = k // 2, k % 2
                    if k == 2:
                        pe.wait_ge(y1_done, j + 1)
                    if k >= 2:
                        pe.wait_ge(sc_done, 4 * j + (k - 1))
                    pe.matmul(ps[:, 6 + t, :], selT[:, t * P:(t + 1) * P],
                              ysb[:, half * CW:(half + 1) * CW], start=True, stop=True).then_inc(sc_ready, 1)
            pe.wait_ge(x_done, 5)
            embedding(1, U_PROJ1, U_GATE1, C_GATE1, 5, 7, jobs)

        @block.scalar
        def _(act):
            def split_hi(u, j):
                act.wait_ge(piece_in[(u // 2) % RING],
                            after(16 * (u // 2 // RING + 1), 16 * (JOB // 2 // RING), j))
                if u >= SPLIT:
                    act.wait_ge(unit_used, after(u - SPLIT + 1, JOB, j))
                act.activation(whi[:, u % SPLIT, :], raw(u), ACT.Copy).then_inc(hi_done, 1)

            split = Splitter(split_hi)
            own = Order(act, act_seq)

            rows = [(V_MIX, mix_norm_g, 16), (V_FFN, ffn_norm_g, 16), (V_PLEG, ple_gate_norm_g, 16),
                    (V_BPW1, conv_b_pw1, 16), (V_BDW, conv_b_dw, 8), (V_LNG, conv_ln_g, 8),
                    (V_LNB, conv_ln_b, 8)]
            for at, src, n in rows:
                act.dma_start(kT[at:at + n, 0, 0:P], src.rearrange("l (c n) -> (l c) n", n=P)
                              ).then_inc(consts_in, 16)
            for at, src in ((V_GQ, attn_g_q), (V_GK, attn_g_k)):
                act.dma_start(kT[at:at + 1, 0, 0:P], src.rearrange("l c n -> l (c n)")).then_inc(consts_in, 16)
            act.dma_start(kT[V_GSUB:V_GSUB + 1, 0, 0:P], attn_g_sub).then_inc(consts_in, 16)
            tap_rows = conv_w_dw[0].rearrange("k (c n) -> (k c) n", n=P)
            for i in range(2):
                act.dma_start(stage_t[i], tap_rows[i * TAPROWS:(i + 1) * TAPROWS, :]).then_inc(consts_in, 16)
            for i, src in enumerate((attn_lam_q1, attn_lam_k1, attn_lam_q2, attn_lam_k2)):
                act.dma_start(lamv[:, i, :], src.broadcast_to([P, HD])).then_inc(consts_in, 16)
            act.dma_start(wr[:, :, :], moe_w_router[0].rearrange("(t p) e -> p t e", p=P)).then_inc(consts_in, 16)
            act.dma_start(rbias[:, :], moe_b_router.broadcast_to([P, NE])).then_inc(consts_in, 16)

            def norm(r, q, updates):
                split.to(q + 5)
                if updates:
                    act.wait_ge(x_done, updates)
                else:
                    act.wait_ge(x_in, 16)
                    act.wait_ge(vecs_done, 1)
                act.activation(xn[:, 0, :], xres[:, 0, :], ACT.Square, accum_out=ssq[:, 0:1]).then_inc(ssq_a, 1)
                act.wait_ge(ssq_a, r + 1)
                act.wait_ge(ssq_d, r + 1)
                act.activation(std, ssq, ACT.Sqrt, bias=eps, scale=1.0 / D).then_inc(std_done, 1)

            def act_hi(m, tp, gain):
                for b in range(4):
                    act.wait_ge(tp_ready, tp + b + 1)
                    for k in range(2):
                        ins = act.activation(ahi[:, 2 * b + k, :], ps[:, b, k * S:(k + 1) * S],
                                             ACT.Copy, scale=gain(2 * b + k))
                    ins.then_inc(ahi_done, 1)

            def vec(at):
                return lambda kt: vecs[:, at + kt:at + kt + 1]

            act.wait_ge(lam_part, 1)
            act.activation(lamexp, lamsum, ACT.Exp).then_inc(lam_part, 1)
            act.wait_ge(consts_in, 16 * N_CONSTS)
            act.activation(wrhi[:, :, :], wr[:, :, :], ACT.Copy).then_inc(wr_done, 1)

            norm(0, -1, 0)
            act_hi(0, 0, vec(V_MIX))

            def qk_transposed(c):
                act.wait_ge(qkT_ready, c + 1)
                dst, gain = (qT, V_GQ) if c < 2 else (kT, V_GK)
                for t in range(T):
                    ins = act.activation(dst[:, 4 * (c % 2):4 * (c % 2) + 4, t * P:(t + 1) * P],
                                         ps[:, 4 + t, :].rearrange("p (h n) -> p h n", h=4), ACT.Copy,
                                         scale=vecs[:, gain:gain + 1])
                ins.then_inc(qkT_done, 1)

            for c in range(NQKV):
                q = U_QKV + 4 * c + 3
                pair = ps[:, 2 * (c % 2):2 * (c % 2) + 2, :]
                if c < 4:
                    split.to(q + 4)
                    act.wait_ge(unit_used, q + 1)
                    if c:
                        act.wait_ge(qk_ssq, c)
                    act.activation(xn[:, :, CW:D], pair, ACT.Square).then_inc(qk_sq, 1)
                    act.wait_ge(qk_ssq, c + 1)
                    act.activation(hstd, hsq, ACT.Sqrt, bias=eps, scale=1.0 / HD).then_inc(qk_std, 1)
                    split.to(q + 6)
                    qk_transposed(c)
                else:
                    split.to(q + 4)
                    act.wait_ge(unit_used, q + 1)
                    act.activation(v_sb[:, :, (c - 4) * CW:(c - 3) * CW], pair, ACT.Copy).then_inc(v_done, 1)

            def exps(h):
                act.wait_ge(sm_done, h + 1)
                for t in range(T):
                    for c in range(2):
                        i = 4 * (h % 2) + 2 * t + c
                        part = prob[:, h % 2, c, 0:P] if t == 0 else prob[:, h % 2, c, P:3 * P]
                        ins = act.activation(part, part, ACT.Exp, bias=nmx[:, i:i + 1],
                                             accum_out=psum_e[:, i:i + 1])
                ins.then_inc(exp_done, 1)

            exps(0)
            for h in range(H):
                if h + 1 < H:
                    exps(h + 1)
                act.wait_ge(amT_ready, h + 1)
                if h >= 2:
                    act.wait_ge(o_ready, h - 1)
                act.activation(amixT[:, h % 2, :], ps[:, 4 + h % 2, 0:3 * P], ACT.Copy).then_inc(amT_done, 1)
                act.wait_ge(o_ready, h + 1)
                act.activation(xn[:, :, h * P:(h + 1) * P],
                               ps[:, 6 + h % 2, 0:S].rearrange("p (t n) -> p t n", t=T),
                               ACT.Copy).then_inc(o_done, 1)
            split.to(U_WO + 4)
            act.wait_ge(on_step, 1)
            act.activation(hstd, hsq, ACT.Sqrt, bias=eps, scale=1.0 / P).then_inc(on_step, 1)
            act_hi(1, 4, lambda kt: gsub)

            def feed_forward(u0, n0, tiles, j, side):
                u, up = u0, 2 // (3 - tiles)

                def hidden_hi(n):
                    act.wait_ge(hT_ready, after(n, STEPS, j))
                    act.activation(hThi[:, 0:tiles, :], ps[:, up:up + tiles, :], ACT.Copy).then_inc(hThi_done, 1)

                for s in range(STEPS):
                    n = n0 + s
                    if s:
                        split.to(u + 5)
                        hidden_hi(n)
                    split.to(u + 7)
                    act.wait_ge(unit_used, after(u + 4, JOB, j))
                    if n:
                        act.wait_ge(h_done, after(n, STEPS, j))
                    act.activation(sg[:, 0:tiles, :], ps[:, 0:tiles, :], ACT.Silu).then_inc(silu_done, 1)
                    side(s, u + 4)
                    u += 12 if s else 8
                side(STEPS, u)
                split.to(u + 4)
                hidden_hi(n0 + STEPS)
                return u

            norm(1, U_FFN - 1, 1)
            act_hi(2, 8, vec(V_FFN))
            feed_forward(U_FFN, 0, T, None, lambda place, u: None)

            def embedding(i, u_proj, u_gate, r, tp, updates, j):
                split.to(u_proj + 4)
                act.wait_ge(pT_ready, i + 1)
                act.activation(pThi[:, :, :], ps[:, 0, :].rearrange("p (k n) -> p k n", k=2),
                               ACT.Copy).then_inc(pThi_done, 1)
                norm(r, u_proj - 1, updates)
                act.wait_ge(unit_used, after(u_proj + 2, JOB, j))
                for t in range(T):
                    ins = act.activation(emb[:, t, :], ps[:, 4 + 2 * t:6 + 2 * t, :].rearrange("p b n -> p (b n)"),
                                         ACT.Square, accum_out=hsq[:, t:t + 1])
                own.step(ins)
                act.activation(hstd[:, 0:2], hsq[:, 0:2], ACT.Sqrt, bias=eps, scale=1.0 / D).then_inc(e_std, 1)
                act_hi(0, tp, vec(V_PLEG + KT * i))
                for c in range(NO):
                    q = u_gate + 4 * c + 3
                    split.to(min(q + 4, U_END) if i else q + 4)
                    act.wait_ge(unit_used, after(q + 1, JOB, j))
                    if c:
                        act.wait_ge(chunk_free, C_GATE0 + 1 if i == 0 else C_GATE1 + 1)
                    act.activation(sgm[:, :, :], ps[:, 2 * c:2 * c + 2, :], ACT.Sigmoid).then_inc(sgm_done, 1)

            embedding(0, U_PROJ0, U_GATE0, 2, 12, 2, None)

            norm(3, U_PW1 - 1, 3)
            act_hi(4, 16, vec(V_MIX + KT))
            for cc in range(2):
                q = U_PW1 + 8 * cc + 7
                split.to(q + 4)
                act.wait_ge(unit_used, q + 1)
                if cc:
                    act.wait_ge(glu_done, 4)
                for b in range(4):
                    ch = 4 * cc + b
                    act.activation(xn[:, b // 2, (b % 2) * CW:(b % 2) * CW + S],
                                   ps[:, 2 + b // 2, (b % 2) * S:(b % 2 + 1) * S], ACT.Sigmoid,
                                   bias=vecs[:, V_BPW1 + KT + ch:V_BPW1 + KT + ch + 1]).then_inc(glu_sig, 1)
            act.wait_ge(mean_ready, 1)
            act.activation(xn[:, 0, 0:S], ps[:, 4, 0:S], ACT.Copy, scale=1.0 / D).then_inc(mean_done, 1)
            act.wait_ge(cent_done, 1)
            act.activation(csq[:, :, :], cy[:, :, :], ACT.Square).then_inc(csq_done, 1)
            act.wait_ge(var_ready, 1)
            act.activation(xn[:, 0, CW:CW + S], ps[:, 5, 0:S], ACT.Sqrt, bias=lneps,
                           scale=1.0 / D).then_inc(cstd_done, 1)
            act.wait_ge(cn_done, 1)
            for b in range(KT):
                act.activation(csq[:, b, :], cy[:, b, :], ACT.Silu, bias=vecs[:, V_LNB + b:V_LNB + b + 1],
                               scale=vecs[:, V_LNG + b:V_LNG + b + 1]).then_inc(cs_done, 1)
                if b % 2:
                    act.wait_ge(cs_done, b + 1)
                    act.activation(ahi[:, b - 1:b + 1, :], csq[:, b - 1:b + 1, :], ACT.Copy).then_inc(ahi_done, 1)

            norm(4, U_MOE - 1, 4)
            act_hi(6, 20, vec(V_FFN + KT))
            act.wait_ge(r_step, 1)
            act.activation(small[:, 140:142], small[:, 138:140], ACT.Exp).then_inc(r_step, 1)

            def gather_hi(n, j):
                for b in range(2):
                    act.wait_ge(xe_ready, after(n + b + 1, 2, j))
                    act.activation(ahi[:, 4 * b:4 * b + 4, 0:P],
                                   ps[:, 2 + b, :].rearrange("p (k n) -> p k n", k=4),
                                   ACT.Copy).then_inc(xehi_done, 1)

            gather_hi(0, None)
            act.wait_ge(tab_done, 1)
            jobs = act.snap(act.value_load(jtab[0:1, NCOL:NCOL + 1], min_val=NE, max_val=MAXJOBS))
            split.to(U_MOE + 4)
            with act.Fori(0, jobs) as j:
                def side(place, u):
                    if place == 2:
                        split.to(u + 5)
                        act.wait_ge(selT_ready, j + 1)
                        act.activation(selT[:, :], ps[:, 3, 0:S], ACT.Copy).then_inc(selT_done, 1)

                split.j, split.next = j, U_MOE + 4
                u = feed_forward(U_MOE, STEPS, 1, j, side)
                gather_hi(2, j)
                act.wait_ge(unit_used, after(u + 2, JOB, j))
                act.activation(ysb[:, 0:CW], ps[:, 4, :], ACT.Copy).then_inc(y0_done, 1)
                split.to(U_MOE + JOB + 4)
            split.j, split.next = jobs, U_MOE + 4
            embedding(1, U_PROJ1, U_GATE1, 5, 24, 5, jobs)

        @block.vector
        def _(dve):
            def split_lo(u, j):
                dve.wait_ge(hi_done, after(u + 1, JOB, j))
                dve.tensor_tensor(wlo[:, u % SPLIT, :], raw(u), whi[:, u % SPLIT, :].bitcast(F32),
                                  ALU.subtract).then_inc(lo_done, 1)

            split = Splitter(split_lo)
            own = Order(dve, dve_seq)

            def norm(r, q, updates):
                split.to(q + 5)
                if updates:
                    dve.wait_ge(x_done, updates)
                else:
                    dve.wait_ge(x_in, 16)
                dve.tensor_tensor_reduce(out=xn[:, 1, :], in0=xres[:, 1, :], in1=xres[:, 1, :], scale=1.0,
                                         scalar=0.0, op0=ALU.mult, op1=ALU.add,
                                         accum_out=ssq[:, 1:2]).then_inc(ssq_d, 1)
                dve.wait_ge(std_done, r + 1)
                dve.wait_ge(ssq_d, r + 1)
                own.step(dve.reciprocal(rstd, std))
                for t in range(T):
                    dve.tensor_scalar(xn[:, t, :], xres[:, t, :], rstd[:, t:t + 1], None,
                                      ALU.mult).then_inc(xn_done, 1)

            def act_lo(m, gain):
                for b in range(4):
                    dve.wait_ge(ahi_done, 4 * m + b + 1)
                    for k in range(2):
                        kt = 2 * b + k
                        ins = dve.scalar_tensor_tensor(alo[:, kt, :], ps[:, b, k * S:(k + 1) * S], gain(kt),
                                                       ahi[:, kt, :].bitcast(F32), ALU.mult, ALU.subtract)
                    ins.then_inc(alo_done, 1)

            def vec(at):
                return lambda kt: vecs[:, at + kt:at + kt + 1]

            dve.memset(eps, EPS)
            dve.memset(lneps, LN_EPS)
            own.step(dve.memset(jpos[:, :, :], -1.0))
            own.step(dve.memset(jgate[:, :, :], 0.0))
            dve.wait_ge(consts_in, 16 * N_CONSTS)
            own.step(dve.tensor_tensor(lamv[:, 0:4:2, :], lamv[:, 0:4:2, :], lamv[:, 1:4:2, :], ALU.mult))
            dve.reduce_sum(lamsum, lamv[:, 0:4:2, :], AX).then_inc(lam_part, 1)
            dve.wait_ge(vecsT_ready, 1)
            dve.tensor_copy(vecs[:, 0:NV], ps[:, 0, 0:NV])
            own.step(dve.tensor_copy(taps[:, :].rearrange("p (a n) -> p a n", a=2),
                                     ps[:, 0, P:3 * P].rearrange("p (a n) -> p a n", a=2)[:, :, 0:TAPROWS]))
            dve.wait_ge(lam_part, 2)
            own.step(dve.tensor_scalar(gsub, vecs[:, V_GSUB:V_GSUB + 1], 1.0 - LAM0, None, ALU.mult))
            own.step(dve.tensor_tensor(neglam, lamexp[:, 1:2], lamexp[:, 0:1], ALU.subtract))
            dve.tensor_scalar(neglam, neglam, -LAM0, None, ALU.add).then_inc(vecs_done, 1)
            dve.wait_ge(wr_done, 1)
            own.step(dve.tensor_tensor(wrlo[:, :, :], wr[:, :, :], wrhi[:, :, :].bitcast(F32), ALU.subtract))

            norm(0, -1, 0)
            act_lo(0, vec(V_MIX))
            for c in range(NQKV):
                q = U_QKV + 4 * c + 3
                pair = ps[:, 2 * (c % 2):2 * (c % 2) + 2, :]
                split.to(q + 4)
                if c < 4:
                    groups = "p t (g n) -> p t g n"
                    h16 = hsq.rearrange("p (t g) -> p t g", t=T)
                    dve.wait_ge(qk_sq, c + 1)
                    dve.tensor_reduce(h16, xn[:, :, CW:D].rearrange(groups, n=HD), AX,
                                      ALU.add).then_inc(qk_ssq, 1)
                    dve.wait_ge(qk_std, c + 1)
                    own.step(dve.reciprocal(hrstd, hstd))
                    if c:
                        dve.wait_ge(qkT_ready, c)
                    for t in range(T):
                        ins = dve.tensor_tensor(
                            xn[:, t, 0:CW].rearrange("p (g n) -> p g n", n=HD),
                            pair[:, t, :].rearrange("p (g n) -> p g n", n=HD),
                            hrstd[:, 8 * t:8 * t + 8].unsqueeze(2).broadcast_to([P, 8, HD]), ALU.mult)
                        own.step(ins)
                    dve.sem_inc(qk_n, 1)
                    dve.sem_inc(chunk_free, 1)
                else:
                    dve.wait_ge(v_done, c - 3)
                    dve.sem_inc(chunk_free, 1)

            def masked(h):
                dve.wait_ge(s_ready, h + 1)
                b = h % 2
                for c in range(2):
                    n = own.add(dve.scalar_tensor_tensor(prob[:, b, c, :], ps[:, 2 * b + c, 0:3 * P], HD ** -0.5,
                                                         mask[:, :], ALU.mult, ALU.add))
                own.wait(n)
                dve.reduce_max(mx[:, 4 * b:4 * b + 2], prob[:, b, :, 0:P], AX)
                own.step(dve.reduce_max(mx[:, 4 * b + 2:4 * b + 4], prob[:, b, :, P:3 * P], AX))
                dve.tensor_scalar(nmx[:, 4 * b:4 * b + 4], mx[:, 4 * b:4 * b + 4], -1.0, None,
                                  ALU.mult).then_inc(sm_done, 1)

            dve.wait_ge(masks_done, 5)
            masked(0)
            for h in range(H):
                if h + 1 < H:
                    masked(h + 1)
                b = h % 2
                dve.wait_ge(exp_done, h + 1)
                own.step(dve.reciprocal(pinv[:, 4 * b:4 * b + 4], psum_e[:, 4 * b:4 * b + 4]))
                comp1 = pinv[:, 4 * b + 1:4 * b + 4:2]
                own.step(dve.tensor_scalar(comp1, comp1, neglam, None, ALU.mult))
                if h >= 2:
                    dve.wait_ge(amT_ready, h - 1)
                parts = (slice(0, P), slice(P, 3 * P))
                for t in range(T):
                    n = own.add(dve.tensor_scalar(amix[:, b, parts[t]], prob[:, b, 0, parts[t]],
                                                  pinv[:, 4 * b + 2 * t:4 * b + 2 * t + 1], None, ALU.mult))
                own.wait(n)
                for t in range(T):
                    ins = dve.scalar_tensor_tensor(amix[:, b, parts[t]], prob[:, b, 1, parts[t]],
                                                   pinv[:, 4 * b + 2 * t + 1:4 * b + 2 * t + 2],
                                                   amix[:, b, parts[t]], ALU.mult, ALU.add)
                ins.then_inc(am_done, 1)
            split.to(U_WO + 4)
            dve.wait_ge(o_done, H)
            o16 = xn[:, :, :].rearrange("p t (h n) -> p (t h) n", n=P)
            sq16 = qT[:, :, :].rearrange("p h s -> p (h s)").rearrange("p (g n) -> p g n", n=P)
            own.step(dve.tensor_tensor(sq16, o16, o16, ALU.mult))
            dve.tensor_reduce(hsq, sq16, AX, ALU.add).then_inc(on_step, 1)
            dve.wait_ge(on_step, 2)
            own.step(dve.reciprocal(hrstd, hstd))
            dve.tensor_tensor(o16, o16, hrstd.unsqueeze(2).broadcast_to([P, T * H, P]),
                              ALU.mult).then_inc(on_step, 1)
            act_lo(1, lambda kt: gsub)

            for c in range(NO):
                q = U_WO + 4 * c + 3
                split.to(q + 4)
                dve.wait_ge(unit_used, q + 1)
                cols = xres[:, :, c * CW:(c + 1) * CW]
                own.step(dve.tensor_tensor(cols, cols, ps[:, 2 * c:2 * c + 2, :], ALU.add))
                dve.sem_inc(chunk_free, 1)
            dve.sem_inc(x_done, 1)

            def feed_forward(u0, n0, tiles, j, side):
                u, up = u0, 2 // (3 - tiles)

                def hidden(n):
                    dve.wait_ge(silu_done, after(n, STEPS, j))
                    if n > 1:
                        dve.wait_ge(hT_ready, after(n - 1, STEPS, j))
                    dve.tensor_tensor(hid[:, 0:tiles, :], sg[:, 0:tiles, :], ps[:, up:up + tiles, :],
                                      ALU.mult).then_inc(h_done, 1)

                def hidden_lo(n):
                    dve.wait_ge(hThi_done, after(n, STEPS, j))
                    dve.tensor_tensor(hTlo[:, 0:tiles, :], ps[:, up:up + tiles, :],
                                      hThi[:, 0:tiles, :].bitcast(F32), ALU.subtract).then_inc(hTlo_done, 1)

                for s in range(STEPS):
                    n = n0 + s
                    if s:
                        split.to(u + 3)
                        dve.wait_ge(unit_used, after(u, JOB, j))
                        hidden(n)
                        split.to(u + 5)
                        hidden_lo(n)
                    side(s, u + 4)
                    u += 12 if s else 8
                split.to(u + 3)
                dve.wait_ge(unit_used, after(u, JOB, j))
                hidden(n0 + STEPS)
                split.to(u + 4)
                hidden_lo(n0 + STEPS)
                return u

            norm(1, U_FFN - 1, 1)
            act_lo(2, vec(V_FFN))
            feed_forward(U_FFN, 0, T, None, lambda place, u: None)
            split.to(U_PROJ0 + 4)
            dve.wait_ge(unit_used, U_PROJ0)
            dve.tensor_tensor(xres[:, :, :], xres[:, :, :],
                              ps[:, 4:8, :].rearrange("p (t b) n -> p t (b n)", t=T), ALU.add).then_inc(x_done, 1)

            def embedding(i, u_proj, u_gate, r, m, updates, k0, j):
                split.to(u_proj + 4)
                dve.wait_ge(pThi_done, i + 1)
                dve.tensor_tensor(pTlo[:, :, :], ps[:, 0, :].rearrange("p (k n) -> p k n", k=2),
                                  pThi[:, :, :].bitcast(F32), ALU.subtract).then_inc(pTlo_done, 1)
                norm(r, u_proj - 1, updates)
                dve.wait_ge(e_std, i + 1)
                own.step(dve.reciprocal(hrstd[:, 0:2], hstd[:, 0:2]))
                for t in range(T):
                    n = own.add(dve.scalar_tensor_tensor(
                        emb[:, t, :], ps[:, 4 + 2 * t:6 + 2 * t, :].rearrange("p b n -> p (b n)"),
                        hrstd[:, t:t + 1], gbc[:, :], ALU.mult, ALU.mult))
                own.wait(n)
                act_lo(m, vec(V_PLEG + KT * i))
                for c in range(NO):
                    q = u_gate + 4 * c + 3
                    split.to(min(q + 4, U_END) if i else q + 4)
                    dve.wait_ge(sgm_done, 2 * i + c + 1)
                    cols = xres[:, :, c * CW:(c + 1) * CW]
                    own.step(dve.tensor_tensor(emb[:, :, c * CW:(c + 1) * CW], emb[:, :, c * CW:(c + 1) * CW],
                                               sgm[:, :, :], ALU.mult))
                    dve.sem_inc(chunk_free, 1)
                    ins = dve.tensor_tensor(cols, cols, emb[:, :, c * CW:(c + 1) * CW], ALU.add)
                    own.step(ins)
                    if i or c:
                        dve.sem_inc(x_done, 1)

            embedding(0, U_PROJ0, U_GATE0, 2, 3, 2, C_GATE0, None)

            norm(3, U_PW1 - 1, 3)
            act_lo(4, vec(V_MIX + KT))
            own.step(dve.memset(cT[:, :, 0:TAPS - 1], 0.0))
            for cc in range(2):
                q = U_PW1 + 8 * cc + 7
                split.to(q + 4)
                for b in range(4):
                    ch = 4 * cc + b
                    dve.wait_ge(glu_sig, ch + 1)
                    ins = dve.scalar_tensor_tensor(
                        cT[:, ch, TAPS - 1:TAPS - 1 + S], ps[:, b // 2, (b % 2) * S:(b % 2 + 1) * S],
                        vecs[:, V_BPW1 + ch:V_BPW1 + ch + 1], xn[:, b // 2, (b % 2) * CW:(b % 2) * CW + S],
                        ALU.add, ALU.mult)
                    ins.then_inc(glu_done, 1)
                dve.wait_ge(glu_done, 4 * cc + 4)
                dve.sem_inc(chunk_free, 2)
                base = own.n
                for k in range(TAPS):
                    if cc == 0 and k % 4 == 3:
                        split.to(q + 5 + k // 4)
                    for b in range(4):
                        ch = 4 * cc + b
                        src, w = cT[:, ch, k:k + S], taps[:, k * KT + ch:k * KT + ch + 1]
                        if k == 0:
                            own.add(dve.tensor_scalar(cy[:, ch, :], src, w,
                                                      vecs[:, V_BDW + ch:V_BDW + ch + 1], ALU.mult, ALU.add))
                            continue
                        own.wait(base + 4 * (k - 1) + b + 1)
                        ins = dve.scalar_tensor_tensor(cy[:, ch, :], src, w, cy[:, ch, :], ALU.mult, ALU.add)
                        if k < TAPS - 1:
                            own.add(ins)
                        else:
                            ins.then_inc(conv_done, 1)
            dve.wait_ge(mean_done, 1)
            dve.tensor_tensor(cy[:, :, :], cy[:, :, :], xn[:, 0:1, 0:S].broadcast_to([P, KT, S]),
                              ALU.subtract).then_inc(cent_done, 1)
            dve.wait_ge(cstd_done, 1)
            own.step(dve.reciprocal(xn[:, 1, 0:S], xn[:, 0, CW:CW + S]))
            dve.tensor_tensor(cy[:, :, :], cy[:, :, :], xn[:, 1:2, 0:S].broadcast_to([P, KT, S]),
                              ALU.mult).then_inc(cn_done, 1)
            for b in range(4):
                dve.wait_ge(ahi_done, 20 + b + 1)
                dve.tensor_tensor(alo[:, 2 * b:2 * b + 2, :], csq[:, 2 * b:2 * b + 2, :],
                                  ahi[:, 2 * b:2 * b + 2, :].bitcast(F32), ALU.subtract).then_inc(alo_done, 1)
            dve.wait_ge(b_in, 16)
            for c in range(NO):
                bias = cT[:, 2 * c:2 * c + 2, 0:2 * P].unsqueeze(1).broadcast_to([P, T, 2, 2 * P])
                q = U_PW2 + 4 * c + 3
                split.to(q + 4)
                dve.wait_ge(unit_used, q + 1)
                for t in range(T):
                    cols = xres[:, t, c * CW:(c + 1) * CW]
                    own.step(dve.tensor_tensor(cols, cols, ps[:, 2 * c + t, :], ALU.add))
                    own.step(dve.tensor_tensor(cols.rearrange("p (a n) -> p a n", a=2),
                                               cols.rearrange("p (a n) -> p a n", a=2),
                                               cT[:, 2 * c:2 * c + 2, 0:2 * P], ALU.add))
                dve.sem_inc(chunk_free, 1)
            dve.sem_inc(x_done, 1)

            norm(4, U_MOE - 1, 4)
            act_lo(6, vec(V_FFN + KT))
            m12, g12 = small[:, 128:132], small[:, 132:136]
            pick = small[:, 112:128].rearrange("p (t e) -> p t e", t=T)
            tmp = hid[:, 0, 0:2 * P].rearrange("p (i n) -> p i n", n=16)
            e3 = lambda i: tmp[:, i, :].rearrange("p (t e) -> p t e", t=T)
            back, oh1, oh2, cand, l2 = e3(0), e3(1), e3(2), e3(3), e3(4)
            row = lambda v: v.unsqueeze(2).broadcast_to([P, T, NE])
            iota8 = iota[:, 0:NE].unsqueeze(1).broadcast_to([P, T, NE])
            dve.wait_ge(log_ready, 1)
            own.step(dve.tensor_scalar(back, iota8, -1.0, float(NE), ALU.mult, ALU.add))
            own.step(dve.tensor_tensor(logits, ps[:, 4:6, 0:NE],
                                       rbias[:, :].unsqueeze(1).broadcast_to([P, T, NE]), ALU.add))

            def top(src, mval, hot):
                own.step(dve.reduce_max(mval, src, AX))
                own.step(dve.tensor_tensor(cand, src, row(mval), ALU.is_equal))
                own.step(dve.tensor_tensor(cand, cand, back, ALU.mult))
                own.step(dve.reduce_max(g12[:, 0:2], cand, AX))
                own.step(dve.tensor_tensor(hot, back, row(g12[:, 0:2]), ALU.is_equal))

            top(logits, m12[:, 0:2], oh1)
            own.step(dve.scalar_tensor_tensor(l2, oh1, -3e38, logits, ALU.mult, ALU.add))
            top(l2, m12[:, 2:4], oh2)
            own.step(dve.tensor_tensor(pick, oh1, oh2, ALU.add))
            dve.sem_inc(rm_done, 1)
            dve.tensor_tensor(small[:, 138:140], m12[:, 2:4], m12[:, 0:2], ALU.subtract).then_inc(r_step, 1)
            dve.wait_ge(r_step, 2)
            own.step(dve.tensor_scalar(g12[:, 0:2], small[:, 140:142], 1.0, None, ALU.add))
            own.step(dve.reciprocal(g12[:, 0:2], g12[:, 0:2]))
            own.step(dve.tensor_tensor(g12[:, 2:4], g12[:, 0:2], small[:, 140:142], ALU.mult))
            own.step(dve.tensor_tensor(oh1, oh1, row(g12[:, 0:2]), ALU.mult))
            own.step(dve.tensor_tensor(oh2, oh2, row(g12[:, 2:4]), ALU.mult))
            gate8 = jgate[:, :, 0:NE]
            own.step(dve.tensor_tensor(gate8, oh1, oh2, ALU.add))
            FAR = 10000.0
            dve.wait_ge(cnt_ready, 1)
            pos8 = jpos[:, :, 0:NE]
            own.step(dve.tensor_scalar(pos8, ps[:, 6, 0:2 * NE].rearrange("p (t e) -> p t e", t=T), FAR, None, ALU.add))
            own.step(dve.tensor_tensor(pos8, pos8, pick, ALU.mult))
            own.step(dve.tensor_scalar(pos8, pos8, -FAR, None, ALU.add))
            over, rank, shift, which = (tmp[:, 5 + i, 0:NE] for i in range(4))
            own.step(dve.tensor_scalar(over, ps[:, 6, 2 * NE:3 * NE], P + 0.5, None, ALU.is_gt))
            own.step(dve.tensor_copy(rank, over))
            for d in (1, 2, 4):
                own.step(dve.tensor_copy(shift, rank))
                own.step(dve.tensor_tensor(rank[:, d:NE], shift[:, d:NE], shift[:, 0:NE - d], ALU.add))
            own.step(dve.tensor_tensor(which, rank, over, ALU.mult))
            trow = tmp[:, 9, 0:16]
            own.step(dve.memset(trow, 0.0))
            own.step(dve.tensor_copy(trow[:, 0:NE], iota[:, 0:NE]))
            own.step(dve.tensor_scalar(trow[:, NCOL:NCOL + 1], rank[:, NE - 1:NE], float(NE), None, ALU.add))
            for k in range(MAXJOBS - NE):
                own.step(dve.tensor_scalar(shift, which, k + 1.0, None, ALU.is_equal))
                s8 = shift.unsqueeze(1).broadcast_to([P, T, NE])
                own.step(dve.tensor_tensor(l2, pos8, s8, ALU.mult))
                own.step(dve.reduce_sum(jpos[:, :, NE + k:NE + k + 1].rearrange("p t o -> p (t o)"), l2, AX))
                own.step(dve.tensor_scalar(jpos[:, :, NE + k:NE + k + 1], jpos[:, :, NE + k:NE + k + 1],
                                           -float(P), None, ALU.add))
                own.step(dve.tensor_tensor(l2, gate8, s8, ALU.mult))
                own.step(dve.reduce_sum(jgate[:, :, NE + k:NE + k + 1].rearrange("p t o -> p (t o)"), l2, AX))
                own.step(dve.tensor_tensor(cand[:, 0, :], shift, iota[:, 0:NE], ALU.mult))
                own.step(dve.reduce_sum(trow[:, NE + k:NE + k + 1], cand[:, 0, :], AX))
            own.step(dve.tensor_copy(jtab[0:1, :], trow[0:1, :]))
            dve.sem_inc(tab_done, 1)

            dve.wait_ge(g_in, 16)
            for t in range(T):
                ins = dve.tensor_tensor(xn[:, t, :], xn[:, t, :], ysb[:, :], ALU.mult)
                own.step(ins)
            dve.sem_inc(hg_done, 1)

            def one_hot(col):
                for t in range(T):
                    dve.tensor_scalar(sel[:, t, :], iota[:, :], jpos[:, t, col], None, ALU.is_equal)
                    ins = dve.tensor_scalar(selg[:, t, :], iota[:, :], jpos[:, t, col], jgate[:, t, col],
                                            ALU.is_equal, ALU.mult)
                ins.then_inc(sel_done, 1)

            one_hot(slice(0, 1))

            def gather_lo(n, j):
                for b in range(2):
                    dve.wait_ge(xehi_done, after(n + b + 1, 2, j))
                    dve.tensor_tensor(alo[:, 4 * b:4 * b + 4, 0:P],
                                      ps[:, 2 + b, :].rearrange("p (k n) -> p k n", k=4),
                                      ahi[:, 4 * b:4 * b + 4, 0:P].bitcast(F32),
                                      ALU.subtract).then_inc(xelo_done, 1)

            gather_lo(0, None)
            jobs = dve.snap(dve.value_load(jtab[0:1, NCOL:NCOL + 1], min_val=NE, max_val=MAXJOBS))
            split.to(U_MOE + 4)
            with dve.Fori(0, jobs) as j:
                def side(place, u):
                    if place == 3:
                        dve.wait_ge(selT_ready, j + 1)
                        one_hot(bass.ds(j + 1, 1))

                split.j, split.next = j, U_MOE + 4
                u = feed_forward(U_MOE, STEPS, 1, j, side)
                gather_lo(2, j)
                split.to(u + 8)
                dve.wait_ge(unit_used, after(u + 4, JOB, j))
                dve.tensor_copy(ysb[:, CW:D], ps[:, 5, :]).then_inc(y1_done, 1)
                for k in range(4):
                    half, t = k // 2, k % 2
                    dve.wait_ge(sc_ready, 4 * j + k + 1)
                    cols = xres[:, t, half * CW:(half + 1) * CW]
                    dve.tensor_tensor(cols, cols, ps[:, 6 + t, :], ALU.add).then_inc(sc_done, 1)
                split.to(U_MOE + JOB + 4)
            split.j, split.next = jobs, U_MOE + 4
            dve.wait_ge(sc_done, jobs * 4)
            dve.sem_inc(x_done, 1)
            embedding(1, U_PROJ1, U_GATE1, 5, 7, 5, C_GATE1, jobs)


INPUTS = ["x", "p", "mix_norm_g", "ffn_norm_g", "attn_w_qkv", "attn_w_o", "attn_g_q", "attn_g_k",
          "attn_lam_q1", "attn_lam_k1", "attn_lam_q2", "attn_lam_k2", "attn_g_sub",
          "conv_w_pw1", "conv_b_pw1", "conv_w_dw", "conv_b_dw", "conv_ln_g", "conv_ln_b",
          "conv_w_pw2", "conv_b_pw2", "ffn_w_gate", "ffn_w_up", "ffn_w_down",
          "moe_w_router", "moe_b_router", "moe_w_gate", "moe_w_up", "moe_w_down",
          "ple_w_proj", "ple_norm_g", "ple_gate_norm_g", "ple_w_gate"]


def kernel(**inputs):
    import numpy as np
    import concourse.bacc as bacc
    from concourse.bass_utils import run_bass_kernel_spmd

    nc = bacc.Bacc("TRN2", target_bir_lowering=False, num_devices=1)
    arrays, args = {}, []
    for name in INPUTS:
        a = np.ascontiguousarray(inputs[name])
        arrays[f"in_{name}"] = a
        args.append(nc.dram_tensor(f"in_{name}", a.shape, mybir.dt.from_np(a.dtype), kind="ExternalInput").ap())
    args.append(nc.dram_tensor("out", inputs["x"].shape, F32, kind="ExternalOutput").ap())
    program(nc, *args)
    result = run_bass_kernel_spmd(nc, [arrays], core_ids=[0])
    return result.results[0]["out"]
```

```python
from contextlib import ExitStack

import concourse.bass as bass
from concourse import mybir

F32 = mybir.dt.float32
F32R = mybir.dt.float32r
I32 = mybir.dt.int32
ACT = mybir.ActivationFunctionType
ALU = mybir.AluOpType
AX = mybir.AxisListType.X

P = 128
CW = 512
UNIT = 2 * CW
N_CONSTS = 18
DVE_BLOCKS = [0, 1, 2, 3, 4]
PE_BLOCKS = [5, 6, 7]
RING = 14
SPLIT = 4


def program(nc, x, p, mix_norm_g, ffn_norm_g, attn_w_qkv, attn_w_o, attn_g_q, attn_g_k,
            attn_lam_q1, attn_lam_k1, attn_lam_q2, attn_lam_k2, attn_g_sub,
            conv_w_pw1, conv_b_pw1, conv_w_dw, conv_b_dw, conv_ln_g, conv_ln_b,
            conv_w_pw2, conv_b_pw2, ffn_w_gate, ffn_w_up, ffn_w_down,
            moe_w_router, moe_b_router, moe_w_gate, moe_w_up, moe_w_down,
            ple_w_proj, ple_norm_g, ple_gate_norm_g, ple_w_gate, out):
    _, S, D = x.shape
    T = S // P
    KT = D // P
    FF = ffn_w_gate.shape[2]
    STEPS = FF // CW
    NE = moe_w_router.shape[2]
    H = attn_w_o.shape[1] // P
    HD = P // 2
    TAPS = conv_w_dw.shape[1]
    NQKV = attn_w_qkv.shape[2] // CW
    NO = D // CW
    MAXJOBS = NE + (2 * S) // (P + 1)
    NCOL = MAXJOBS + 1
    LAM0 = 0.2
    assert (T, KT, STEPS, NE, H, NQKV, NO) == (2, 8, 7, 8, 8, 6, 2) and 3 * STEPS * 2 % RING == 0
    EPS, LN_EPS = 1e-6, 1e-5
    NEG = -1e30

    U_QKV = 0
    U_WO = U_QKV + 4 * NQKV
    U_FFN = U_WO + 4 * NO
    JOB = 3 * STEPS * 4
    U_PROJ0 = U_FFN + JOB - 4
    U_GATE0 = U_FFN + JOB + 2
    U_PW1 = U_GATE0 + 4 * NO
    U_PW2 = U_PW1 + 16
    U_MOE = U_PW2 + 4 * NO
    U_PROJ1 = U_MOE
    U_GATE1 = U_PROJ1 + 2
    U_END = U_GATE1 + 4 * NO
    C_QKV, C_WO, C_GATE0, C_PW1, C_PW2, C_GATE1 = 0, 6, 8, 10, 14, 16

    wqkv, wo = attn_w_qkv[0], attn_w_o[0]
    wpw1, wpw2 = conv_w_pw1[0], conv_w_pw2[0]

    with ExitStack() as ctx:
        def sb(name, shape, dt=F32, to=ctx):
            return to.enter_context(nc.sbuf_tensor(name, shape, dt))

        def sem(name):
            return ctx.enter_context(nc.semaphore(name))

        ring = sb("weight_ring", [P, RING, 2 * UNIT])
        whi = sb("weight_hi", [P, SPLIT, UNIT], F32R)
        wlo = sb("weight_lo", [P, SPLIT, UNIT], F32R)
        xres = sb("residual", [P, T, D])
        ident = sb("identity", [P, P])
        iota = sb("iota", [P, P])
        upper = sb("strict_upper", [P, P])
        ones = sb("ones", [P, P])
        vecs = sb("column_vectors", [P, 96])
        taps = sb("conv_taps", [P, TAPS * KT])
        mask = sb("causal_mask", [P, 3 * P])
        small = sb("small", [P, 160])
        wr = sb("router_raw", [P, KT, NE])
        wrhi = sb("router_hi", [P, KT, NE], F32R)
        wrlo = sb("router_lo", [P, KT, NE], F32R)
        rbias = sb("router_bias", [P, NE])
        jpos = sb("job_positions", [P, T, NCOL])
        jgate = sb("job_gates", [P, T, NCOL])
        jtab = sb("job_table", [1, 16], I32)
        def overlay(*specs):
            with ExitStack() as phase:
                return [sb(name, shape, dt, phase) for name, shape, dt in specs]

        hhi, = overlay(("h_rows_hi", [P, T, D], F32R))
        xn = sb("normed", [P, T, D])
        ahi, alo = overlay(("act_hi", [P, KT, S], F32R), ("act_lo", [P, KT, S], F32R))
        prob, amix, amixT = overlay(("prob", [P, 3, 2, 3 * P], F32), ("mixed_prob", [P, 2, 3 * P], F32),
                                    ("mixed_prob_T", [P, 2, 3 * P], F32))
        xehi, xelo, hlo = overlay(("job_act_hi", [P, KT, P], F32R), ("job_act_lo", [P, KT, P], F32R),
                                  ("h_rows_lo", [P, T, D], F32R))
        sb("act_region", [P, 2 * KT * S])
        v_sb, qT, kT, lamv = overlay(("values", [P, T, D], F32), ("q_T", [P, H, S], F32),
                                     ("k_T", [P, H, S], F32), ("lambda_vectors", [P, 4, HD], F32))
        sg, hid, hThi, hTlo, ysb, sel, selg, selT = overlay(
            ("silu_gate", [P, T, CW], F32), ("hidden", [P, T, CW], F32),
            ("hidden_T_hi", [P, T, CW], F32R), ("hidden_T_lo", [P, T, CW], F32R),
            ("expert_out", [P, D], F32), ("one_hot", [P, T, P], F32R),
            ("one_hot_gated", [P, T, P], F32), ("one_hot_gated_T", [P, S], F32))
        hrow, = overlay(("h_rows", [P, T, D], F32))
        cT, cy, csq = overlay(("conv_in_T", [P, KT, TAPS - 1 + S], F32), ("conv_out_T", [P, KT, S], F32),
                              ("conv_square", [P, KT, S], F32))
        emb, _, sgm, gbc, pThi, pTlo = overlay(
            ("embedding", [P, T, D], F32), ("beside_hidden_T", [P, D], F32), ("gate_sigmoid", [P, T, CW], F32),
            ("norm_row", [P, D], F32), ("p_T_hi", [P, 2, S], F32R), ("p_T_lo", [P, 2, S], F32R))
        _, pnat = overlay(("before_p_rows", [P, 3 * D], F32), ("p_rows", [P, T, 2 * P], F32))
        sb("stage_region", [P, KT * (TAPS - 1 + S) + 2 * KT * S])
        diag = csq[:, :, :].rearrange("p k (a n) -> p (k a) n", n=P)
        NDIAG = 2 * KT

        ps = ctx.enter_context(nc.psum_tensor("psum", [P, 8, CW], F32))

        eps, lneps = small[:, 0:1], small[:, 1:2]
        ssum, std, rstd = small[:, 2:4], small[:, 4:6], small[:, 6:8]
        ssq = small[:, 142:146]
        hsq, hstd, hrstd = small[:, 8:24], small[:, 24:40], small[:, 40:56]
        neglam, lamsum, lamexp = small[:, 56:57], small[:, 57:59], small[:, 59:61]
        gsub = small[:, 61:62]
        mx, nmx = small[:, 64:68], small[:, 68:80]
        psum_e, pinv = small[:, 80:92], small[:, 92:96]
        logits = small[:, 96:112].rearrange("p (t e) -> p t e", t=T)

        V_MIX, V_FFN, V_PLEG, V_BPW1, V_BDW, V_LNG, V_LNB, V_GQ, V_GK, V_GSUB = \
            0, 16, 32, 48, 64, 72, 80, 88, 89, 90
        NV = 91
        TAPROWS = TAPS * KT // 2
        stage_v = kT[0:NV, 0, 0:P]
        stage_t = [kT[0:TAPROWS, 1, 0:P], kT[0:TAPROWS, 2, 0:P]]

        piece_in = [sem(f"piece_in{i}") for i in range(RING)]
        hi_done = sem("hi_done")
        lo_done = sem("lo_done")
        unit_used = sem("unit_used")
        consts_in = sem("consts_in")
        x_in = sem("x_in")
        p_in = sem("p_in")
        g_in = sem("g_in")
        b_in = sem("b_in")
        masks_done = sem("masks_done")
        pool_seq = sem("pool_seq")
        vecsT_ready = sem("vecsT_ready")
        vecs_done = sem("vecs_done")
        wr_done = sem("wr_done")
        lam_part = sem("lam_part")
        first_a = sem("first_a")
        first_d = sem("first_d")
        first_std = sem("first_std")
        xn_done = sem("xn_done")
        x_half = sem("x_half")
        ssq_a = sem("ssq_a")
        ssq_d = sem("ssq_d")
        sum_done = sem("sum_done")
        std_done = sem("std_done")
        rstd_done = sem("rstd_done")
        tp_ready = sem("tp_ready")
        ahi_done = sem("ahi_done")
        alo_done = sem("alo_done")
        chunk_free = sem("chunk_free")
        qk_sq = sem("qk_sq")
        qk_ssq = sem("qk_ssq")
        qk_std = sem("qk_std")
        qk_n = sem("qk_n")
        qkT_ready = sem("qkT_ready")
        qkT_done = sem("qkT_done")
        v_done = sem("v_done")
        s_ready = sem("scores_ready")
        sm_done = sem("masked_done")
        exp_done = sem("exp_done")
        am_done = sem("mixed_done")
        amT_ready = sem("mixedT_ready")
        amT_done = sem("mixedT_done")
        o_ready = sem("o_ready")
        o_done = sem("o_done")
        on_step = sem("o_norm_step")
        silu_done = sem("silu_done")
        h_done = sem("h_done")
        hT_ready = sem("hT_ready")
        hThi_done = sem("hThi_done")
        hTlo_done = sem("hTlo_done")
        pT_ready = sem("pT_ready")
        pThi_done = sem("pThi_done")
        pTlo_done = sem("pTlo_done")
        e_sq = sem("e_sq")
        e_std = sem("e_std")
        e_done = sem("e_done")
        sgm_done = sem("sgm_done")
        rdiag_done = sem("rdiag_done")
        rbc_ready = sem("rbc_ready")
        rbc_done = sem("rbc_done")
        glu_in = sem("glu_in")
        glu_sig = sem("glu_sig")
        glu_done = sem("glu_done")
        diag_done = sem("diag_done")
        diag_used = sem("diag_used")
        convp_done = sem("convp_done")
        conv_done = sem("conv_done")
        mean_ready = sem("mean_ready")
        mean_done = sem("mean_done")
        cent_done = sem("centred_done")
        csq_done = sem("csq_done")
        var_ready = sem("var_ready")
        cstd_done = sem("cstd_done")
        cn_done = sem("conv_normed_done")
        cs_done = sem("conv_silu_done")
        log_ready = sem("logits_ready")
        r_step = sem("router_exp")
        rm_done = sem("route_mask_done")
        cnt_ready = sem("counts_ready")
        tab_done = sem("job_table_done")
        hf_done = sem("h_rows_done")
        hhi_done = sem("h_rows_hi_done")
        hlo_done = sem("h_rows_lo_done")
        sel_done = sem("one_hot_done")
        xe_ready = sem("gather_ready")
        xehi_done = sem("gather_hi_done")
        xelo_done = sem("gather_lo_done")
        selT_ready = sem("one_hot_T_ready")
        selT_done = sem("one_hot_T_done")
        y0_done = sem("y0_done")
        y1_done = sem("y1_done")
        sc_ready = sem("scatter_ready")
        sc_done = sem("scatter_added")
        dve_seq = sem("dve_seq")
        act_seq = sem("act_seq")
        stored = sem("stored")

        def after(n, per, j):
            return n if j is None else j * per + n

        class Splitter:

            def __init__(self, one):
                self.next, self.one, self.j = 0, one, None

            def to(self, n):
                while self.next < n:
                    self.one(self.next, self.j)
                    self.next += 1

        class Order:

            def __init__(self, eng, s):
                self.eng, self.s, self.n = eng, s, 0

            def add(self, ins):
                ins.then_inc(self.s, 1)
                self.n += 1
                return self.n

            def wait(self, n):
                self.eng.wait_ge(self.s, n)

            def step(self, ins):
                self.wait(self.add(ins))

        def raw(u):
            return ring[:, (u // 2) % RING, (u % 2) * UNIT:(u % 2 + 1) * UNIT]

        block = ctx.enter_context(nc.Block())

        @block.sync
        def _(sp):
            def load(piece, src, j, kt=4):
                slot = piece % RING
                if piece >= RING:
                    sp.wait_ge(lo_done, after(2 * (piece - RING) + 2, JOB, j))
                dst = ring[:, slot, :].rearrange("p (t n) -> p t n", t=kt)
                sp.dma_start(dst, src).then_inc(piece_in[slot], 16)

            def columns(first, w, chunk, j=None):
                for k in range(2):
                    load(first + k, w[k * 4 * P:(k + 1) * 4 * P, chunk * CW:(chunk + 1) * CW]
                         .rearrange("(t p) n -> p t n", p=P), j)

            def feed_forward(first, wg, wu, wd, j=None, proj=None):
                def rows(at, s):
                    for half in range(2):
                        load(at + half, wd[s * CW:(s + 1) * CW, half * CW:(half + 1) * CW]
                             .rearrange("(t p) n -> p t n", p=P), j)
                at = first
                for s in range(STEPS):
                    columns(at, wg, s, j)
                    at += 2
                    if s:
                        rows(at, s - 1)
                        at += 2
                    columns(at, wu, s, j)
                    at += 2
                if proj is not None:
                    load(at, proj.rearrange("(t p) n -> p t n", p=P), None, 2)
                    at += 1
                rows(at, STEPS - 1)

            for t in range(T):
                sp.dma_start(xres[:, t, :], x[0, t * P:(t + 1) * P, :]).then_inc(x_in, 16)
            sp.wait_ge(consts_in, 16 * N_CONSTS)
            for c in range(NQKV):
                columns((U_QKV + 4 * c) // 2, wqkv, c)
            for c in range(NO):
                columns((U_WO + 4 * c) // 2, wo, c)
            feed_forward(U_FFN // 2, ffn_w_gate[0], ffn_w_up[0], ffn_w_down[0],
                         proj=ple_w_proj[0])
            for c in range(NO):
                columns((U_GATE0 + 4 * c) // 2, ple_w_gate[0], c)
            for i, c in enumerate((0, 2, 1, 3)):
                columns((U_PW1 + 4 * i) // 2, wpw1, c)
            for c in range(NO):
                columns((U_PW2 + 4 * c) // 2, wpw2, c)
            feed_forward(U_MOE // 2, moe_w_gate[0, 0], moe_w_up[0, 0], moe_w_down[0, 0])
            sp.wait_ge(tab_done, 1)
            jobs = sp.snap(sp.value_load(jtab[0:1, NCOL:NCOL + 1], min_val=NE, max_val=MAXJOBS))
            with sp.Fori(1, jobs) as j:
                e = sp.snap(sp.value_load(jtab[0:1, bass.ds(j, 1)], min_val=0, max_val=NE - 1))
                feed_forward(U_MOE // 2, *(w[0, bass.ds(e, 1), :, :].rearrange("a k n -> (a k) n")
                                           for w in (moe_w_gate, moe_w_up, moe_w_down)), j)
            load(U_PROJ1 // 2, ple_w_proj[1].rearrange("(t p) n -> p t n", p=P), jobs, 2)
            for c in range(NO):
                columns((U_GATE1 + 4 * c) // 2, ple_w_gate[1], c, jobs)
            for c in range(NO):
                sp.wait_ge(x_half, 11 + c)
                sp.dma_start(out[0].rearrange("(t p) d -> p t d", p=P)[:, :, c * CW:(c + 1) * CW],
                             xres[:, :, c * CW:(c + 1) * CW]).then_inc(stored, 16)
            sp.wait_ge(stored, 32)

        @block.gpsimd
        def _(pool):
            pool.memset(ident[:, :], 0.0).then_inc(pool_seq, 1)
            pool.memset(mask[:, :], 0.0).then_inc(pool_seq, 1)
            pool.memset(ones[:, :], 1.0).then_inc(pool_seq, 1)
            pool.wait_ge(pool_seq, 3)
            pool.affine_select(out=ident[:, :], in_=ident[:, :], compare_op=ALU.not_equal, fill=1.0,
                               base=0, pattern=[[-1, P]], channel_multiplier=1).then_inc(masks_done, 1)
            for at in (0, 2 * P):
                pool.affine_select(out=mask[:, at:at + P], in_=mask[:, at:at + P], compare_op=ALU.is_ge,
                                   fill=NEG, base=0, pattern=[[-1, P]],
                                   channel_multiplier=1).then_inc(masks_done, 1)
            pool.affine_select(out=upper[:, :], in_=ones[:, :], compare_op=ALU.is_gt, fill=0.0,
                               base=0, pattern=[[1, P]], channel_multiplier=-1).then_inc(masks_done, 1)
            pool.iota(iota[:, :], pattern=[[1, P]], base=0, channel_multiplier=0,
                      allow_small_or_imprecise_dtypes=True).then_inc(masks_done, 1)

            def embedding_inputs(i, updates):
                pool.wait_ge(x_half, updates)
                pool.dma_start(pnat[:, :, :], p[i, 0].rearrange("(t p) d -> p t d", p=P)).then_inc(p_in, 16)
                pool.dma_start(gbc[:, :], ple_norm_g[i:i + 1, :].broadcast_to([P, D])).then_inc(p_in, 16)

            embedding_inputs(0, 1)
            pool.wait_ge(cn_done, 1)
            pool.dma_start(cT[:, 0:4, 0:2 * P], conv_b_pw2[0:1, :].rearrange("a (c n) -> a c n", c=4)
                           .broadcast_to([P, 4, 2 * P])).then_inc(b_in, 16)
            pool.wait_ge(alo_done, 24)
            pool.dma_start(ysb[:, :], ffn_norm_g[1:2, :].broadcast_to([P, D])).then_inc(g_in, 16)
            embedding_inputs(1, 10)

        @block.tensor
        def _(pe):
            def wait_unit(u, j):
                pe.wait_ge(lo_done, after(u + 1, JOB, j))

            def three(dst, ahi_, alo_, bhi_, blo_, first, last, **kw):
                pe.matmul(dst, ahi_, bhi_, start=first, stop=False, **kw)
                pe.matmul(dst, ahi_, blo_, start=False, stop=False, **kw)
                return pe.matmul(dst, alo_, bhi_, start=False, stop=last, **kw)

            def linear_unit(u, i, banks, tiles, j=None, ah=ahi, al=alo):
                wait_unit(u, j)
                s = u % SPLIT
                for k in range(2):
                    kt = 2 * i + k
                    cols = slice(k * CW, (k + 1) * CW)
                    for t in range(tiles):
                        rows = slice(t * P, (t + 1) * P)
                        last = three(ps[:, banks + t, :], ah[:, kt, rows], al[:, kt, rows],
                                     whi[:, s, cols], wlo[:, s, cols], kt == 0, kt == KT - 1)
                last.then_inc(unit_used, 1)

            def transpose_half(src, half):
                for b in range(2):
                    bank = 4 + 2 * half + b
                    for k in range(2):
                        for t in range(T):
                            kt = 4 * half + 2 * b + k
                            at = k * S + t * P
                            last = pe.transpose(ps[:, bank, at:at + P], src[:, t, kt * P:(kt + 1) * P],
                                                ident[:, :])
                    last.then_inc(tp_ready, 1)

            def x_transpose(update, half):
                pe.wait_ge(x_half, 2 * (update - 1) + half + 1)
                transpose_half(xres, half)

            def linear(u0, c0, chunks, stage, update=None):
                for c in range(chunks):
                    if c0 + c >= 2:
                        pe.wait_ge(chunk_free, c0 + c - 1)
                    for i in range(4):
                        if c == 0:
                            pe.wait_ge(alo_done, 4 * stage + i + 1)
                        linear_unit(u0 + 4 * c + i, i, 2 * ((c0 + c) % 2), T)
                        if update is not None and c == 1 and i == 1:
                            x_transpose(update, 0)

            def hidden_transpose(n, tiles, j):
                pe.wait_ge(h_done, after(n, STEPS, j))
                for t in range(tiles):
                    for k in range(4):
                        last = pe.transpose(ps[:, 2 // (3 - tiles) + t, k * P:(k + 1) * P],
                                            hid[:, t, k * P:(k + 1) * P], ident[:, :])
                last.then_inc(hT_ready, 1)

            def down(u, n, s, tiles, j, side=lambda place: None):
                pe.wait_ge(hTlo_done, after(n, STEPS, j))
                for i in range(4):
                    half = i // 2
                    wait_unit(u + i, j)
                    for k in range(2):
                        kt = 2 * (i % 2) + k
                        cols = slice(k * CW, (k + 1) * CW)
                        for t in range(tiles):
                            last = three(ps[:, 4 + 2 * half + t, :], hThi[:, t, kt * P:(kt + 1) * P],
                                         hTlo[:, t, kt * P:(kt + 1) * P], whi[:, (u + i) % SPLIT, cols],
                                         wlo[:, (u + i) % SPLIT, cols], s == 0 and kt == 0,
                                         s == STEPS - 1 and kt == 3)
                    last.then_inc(unit_used, 1)
                    if s == STEPS - 1:
                        side(STEPS + 2 + i)

            def feed_forward(u0, n0, tiles, j, side, ah=ahi, al=alo, gap=0):
                u, up = u0, 2 // (3 - tiles)
                for s in range(STEPS):
                    n = n0 + s
                    if n:
                        pe.wait_ge(silu_done, after(n, STEPS, j))
                    for i in range(4):
                        if j is None and s == 0:
                            pe.wait_ge(alo_done, 8 + i + 1)
                        linear_unit(u + i, i, 0, tiles, j, ah, al)
                        if i == 1 and s:
                            hidden_transpose(n, tiles, j)
                        if i == 1 and not s:
                            side(-1)
                    u += 4
                    if s:
                        down(u, n, s - 1, tiles, j)
                        u += 4
                    side(s)
                    if s == 0 and n:
                        pe.wait_ge(hTlo_done, after(n, STEPS, j))
                    for i in range(4):
                        linear_unit(u + i, i, up, tiles, j, ah, al)
                    u += 4
                side(STEPS)
                hidden_transpose(n0 + STEPS, tiles, j)
                side(STEPS + 1)
                down(u + gap, n0 + STEPS, STEPS - 1, tiles, j, side)

            pe.wait_ge(consts_in, 16 * N_CONSTS)
            pe.wait_ge(masks_done, 5)
            pe.transpose(ps[:, 0, 0:NV], stage_v, ident[0:NV, 0:NV])
            pe.transpose(ps[:, 0, P:P + TAPROWS], stage_t[0], ident[0:TAPROWS, 0:TAPROWS])
            pe.transpose(ps[:, 0, 2 * P:2 * P + TAPROWS], stage_t[1],
                         ident[0:TAPROWS, 0:TAPROWS]).then_inc(vecsT_ready, 1)

            pe.wait_ge(vecs_done, 1)
            pe.wait_ge(xn_done, 2)
            for half in range(2):
                transpose_half(xn, half)
            for c in range(NQKV):
                if c >= 2:
                    pe.wait_ge(chunk_free, c - 1)
                for i in range(4):
                    if c == 0:
                        pe.wait_ge(alo_done, i + 1)
                    linear_unit(U_QKV + 4 * c + i, i, 2 * (c % 2), T)
                    if i == 1 and 1 <= c <= 4:
                        pe.wait_ge(qk_n, c)
                        if c >= 2:
                            pe.wait_ge(qkT_done, c - 1)
                        for t in range(T):
                            for h in range(4):
                                last = pe.transpose(ps[:, 4 + t, h * P:(h + 1) * P],
                                                    xn[:, t, h * P:(h + 1) * P], ident[:, :])
                        last.then_inc(qkT_ready, 1)

            def scores(h):
                if h >= 2:
                    pe.wait_ge(sm_done, h - 1)
                for c in range(2):
                    rows = slice(c * HD, (c + 1) * HD)
                    b = 2 * (h % 2) + c
                    pe.matmul(ps[:, b, 0:P], qT[rows, h, 0:P], kT[rows, h, 0:P], start=True, stop=True)
                    last = pe.matmul(ps[:, b, P:3 * P], qT[rows, h, P:S], kT[rows, h, 0:S],
                                     start=True, stop=True)
                last.then_inc(s_ready, 1)

            def head_out(h):
                pe.wait_ge(amT_done, h + 1)
                if h >= 2:
                    pe.wait_ge(o_done, h - 1)
                b, e = 6 + h % 2, slice(h * P, (h + 1) * P)
                pe.matmul(ps[:, b, 0:P], amixT[:, h % 2, 0:P], v_sb[:, 0, e], start=True, stop=True)
                pe.matmul(ps[:, b, P:S], amixT[:, h % 2, P:2 * P], v_sb[:, 0, e], start=True, stop=False)
                pe.matmul(ps[:, b, P:S], amixT[:, h % 2, 2 * P:3 * P], v_sb[:, 1, e],
                          start=False, stop=True).then_inc(o_ready, 1)

            pe.wait_ge(qkT_done, 4)
            pe.wait_ge(v_done, 2)
            scores(0)
            scores(1)
            for h in range(H):
                if h + 2 < H:
                    scores(h + 2)
                pe.wait_ge(am_done, h + 1)
                if h >= 2:
                    pe.wait_ge(amT_done, h - 1)
                for k in range(3):
                    last = pe.transpose(ps[:, 4 + h % 2, k * P:(k + 1) * P],
                                        amix[:, h % 2, k * P:(k + 1) * P], ident[:, :])
                last.then_inc(amT_ready, 1)
                if h:
                    head_out(h - 1)
            head_out(H - 1)
            pe.wait_ge(on_step, 3)
            for half in range(2):
                transpose_half(xn, half)
            linear(U_WO, C_WO, NO, 1, update=1)

            def p_transpose(i, bank):
                pe.wait_ge(p_in, 32 * (i + 1))
                for k in range(2):
                    for t in range(T):
                        last = pe.transpose(ps[:, bank, k * S + t * P:k * S + (t + 1) * P],
                                            pnat[:, t, k * P:(k + 1) * P], ident[:, :])
                last.then_inc(pT_ready, 1)

            def p_project(u, j, i):
                pe.wait_ge(pTlo_done, i + 1)
                for k in range(2):
                    wait_unit(u + k, j)
                    s = (u + k) % SPLIT
                    for t in range(T):
                        if j is None and k == 0 and t == 1:
                            pe.wait_ge(hTlo_done, STEPS)
                        for half in range(2):
                            rows, cols = slice(t * P, (t + 1) * P), slice(half * CW, (half + 1) * CW)
                            last = three(ps[:, 2 * t + half, :], pThi[:, k, rows], pTlo[:, k, rows],
                                         whi[:, s, cols], wlo[:, s, cols], k == 0, k == 1)
                    last.then_inc(unit_used, 1)

            def dense_side(place):
                if place == -1:
                    x_transpose(1, 1)
                    pe.wait_ge(alo_done, 8 + 2)
                    p_transpose(0, 4)
                if place == STEPS + 1:
                    pe.wait_ge(silu_done, STEPS)
                    p_project(U_PROJ0, None, 0)
                if place == STEPS + 4:
                    x_transpose(2, 0)

            feed_forward(U_FFN, 0, T, None, dense_side, gap=2)

            def gate(u_gate, stage, update, i, j, late):
                pe.wait_ge(e_done, i + 1)
                for c in range(NO):
                    for n in range(4):
                        if c == 0:
                            pe.wait_ge(alo_done, 4 * stage + n + 1)
                        linear_unit(u_gate + 4 * c + n, n, 2 * c, T, j)
                        if n == 1:
                            late(c)

            gate(U_GATE0, 3, 3, 0, None, lambda c: x_transpose(2 + c, 1 - c))

            for c in range(4):
                pe.wait_ge(chunk_free, C_PW1 + c - 1)
                for i in range(4):
                    u = U_PW1 + 4 * c + i
                    if c == 0:
                        pe.wait_ge(alo_done, 16 + i + 1)
                    wait_unit(u, None)
                    for k in range(2):
                        kt = 2 * i + k
                        for b in range(4):
                            cols = slice(k * CW + b * P, k * CW + (b + 1) * P)
                            bank, at = 2 * (c % 2) + b // 2, (b % 2) * S
                            last = three(ps[:, bank, at:at + S], whi[:, u % SPLIT, cols],
                                         wlo[:, u % SPLIT, cols], ahi[:, kt, :], alo[:, kt, :],
                                         kt == 0 and b % 2 == 0, kt == KT - 1, skip_group_check=True)
                    last.then_inc(unit_used, 1)
                    if c == 0 and i == 1:
                        x_transpose(3, 1)
                if c == 0:
                    pe.wait_ge(rdiag_done, 1)
                    for t in range(T):
                        last = pe.matmul(ps[:, 4, t * P:(t + 1) * P], ones[:, :],
                                         xn[:, 0, S + t * P:S + (t + 1) * P], start=True, stop=True)
                    last.then_inc(rbc_ready, 1)
            n = 0
            pe.wait_ge(glu_done, 2)
            for ch in PE_BLOCKS:
                for k in range(TAPS):
                    pe.wait_ge(diag_done, n + 1)
                    pe.matmul(ps[:, ch - 1, 0:S], diag[:, n % NDIAG, :], cT[:, ch, k:k + S],
                              start=k == 0, stop=k == TAPS - 1).then_inc(diag_used, 1)
                    n += 1
            for n, ch in enumerate(DVE_BLOCKS[:4] + PE_BLOCKS + DVE_BLOCKS[4:]):
                if ch in PE_BLOCKS:
                    pe.wait_ge(convp_done, PE_BLOCKS.index(ch) + 1)
                else:
                    pe.wait_ge(conv_done, DVE_BLOCKS.index(ch) + 1)
                last = pe.matmul(ps[:, 7, 0:S], ones[:, :], cy[:, ch, :], start=n == 0, stop=n == KT - 1)
            last.then_inc(mean_ready, 1)
            for b in range(KT):
                pe.wait_ge(csq_done, b // 4 + 1)
                last = pe.matmul(ps[:, 3, 0:S], ones[:, :], csq[:, b, :], start=b == 0, stop=b == KT - 1)
            last.then_inc(var_ready, 1)
            linear(U_PW2, C_PW2, NO, 5, update=4)
            x_transpose(4, 1)

            for t in range(T):
                rows = slice(t * P, (t + 1) * P)
                for kt in range(KT):
                    pe.wait_ge(alo_done, 24 + kt // 2 + 1)
                    for a, b in ((ahi, wrhi), (ahi, wrlo), (alo, wrhi), (alo, wrlo)):
                        last = pe.matmul(ps[:, 0, t * NE:(t + 1) * NE], a[:, kt, rows], b[:, kt, :],
                                         start=kt == 0 and a is ahi and b is wrhi,
                                         stop=kt == KT - 1 and a is alo and b is wrlo)
            last.then_inc(log_ready, 1)
            pe.wait_ge(rm_done, 1)
            m = small[:, 112:128].rearrange("p (t e) -> p t e", t=T)
            pe.matmul(ps[:, 1, 0:NE], upper[:, :], m[:, 0, :], start=True, stop=True)
            pe.matmul(ps[:, 1, NE:2 * NE], ones[:, :], m[:, 0, :], start=True, stop=False)
            pe.matmul(ps[:, 1, NE:2 * NE], upper[:, :], m[:, 1, :], start=False, stop=True)
            pe.matmul(ps[:, 1, 2 * NE:3 * NE], ones[:, :], m[:, 0, :], start=True, stop=False)
            pe.matmul(ps[:, 1, 2 * NE:3 * NE], ones[:, :], m[:, 1, :], start=False,
                      stop=True).then_inc(cnt_ready, 1)

            def gather(bank):
                for k in range(4):
                    kt = 4 * (bank - 2) + k
                    cols = slice(kt * P, (kt + 1) * P)
                    for t in range(T):
                        pe.matmul(ps[:, bank, k * P:(k + 1) * P], hhi[:, t, cols], sel[:, t, :],
                                  start=t == 0, stop=False)
                        last = pe.matmul(ps[:, bank, k * P:(k + 1) * P], hlo[:, t, cols], sel[:, t, :],
                                         start=False, stop=t == T - 1)
                last.then_inc(xe_ready, 1)

            pe.wait_ge(hlo_done, T)
            pe.wait_ge(sel_done, 1)
            gather(2)
            gather(3)
            pe.wait_ge(tab_done, 1)
            jobs = pe.snap(pe.value_load(jtab[0:1, NCOL:NCOL + 1], min_val=NE, max_val=MAXJOBS))
            with pe.Fori(0, jobs) as j:
                def side(place):
                    if place == 2:
                        for t in range(T):
                            last = pe.transpose(ps[:, 3, t * P:(t + 1) * P], selg[:, t, :], ident[:, :])
                        last.then_inc(selT_ready, 1)
                    if place == STEPS:
                        pe.wait_ge(selT_done, j + 1)
                        pe.wait_ge(sel_done, j + 2)
                        gather(2)
                    if place == STEPS + 1:
                        gather(3)

                pe.wait_ge(xelo_done, 2 * j + 2)
                feed_forward(U_MOE, STEPS, 1, j, side, xehi, xelo)
                pe.wait_ge(y0_done, j + 1)
                for k in range(4):
                    half, t = k // 2, k % 2
                    if k == 2:
                        pe.wait_ge(y1_done, j + 1)
                    if k >= 2:
                        pe.wait_ge(sc_done, 4 * j + (k - 1))
                    pe.matmul(ps[:, 5 + 2 * t, :], selT[:, t * P:(t + 1) * P],
                              ysb[:, half * CW:(half + 1) * CW], start=True, stop=True).then_inc(sc_ready, 1)
            pe.wait_ge(x_half, 10)
            p_transpose(1, 0)
            p_project(U_PROJ1, jobs, 1)
            x_transpose(5, 0)
            x_transpose(5, 1)
            gate(U_GATE1, 7, 6, 1, jobs, lambda c: None)

        @block.scalar
        def _(act):
            def split_hi(u, j):
                act.wait_ge(piece_in[(u // 2) % RING],
                            after(16 * (u // 2 // RING + 1), 16 * (JOB // 2 // RING), j))
                if u >= SPLIT:
                    act.wait_ge(unit_used, after(u - SPLIT + 1, JOB, j))
                act.activation(whi[:, u % SPLIT, :], raw(u), ACT.Copy).then_inc(hi_done, 1)

            split = Splitter(split_hi)
            own = Order(act, act_seq)

            rows = [(V_MIX, mix_norm_g, 16), (V_FFN, ffn_norm_g, 16), (V_PLEG, ple_gate_norm_g, 16),
                    (V_BPW1, conv_b_pw1, 16), (V_BDW, conv_b_dw, 8), (V_LNG, conv_ln_g, 8),
                    (V_LNB, conv_ln_b, 8)]
            for at, src, n in rows:
                act.dma_start(kT[at:at + n, 0, 0:P], src.rearrange("l (c n) -> (l c) n", n=P)
                              ).then_inc(consts_in, 16)
            for at, src in ((V_GQ, attn_g_q), (V_GK, attn_g_k)):
                act.dma_start(kT[at:at + 1, 0, 0:P], src.rearrange("l c n -> l (c n)")).then_inc(consts_in, 16)
            act.dma_start(kT[V_GSUB:V_GSUB + 1, 0, 0:P], attn_g_sub).then_inc(consts_in, 16)
            tap_rows = conv_w_dw[0].rearrange("k (c n) -> (k c) n", n=P)
            for i in range(2):
                act.dma_start(stage_t[i], tap_rows[i * TAPROWS:(i + 1) * TAPROWS, :]).then_inc(consts_in, 16)
            for i, src in enumerate((attn_lam_q1, attn_lam_k1, attn_lam_q2, attn_lam_k2)):
                act.dma_start(lamv[:, i, :], src.broadcast_to([P, HD])).then_inc(consts_in, 16)
            act.dma_start(wr[:, :, :], moe_w_router[0].rearrange("(t p) e -> p t e", p=P)).then_inc(consts_in, 16)
            act.dma_start(rbias[:, :], moe_b_router.broadcast_to([P, NE])).then_inc(consts_in, 16)

            def square_half(r, half):
                act.wait_ge(x_half, 2 * (r - 1) + half + 1)
                cols = slice(half * CW, (half + 1) * CW)
                act.activation(xn[:, 0, cols], xres[:, 0, cols], ACT.Square,
                               accum_out=ssq[:, 2 * half:2 * half + 1]).then_inc(ssq_a, 1)

            def root(r):
                act.wait_ge(sum_done, r)
                act.activation(std, ssum, ACT.Sqrt, bias=eps, scale=1.0 / D).then_inc(std_done, 1)

            def hi_half(tp, half, gain):
                for b in range(2):
                    act.wait_ge(tp_ready, tp + 2 * half + b + 1)
                    for k in range(2):
                        kt = 4 * half + 2 * b + k
                        ins = act.activation(ahi[:, kt, :], ps[:, 4 + 2 * half + b, k * S:(k + 1) * S],
                                             ACT.Copy, scale=gain(kt))
                    ins.then_inc(ahi_done, 1)

            def vec(at):
                return lambda kt: vecs[:, at + kt:at + kt + 1]


            act.wait_ge(x_in, 16 * T)
            act.activation(xn[:, 0, :], xres[:, 0, :], ACT.Square, accum_out=ssum[:, 0:1]).then_inc(first_a, 1)
            act.wait_ge(first_a, 1)
            act.wait_ge(first_d, 1)
            act.activation(std, ssum, ACT.Sqrt, bias=eps, scale=1.0 / D).then_inc(first_std, 1)
            act.wait_ge(vecs_done, 1)
            for half in range(2):
                hi_half(0, half, vec(V_MIX))

            def qk_transposed(c):
                act.wait_ge(qkT_ready, c + 1)
                dst, gain = (qT, V_GQ) if c < 2 else (kT, V_GK)
                for t in range(T):
                    ins = act.activation(dst[:, 4 * (c % 2):4 * (c % 2) + 4, t * P:(t + 1) * P],
                                         ps[:, 4 + t, :].rearrange("p (h n) -> p h n", h=4), ACT.Copy,
                                         scale=vecs[:, gain:gain + 1])
                ins.then_inc(qkT_done, 1)

            for c in range(NQKV):
                q = U_QKV + 4 * c + 3
                pair = ps[:, 2 * (c % 2):2 * (c % 2) + 2, :]
                if c < 4:
                    split.to(q + 4)
                    act.wait_ge(unit_used, q + 1)
                    if c:
                        act.wait_ge(qk_ssq, c)
                    act.activation(xn[:, :, CW:D], pair, ACT.Square).then_inc(qk_sq, 1)
                    act.wait_ge(qk_ssq, c + 1)
                    act.activation(hstd, hsq, ACT.Sqrt, bias=eps, scale=1.0 / HD).then_inc(qk_std, 1)
                    split.to(q + 6)
                    qk_transposed(c)
                else:
                    split.to(q + 4)
                    act.wait_ge(unit_used, q + 1)
                    act.activation(v_sb[:, :, (c - 4) * CW:(c - 3) * CW], pair, ACT.Copy).then_inc(v_done, 1)

            act.activation(wrhi[:, :, :], wr[:, :, :], ACT.Copy).then_inc(wr_done, 1)
            act.wait_ge(lam_part, 1)
            act.activation(lamexp, lamsum, ACT.Exp).then_inc(lam_part, 1)

            def exps(h):
                act.wait_ge(sm_done, h + 1)
                for t in range(T):
                    for c in range(2):
                        i = 4 * (h % 3) + 2 * t + c
                        part = prob[:, h % 3, c, 0:P] if t == 0 else prob[:, h % 3, c, P:3 * P]
                        ins = act.activation(part, part, ACT.Exp, bias=nmx[:, i:i + 1],
                                             accum_out=psum_e[:, i:i + 1])
                ins.then_inc(exp_done, 1)

            def head_out(h):
                act.wait_ge(o_ready, h + 1)
                act.activation(xn[:, :, h * P:(h + 1) * P],
                               ps[:, 6 + h % 2, 0:S].rearrange("p (t n) -> p t n", t=T),
                               ACT.Copy).then_inc(o_done, 1)

            exps(0)
            for h in range(H):
                if h + 1 < H:
                    exps(h + 1)
                act.wait_ge(amT_ready, h + 1)
                if h >= 2:
                    act.wait_ge(o_ready, h - 1)
                act.activation(amixT[:, h % 2, :], ps[:, 4 + h % 2, 0:3 * P], ACT.Copy).then_inc(amT_done, 1)
                if h:
                    head_out(h - 1)
            head_out(H - 1)
            split.to(U_WO + 4)
            act.wait_ge(on_step, 1)
            act.activation(hstd, hsq, ACT.Sqrt, bias=eps, scale=1.0 / P).then_inc(on_step, 1)
            for half in range(2):
                hi_half(4, half, lambda kt: gsub)

            def feed_forward(u0, n0, tiles, j, side):
                u, up = u0, 2 // (3 - tiles)

                def hidden_hi(n):
                    act.wait_ge(hT_ready, after(n, STEPS, j))
                    act.activation(hThi[:, 0:tiles, :], ps[:, up:up + tiles, :], ACT.Copy).then_inc(hThi_done, 1)

                for s in range(STEPS):
                    n = n0 + s
                    if s:
                        split.to(u + 5)
                        hidden_hi(n)
                    split.to(u + 7)
                    act.wait_ge(unit_used, after(u + 4, JOB, j))
                    if n:
                        act.wait_ge(h_done, after(n, STEPS, j))
                    if tiles == 1:
                        ins = act.activation(sg[:, 0, :], ps[:, 0, :], ACT.Silu)
                    else:
                        for t in range(tiles):
                            ins = act.activation(sg[:, t, :], ps[:, t, :], ACT.Silu, scale=rstd[:, t:t + 1])
                    ins.then_inc(silu_done, 1)
                    side(s, u + 4)
                    u += 12 if s else 8
                side(STEPS, u)
                split.to(u + 4)
                hidden_hi(n0 + STEPS)
                return u

            q = U_WO + 7
            split.to(q + 2)
            square_half(1, 0)
            hi_half(8, 0, vec(V_FFN))
            split.to(q + 4)
            square_half(1, 1)
            split.to(q + 6)
            hi_half(8, 1, vec(V_FFN))
            act.wait_ge(pT_ready, 1)
            act.activation(pThi[:, :, :], ps[:, 4, :].rearrange("p (k n) -> p k n", k=2),
                           ACT.Copy).then_inc(pThi_done, 1)
            root(1)
            act.wait_ge(rstd_done, 1)
            feed_forward(U_FFN, 0, T, None, lambda place, u: None)

            def embed_root(i, u_proj, j):
                act.wait_ge(unit_used, after(u_proj + 2, JOB, j))
                for t in range(T):
                    ins = act.activation(emb[:, t, :], ps[:, 2 * t:2 * t + 2, :].rearrange("p b n -> p (b n)"),
                                         ACT.Square, accum_out=hsq[:, t:t + 1])
                own.step(ins)
                act.activation(hstd[:, 0:2], hsq[:, 0:2], ACT.Sqrt, bias=eps, scale=1.0 / D).then_inc(e_std, 1)

            def gate_sigmoid(i, c, q, j):
                act.wait_ge(unit_used, after(q + 1, JOB, j))
                if c:
                    act.wait_ge(chunk_free, (C_GATE1 if i else C_GATE0) + 1)
                for t in range(T):
                    ins = act.activation(sgm[:, t, :], ps[:, 2 * c + t, :], ACT.Sigmoid, scale=rstd[:, t:t + 1])
                ins.then_inc(sgm_done, 1)

            split.to(U_PROJ0 + 5)
            embed_root(0, U_PROJ0, None)
            q = U_GATE0 - 1
            split.to(q + 3)
            square_half(2, 0)
            hi_half(12, 0, vec(V_PLEG))
            split.to(q + 4)
            square_half(2, 1)
            split.to(q + 6)
            hi_half(12, 1, vec(V_PLEG))
            root(2)
            act.wait_ge(rstd_done, 2)
            q = U_GATE0 + 3
            split.to(q + 4)
            gate_sigmoid(0, 0, q, None)
            split.to(q + 6)
            square_half(3, 0)
            hi_half(16, 0, vec(V_MIX + KT))
            q += 4
            split.to(q + 4)
            gate_sigmoid(0, 1, q, None)

            split.to(q + 5)
            square_half(3, 1)
            split.to(q + 6)
            hi_half(16, 1, vec(V_MIX + KT))
            root(3)
            split.to(q + 8)
            act.wait_ge(rbc_ready, 1)
            act.activation(xn[:, 1, S:2 * S], ps[:, 4, 0:S], ACT.Copy).then_inc(rbc_done, 1)
            for cc in range(2):
                q = U_PW1 + 8 * cc + 7
                split.to(q + 4)
                act.wait_ge(glu_in, cc + 1)
                for b in range(4):
                    ch = 4 * cc + b
                    ins = act.activation(csq[:, b, :], csq[:, b, :], ACT.Sigmoid,
                                         bias=vecs[:, V_BPW1 + KT + ch:V_BPW1 + KT + ch + 1])
                ins.then_inc(glu_sig, 1)

            def conv_out(i):
                ch = PE_BLOCKS[i]
                act.wait_ge(diag_used, TAPS * (i + 1))
                act.activation(cy[:, ch, :], ps[:, ch - 1, 0:S], ACT.Identity,
                               bias=vecs[:, V_BDW + ch:V_BDW + ch + 1]).then_inc(convp_done, 1)

            split.to(U_PW2 + 4)
            act.wait_ge(glu_done, 2)
            n = 0
            for i, ch in enumerate(PE_BLOCKS):
                for k in range(TAPS):
                    if n >= NDIAG:
                        act.wait_ge(diag_used, n - NDIAG + 1)
                    act.activation(diag[:, n % NDIAG, :], ident[:, :], ACT.Copy,
                                   scale=taps[:, k * KT + ch:k * KT + ch + 1]).then_inc(diag_done, 1)
                    n += 1
                    if i and k == 4:
                        conv_out(i - 1)
            conv_out(len(PE_BLOCKS) - 1)
            act.wait_ge(mean_ready, 1)
            act.activation(xn[:, 0, 0:S], ps[:, 7, 0:S], ACT.Copy, scale=1.0 / D).then_inc(mean_done, 1)
            for b in range(2):
                act.wait_ge(cent_done, b + 1)
                act.activation(csq[:, 4 * b:4 * b + 4, :], cy[:, 4 * b:4 * b + 4, :],
                               ACT.Square).then_inc(csq_done, 1)
            act.wait_ge(var_ready, 1)
            act.activation(xn[:, 0, CW:CW + S], ps[:, 3, 0:S], ACT.Sqrt, bias=lneps,
                           scale=1.0 / D).then_inc(cstd_done, 1)
            for b in range(KT):
                act.wait_ge(cn_done, b // 2 + 1)
                act.activation(csq[:, b, :], cy[:, b, :], ACT.Silu, bias=vecs[:, V_LNB + b:V_LNB + b + 1],
                               scale=vecs[:, V_LNG + b:V_LNG + b + 1]).then_inc(cs_done, 1)
                if b % 2:
                    act.wait_ge(cs_done, b + 1)
                    act.activation(ahi[:, b - 1:b + 1, :], csq[:, b - 1:b + 1, :], ACT.Copy).then_inc(ahi_done, 1)

            q = U_PW2 + 7
            split.to(q + 2)
            square_half(4, 0)
            hi_half(20, 0, vec(V_FFN + KT))
            split.to(q + 4)
            square_half(4, 1)
            hi_half(20, 1, vec(V_FFN + KT))
            root(4)
            for t in range(T):
                act.wait_ge(hf_done, t + 1)
                act.activation(hhi[:, t, :], hrow[:, t, :], ACT.Copy).then_inc(hhi_done, 1)
            act.wait_ge(r_step, 1)
            act.activation(small[:, 140:142], small[:, 138:140], ACT.Exp).then_inc(r_step, 1)

            def gather_hi(n, j):
                for b in range(2):
                    act.wait_ge(xe_ready, after(n + b + 1, 2, j))
                    act.activation(xehi[:, 4 * b:4 * b + 4, :],
                                   ps[:, 2 + b, :].rearrange("p (k n) -> p k n", k=4),
                                   ACT.Copy).then_inc(xehi_done, 1)

            gather_hi(0, None)
            split.to(U_MOE + 4)
            act.wait_ge(tab_done, 1)
            jobs = act.snap(act.value_load(jtab[0:1, NCOL:NCOL + 1], min_val=NE, max_val=MAXJOBS))
            with act.Fori(0, jobs) as j:
                def side(place, u):
                    if place == 2:
                        split.to(u + 8)
                        act.wait_ge(selT_ready, j + 1)
                        act.activation(selT[:, :], ps[:, 3, 0:S], ACT.Copy).then_inc(selT_done, 1)

                split.j, split.next = j, U_MOE + 4
                u = feed_forward(U_MOE, STEPS, 1, j, side)
                gather_hi(2, j)
                split.to(u + 6)
                act.wait_ge(unit_used, after(u + 2, JOB, j))
                act.activation(ysb[:, 0:CW], ps[:, 4, :], ACT.Copy).then_inc(y0_done, 1)
                split.to(U_MOE + JOB + 4)
            split.j, split.next = jobs, U_MOE + 4
            act.wait_ge(pT_ready, 2)
            act.activation(pThi[:, :, :], ps[:, 0, :].rearrange("p (k n) -> p k n", k=2),
                           ACT.Copy).then_inc(pThi_done, 1)
            for half in range(2):
                square_half(5, half)
            root(5)
            split.to(U_GATE1 + 4)
            for half in range(2):
                hi_half(24, half, vec(V_PLEG + KT))
            embed_root(1, U_PROJ1, jobs)
            act.wait_ge(rstd_done, 5)
            for c in range(NO):
                split.to(U_END)
                gate_sigmoid(1, c, U_GATE1 + 4 * c + 3, jobs)

        @block.vector
        def _(dve):
            def split_lo(u, j):
                dve.wait_ge(hi_done, after(u + 1, JOB, j))
                dve.tensor_tensor(wlo[:, u % SPLIT, :], raw(u), whi[:, u % SPLIT, :].bitcast(F32),
                                  ALU.subtract).then_inc(lo_done, 1)

            split = Splitter(split_lo)
            own = Order(dve, dve_seq)

            def square_half(r, half):
                cols = slice(half * CW, (half + 1) * CW)
                dve.tensor_tensor_reduce(out=xn[:, 1, cols], in0=xres[:, 1, cols], in1=xres[:, 1, cols],
                                         scale=1.0, scalar=0.0, op0=ALU.mult, op1=ALU.add,
                                         accum_out=ssq[:, 2 * half + 1:2 * half + 2]).then_inc(ssq_d, 1)

            def root(r):
                dve.wait_ge(ssq_a, 2 * r)
                dve.wait_ge(ssq_d, 2 * r)
                dve.tensor_tensor(ssum, ssq[:, 0:2], ssq[:, 2:4], ALU.add).then_inc(sum_done, 1)
                dve.wait_ge(std_done, r)
                dve.reciprocal(rstd, std).then_inc(rstd_done, 1)
                dve.wait_ge(rstd_done, r)

            def lo_half(m, half, gain):
                for b in range(2):
                    dve.wait_ge(ahi_done, 4 * m + 2 * half + b + 1)
                    for k in range(2):
                        kt = 4 * half + 2 * b + k
                        ins = dve.scalar_tensor_tensor(alo[:, kt, :], ps[:, 4 + 2 * half + b, k * S:(k + 1) * S],
                                                       gain(kt), ahi[:, kt, :].bitcast(F32),
                                                       ALU.mult, ALU.subtract)
                    ins.then_inc(alo_done, 1)

            def add_half(half, q, banks, r):
                dve.wait_ge(unit_used, q + 1)
                cols = xres[:, :, half * CW:(half + 1) * CW]
                dve.tensor_tensor(cols, cols, ps[:, banks:banks + 2, :], ALU.add).then_inc(x_half, 1)
                dve.wait_ge(x_half, 2 * (r - 1) + half + 1)

            def vec(at):
                return lambda kt: vecs[:, at + kt:at + kt + 1]

            dve.memset(eps, EPS)
            dve.memset(lneps, LN_EPS)
            own.step(dve.memset(jpos[:, :, :], -1.0))
            own.step(dve.memset(jgate[:, :, :], 0.0))
            dve.wait_ge(x_in, 16 * T)
            dve.tensor_tensor_reduce(out=xn[:, 1, :], in0=xres[:, 1, :], in1=xres[:, 1, :], scale=1.0,
                                     scalar=0.0, op0=ALU.mult, op1=ALU.add,
                                     accum_out=ssum[:, 1:2]).then_inc(first_d, 1)
            dve.wait_ge(first_std, 1)
            own.step(dve.reciprocal(rstd, std))
            for t in range(T):
                dve.tensor_scalar(xn[:, t, :], xres[:, t, :], rstd[:, t:t + 1], None,
                                  ALU.mult).then_inc(xn_done, 1)
            dve.wait_ge(consts_in, 16 * N_CONSTS)
            own.step(dve.tensor_tensor(lamv[:, 0:4:2, :], lamv[:, 0:4:2, :], lamv[:, 1:4:2, :], ALU.mult))
            dve.reduce_sum(lamsum, lamv[:, 0:4:2, :], AX).then_inc(lam_part, 1)
            dve.wait_ge(vecsT_ready, 1)
            dve.tensor_copy(vecs[:, 0:NV], ps[:, 0, 0:NV])
            own.step(dve.tensor_copy(taps[:, :].rearrange("p (a n) -> p a n", a=2),
                                     ps[:, 0, P:3 * P].rearrange("p (a n) -> p a n", a=2)[:, :, 0:TAPROWS]))
            own.step(dve.tensor_scalar(gsub, vecs[:, V_GSUB:V_GSUB + 1], 1.0 - LAM0, None, ALU.mult))
            dve.sem_inc(vecs_done, 1)

            for half in range(2):
                lo_half(0, half, vec(V_MIX))
            for c in range(NQKV):
                q = U_QKV + 4 * c + 3
                pair = ps[:, 2 * (c % 2):2 * (c % 2) + 2, :]
                split.to(q + 4)
                if c < 4:
                    groups = "p t (g n) -> p t g n"
                    h16 = hsq.rearrange("p (t g) -> p t g", t=T)
                    dve.wait_ge(qk_sq, c + 1)
                    dve.tensor_reduce(h16, xn[:, :, CW:D].rearrange(groups, n=HD), AX,
                                      ALU.add).then_inc(qk_ssq, 1)
                    dve.wait_ge(qk_std, c + 1)
                    own.step(dve.reciprocal(hrstd, hstd))
                    if c:
                        dve.wait_ge(qkT_ready, c)
                    for t in range(T):
                        ins = dve.tensor_tensor(
                            xn[:, t, 0:CW].rearrange("p (g n) -> p g n", n=HD),
                            pair[:, t, :].rearrange("p (g n) -> p g n", n=HD),
                            hrstd[:, 8 * t:8 * t + 8].unsqueeze(2).broadcast_to([P, 8, HD]), ALU.mult)
                        own.step(ins)
                    dve.sem_inc(qk_n, 1)
                    dve.sem_inc(chunk_free, 1)
                else:
                    dve.wait_ge(v_done, c - 3)
                    dve.sem_inc(chunk_free, 1)

            def masked(h):
                dve.wait_ge(s_ready, h + 1)
                b = h % 3
                for c in range(2):
                    n = own.add(dve.scalar_tensor_tensor(prob[:, b, c, :], ps[:, 2 * (h % 2) + c, 0:3 * P],
                                                         HD ** -0.5, mask[:, :], ALU.mult, ALU.add))
                own.wait(n)
                dve.reduce_max(mx[:, 0:2], prob[:, b, :, 0:P], AX)
                own.step(dve.reduce_max(mx[:, 2:4], prob[:, b, :, P:3 * P], AX))
                dve.tensor_scalar(nmx[:, 4 * b:4 * b + 4], mx, -1.0, None, ALU.mult).then_inc(sm_done, 1)

            dve.wait_ge(masks_done, 5)
            masked(0)
            masked(1)
            dve.wait_ge(wr_done, 1)
            own.step(dve.tensor_tensor(wrlo[:, :, :], wr[:, :, :], wrhi[:, :, :].bitcast(F32), ALU.subtract))
            dve.wait_ge(lam_part, 2)
            own.step(dve.tensor_tensor(neglam, lamexp[:, 1:2], lamexp[:, 0:1], ALU.subtract))
            own.step(dve.tensor_scalar(neglam, neglam, -LAM0, None, ALU.add))
            for h in range(H):
                b, b3 = h % 2, h % 3
                dve.wait_ge(exp_done, h + 1)
                if h:
                    dve.wait_ge(am_done, h)
                own.step(dve.reciprocal(pinv, psum_e[:, 4 * b3:4 * b3 + 4]))
                own.step(dve.tensor_scalar(pinv[:, 1:4:2], pinv[:, 1:4:2], neglam, None, ALU.mult))
                if h >= 2:
                    dve.wait_ge(amT_ready, h - 1)
                parts = (slice(0, P), slice(P, 3 * P))
                for t in range(T):
                    n = own.add(dve.tensor_scalar(amix[:, b, parts[t]], prob[:, b3, 0, parts[t]],
                                                  pinv[:, 2 * t:2 * t + 1], None, ALU.mult))
                own.wait(n)
                for t in range(T):
                    ins = dve.scalar_tensor_tensor(amix[:, b, parts[t]], prob[:, b3, 1, parts[t]],
                                                   pinv[:, 2 * t + 1:2 * t + 2],
                                                   amix[:, b, parts[t]], ALU.mult, ALU.add)
                ins.then_inc(am_done, 1)
                if h + 2 < H:
                    masked(h + 2)
            split.to(U_WO + 4)
            dve.wait_ge(o_done, H)
            o16 = xn[:, :, :].rearrange("p t (h n) -> p (t h) n", n=P)
            sq16 = qT[:, :, :].rearrange("p h s -> p (h s)").rearrange("p (g n) -> p g n", n=P)
            own.step(dve.tensor_tensor(sq16, o16, o16, ALU.mult))
            dve.tensor_reduce(hsq, sq16, AX, ALU.add).then_inc(on_step, 1)
            dve.wait_ge(on_step, 2)
            own.step(dve.reciprocal(hrstd, hstd))
            dve.tensor_tensor(o16, o16, hrstd.unsqueeze(2).broadcast_to([P, T * H, P]),
                              ALU.mult).then_inc(on_step, 1)
            for half in range(2):
                lo_half(1, half, lambda kt: gsub)
            q = U_WO + 3
            split.to(q + 4)
            add_half(0, q, 0, 1)
            dve.sem_inc(chunk_free, 1)
            square_half(1, 0)
            q += 4
            split.to(q + 2)
            lo_half(2, 0, vec(V_FFN))
            split.to(q + 4)
            add_half(1, q, 2, 1)
            dve.sem_inc(chunk_free, 1)
            square_half(1, 1)
            split.to(q + 6)
            lo_half(2, 1, vec(V_FFN))

            def feed_forward(u0, n0, tiles, j, side):
                u, up = u0, 2 // (3 - tiles)

                def hidden(n):
                    dve.wait_ge(silu_done, after(n, STEPS, j))
                    if n > 1:
                        dve.wait_ge(hT_ready, after(n - 1, STEPS, j))
                    if tiles == 1:
                        ins = dve.tensor_tensor(hid[:, 0, :], sg[:, 0, :], ps[:, up, :], ALU.mult)
                    else:
                        for t in range(tiles):
                            ins = dve.scalar_tensor_tensor(hid[:, t, :], ps[:, up + t, :], rstd[:, t:t + 1],
                                                           sg[:, t, :], ALU.mult, ALU.mult)
                    ins.then_inc(h_done, 1)

                def hidden_lo(n):
                    dve.wait_ge(hThi_done, after(n, STEPS, j))
                    dve.tensor_tensor(hTlo[:, 0:tiles, :], ps[:, up:up + tiles, :],
                                      hThi[:, 0:tiles, :].bitcast(F32), ALU.subtract).then_inc(hTlo_done, 1)

                for s in range(STEPS):
                    n = n0 + s
                    if s:
                        split.to(u + 3)
                        dve.wait_ge(unit_used, after(u, JOB, j))
                        hidden(n)
                        split.to(u + 5)
                        hidden_lo(n)
                    side(s, u + 4)
                    u += 12 if s else 8
                split.to(u + 3)
                dve.wait_ge(unit_used, after(u, JOB, j))
                hidden(n0 + STEPS)
                split.to(u + 4)
                hidden_lo(n0 + STEPS)
                return u

            dve.wait_ge(pThi_done, 1)
            dve.tensor_tensor(pTlo[:, :, :], ps[:, 4, :].rearrange("p (k n) -> p k n", k=2),
                              pThi[:, :, :].bitcast(F32), ALU.subtract).then_inc(pTlo_done, 1)
            root(1)
            feed_forward(U_FFN, 0, T, None, lambda place, u: None)

            def embed_norm(i):
                dve.wait_ge(e_std, i + 1)
                own.step(dve.reciprocal(hrstd[:, 0:2], hstd[:, 0:2]))
                for t in range(T):
                    n = own.add(dve.scalar_tensor_tensor(
                        emb[:, t, :], ps[:, 2 * t:2 * t + 2, :].rearrange("p b n -> p (b n)"),
                        hrstd[:, t:t + 1], gbc[:, :], ALU.mult, ALU.mult))
                own.wait(n)
                dve.sem_inc(e_done, 1)

            def gated_add(i, c, r):
                dve.wait_ge(sgm_done, 2 * i + c + 1)
                cols = slice(c * CW, (c + 1) * CW)
                own.step(dve.tensor_tensor(emb[:, :, cols], emb[:, :, cols], sgm[:, :, :], ALU.mult))
                dve.sem_inc(chunk_free, 1)
                dve.tensor_tensor(xres[:, :, cols], xres[:, :, cols], emb[:, :, cols],
                                  ALU.add).then_inc(x_half, 1)
                dve.wait_ge(x_half, 2 * (r - 1) + c + 1)

            split.to(U_PROJ0 + 5)
            embed_norm(0)
            q = U_GATE0 - 1
            split.to(q + 2)
            add_half(0, q - 2, 4, 2)
            square_half(2, 0)
            split.to(q + 3)
            lo_half(3, 0, vec(V_PLEG))
            split.to(q + 4)
            add_half(1, q, 6, 2)
            square_half(2, 1)
            split.to(q + 6)
            lo_half(3, 1, vec(V_PLEG))
            root(2)
            q = U_GATE0 + 3
            split.to(q + 4)
            gated_add(0, 0, 3)
            square_half(3, 0)
            split.to(q + 6)
            lo_half(4, 0, vec(V_MIX + KT))
            q += 4
            split.to(q + 4)
            gated_add(0, 1, 3)
            square_half(3, 1)

            split.to(q + 6)
            lo_half(4, 1, vec(V_MIX + KT))
            root(3)
            for t in range(T):
                n = own.add(dve.tensor_scalar(xn[:, 0, S + t * P:S + (t + 1) * P], ident[:, :], rstd[:, t:t + 1],
                                              None, ALU.mult))
            own.wait(n)
            dve.sem_inc(rdiag_done, 1)
            own.step(dve.memset(cT[:, :, 0:TAPS - 1], 0.0))

            def glu_scale(cc):
                dve.wait_ge(unit_used, U_PW1 + 8 * cc + 8)
                rbc = xn[:, 1:2, S:2 * S].broadcast_to([P, 4, S])
                dve.tensor_tensor(csq[:, 0:4, :], ps[:, 2:4, :].rearrange("p b (a n) -> p (b a) n", n=S), rbc,
                                  ALU.mult).then_inc(glu_in, 1)
                own.step(dve.tensor_tensor(csq[:, 4:8, :], ps[:, 0:2, :].rearrange("p b (a n) -> p (b a) n", n=S),
                                           rbc, ALU.mult))
                dve.wait_ge(glu_in, cc + 1)
                dve.sem_inc(chunk_free, 2)

            def glu(cc):
                dve.wait_ge(glu_sig, cc + 1)
                for b in range(4):
                    ch = 4 * cc + b
                    n = own.add(dve.scalar_tensor_tensor(
                        cT[:, ch, TAPS - 1:TAPS - 1 + S], csq[:, 4 + b, :],
                        vecs[:, V_BPW1 + ch:V_BPW1 + ch + 1], csq[:, b, :], ALU.add, ALU.mult))
                own.wait(n)
                dve.sem_inc(glu_done, 1)

            q = U_PW1 + 7
            split.to(q + 4)
            dve.wait_ge(rbc_done, 1)
            glu_scale(0)
            glu(0)
            for blocks in (DVE_BLOCKS[:4], DVE_BLOCKS[4:]):
                first = blocks[0] == 0
                last_of = {}
                for k in range(TAPS):
                    if first and k < 5:
                        split.to(q + 5 + k)
                    if first and k == 11:
                        glu_scale(1)
                    if first and k == 13:
                        glu(1)
                    if first and 14 <= k < 18:
                        split.to(q + 9 + k - 13)
                    for ch in blocks:
                        src, w = cT[:, ch, k:k + S], taps[:, k * KT + ch:k * KT + ch + 1]
                        if k == 0:
                            last_of[ch] = own.add(dve.tensor_scalar(
                                cy[:, ch, :], src, w, vecs[:, V_BDW + ch:V_BDW + ch + 1], ALU.mult, ALU.add))
                            continue
                        own.wait(last_of[ch])
                        ins = dve.scalar_tensor_tensor(cy[:, ch, :], src, w, cy[:, ch, :], ALU.mult, ALU.add)
                        if k < TAPS - 1:
                            last_of[ch] = own.add(ins)
                        else:
                            ins.then_inc(conv_done, 1)
            dve.wait_ge(mean_done, 1)
            for b in range(2):
                dve.tensor_tensor(cy[:, 4 * b:4 * b + 4, :], cy[:, 4 * b:4 * b + 4, :],
                                  xn[:, 0:1, 0:S].broadcast_to([P, 4, S]), ALU.subtract).then_inc(cent_done, 1)
            dve.wait_ge(cstd_done, 1)
            own.step(dve.reciprocal(xn[:, 1, 0:S], xn[:, 0, CW:CW + S]))
            for b in range(4):
                dve.tensor_tensor(cy[:, 2 * b:2 * b + 2, :], cy[:, 2 * b:2 * b + 2, :],
                                  xn[:, 1:2, 0:S].broadcast_to([P, 2, S]), ALU.mult).then_inc(cn_done, 1)
            for b in range(4):
                dve.wait_ge(ahi_done, 20 + b + 1)
                dve.tensor_tensor(alo[:, 2 * b:2 * b + 2, :], csq[:, 2 * b:2 * b + 2, :],
                                  ahi[:, 2 * b:2 * b + 2, :].bitcast(F32), ALU.subtract).then_inc(alo_done, 1)
            dve.wait_ge(b_in, 16)
            for t in range(T):
                row4 = xres[:, t, :].rearrange("p (a n) -> p a n", a=4)
                n = own.add(dve.tensor_tensor(row4, row4, cT[:, 0:4, 0:2 * P], ALU.add))
            own.wait(n)
            q = U_PW2 + 3
            split.to(q + 4)
            add_half(0, q, 0, 4)
            dve.sem_inc(chunk_free, 1)
            square_half(4, 0)
            q += 4
            split.to(q + 2)
            lo_half(6, 0, vec(V_FFN + KT))
            split.to(q + 4)
            add_half(1, q, 2, 4)
            dve.sem_inc(chunk_free, 1)
            square_half(4, 1)
            lo_half(6, 1, vec(V_FFN + KT))
            root(4)
            dve.wait_ge(g_in, 16)
            for t in range(T):
                dve.scalar_tensor_tensor(hrow[:, t, :], xres[:, t, :], rstd[:, t:t + 1], ysb[:, :],
                                         ALU.mult, ALU.mult).then_inc(hf_done, 1)

            m12, g12 = small[:, 128:132], small[:, 132:136]
            pick = small[:, 112:128].rearrange("p (t e) -> p t e", t=T)
            tmp = selT[:, :].rearrange("p (i n) -> p i n", n=16)
            e3 = lambda i: tmp[:, i, :].rearrange("p (t e) -> p t e", t=T)
            back, oh1, oh2, cand, l2 = e3(0), e3(1), e3(2), e3(3), e3(4)
            row = lambda v: v.unsqueeze(2).broadcast_to([P, T, NE])
            iota8 = iota[:, 0:NE].unsqueeze(1).broadcast_to([P, T, NE])
            dve.wait_ge(log_ready, 1)
            own.step(dve.tensor_scalar(back, iota8, -1.0, float(NE), ALU.mult, ALU.add))
            for t in range(T):
                n = own.add(dve.scalar_tensor_tensor(logits[:, t, :], ps[:, 0, t * NE:(t + 1) * NE],
                                                     rstd[:, t:t + 1], rbias[:, :], ALU.mult, ALU.add))
            own.wait(n)

            def top(src, mval, hot):
                own.step(dve.reduce_max(mval, src, AX))
                own.step(dve.tensor_tensor(cand, src, row(mval), ALU.is_equal))
                own.step(dve.tensor_tensor(cand, cand, back, ALU.mult))
                own.step(dve.reduce_max(g12[:, 0:2], cand, AX))
                own.step(dve.tensor_tensor(hot, back, row(g12[:, 0:2]), ALU.is_equal))

            top(logits, m12[:, 0:2], oh1)
            own.step(dve.scalar_tensor_tensor(l2, oh1, -3e38, logits, ALU.mult, ALU.add))
            top(l2, m12[:, 2:4], oh2)
            own.step(dve.tensor_tensor(pick, oh1, oh2, ALU.add))
            dve.sem_inc(rm_done, 1)
            dve.tensor_tensor(small[:, 138:140], m12[:, 2:4], m12[:, 0:2], ALU.subtract).then_inc(r_step, 1)
            for t in range(T):
                dve.wait_ge(hhi_done, t + 1)
                dve.tensor_tensor(hlo[:, t, :], hrow[:, t, :], hhi[:, t, :].bitcast(F32),
                                  ALU.subtract).then_inc(hlo_done, 1)
            dve.wait_ge(r_step, 2)
            own.step(dve.tensor_scalar(g12[:, 0:2], small[:, 140:142], 1.0, None, ALU.add))
            own.step(dve.reciprocal(g12[:, 0:2], g12[:, 0:2]))
            own.step(dve.tensor_tensor(g12[:, 2:4], g12[:, 0:2], small[:, 140:142], ALU.mult))
            own.step(dve.tensor_tensor(oh1, oh1, row(g12[:, 0:2]), ALU.mult))
            own.step(dve.tensor_tensor(oh2, oh2, row(g12[:, 2:4]), ALU.mult))
            gate8 = jgate[:, :, 0:NE]
            own.step(dve.tensor_tensor(gate8, oh1, oh2, ALU.add))
            FAR = 10000.0
            dve.wait_ge(cnt_ready, 1)
            pos8 = jpos[:, :, 0:NE]
            own.step(dve.tensor_scalar(pos8, ps[:, 1, 0:2 * NE].rearrange("p (t e) -> p t e", t=T), FAR, None, ALU.add))
            own.step(dve.tensor_tensor(pos8, pos8, pick, ALU.mult))
            own.step(dve.tensor_scalar(pos8, pos8, -FAR, None, ALU.add))

            def one_hot(col):
                for t in range(T):
                    dve.tensor_scalar(sel[:, t, :], iota[:, :], jpos[:, t, col], None, ALU.is_equal)
                    ins = dve.tensor_scalar(selg[:, t, :], iota[:, :], jpos[:, t, col], jgate[:, t, col],
                                            ALU.is_equal, ALU.mult)
                ins.then_inc(sel_done, 1)

            one_hot(slice(0, 1))
            over, rank, shift, which = (tmp[:, 5 + i, 0:NE] for i in range(4))
            own.step(dve.tensor_scalar(over, ps[:, 1, 2 * NE:3 * NE], P + 0.5, None, ALU.is_gt))
            own.step(dve.tensor_copy(rank, over))
            for d in (1, 2, 4):
                own.step(dve.tensor_copy(shift, rank))
                own.step(dve.tensor_tensor(rank[:, d:NE], shift[:, d:NE], shift[:, 0:NE - d], ALU.add))
            own.step(dve.tensor_tensor(which, rank, over, ALU.mult))
            trow = tmp[:, 9, 0:16]
            own.step(dve.memset(trow, 0.0))
            own.step(dve.tensor_copy(trow[:, 0:NE], iota[:, 0:NE]))
            own.step(dve.tensor_scalar(trow[:, NCOL:NCOL + 1], rank[:, NE - 1:NE], float(NE), None, ALU.add))
            for k in range(MAXJOBS - NE):
                own.step(dve.tensor_scalar(shift, which, k + 1.0, None, ALU.is_equal))
                s8 = shift.unsqueeze(1).broadcast_to([P, T, NE])
                own.step(dve.tensor_tensor(l2, pos8, s8, ALU.mult))
                own.step(dve.reduce_sum(jpos[:, :, NE + k:NE + k + 1].rearrange("p t o -> p (t o)"), l2, AX))
                own.step(dve.tensor_scalar(jpos[:, :, NE + k:NE + k + 1], jpos[:, :, NE + k:NE + k + 1],
                                           -float(P), None, ALU.add))
                own.step(dve.tensor_tensor(l2, gate8, s8, ALU.mult))
                own.step(dve.reduce_sum(jgate[:, :, NE + k:NE + k + 1].rearrange("p t o -> p (t o)"), l2, AX))
                own.step(dve.tensor_tensor(cand[:, 0, :], shift, iota[:, 0:NE], ALU.mult))
                own.step(dve.reduce_sum(trow[:, NE + k:NE + k + 1], cand[:, 0, :], AX))
            own.step(dve.tensor_copy(jtab[0:1, :], trow[0:1, :]))
            dve.sem_inc(tab_done, 1)


            def gather_lo(n, j):
                for b in range(2):
                    dve.wait_ge(xehi_done, after(n + b + 1, 2, j))
                    dve.tensor_tensor(xelo[:, 4 * b:4 * b + 4, :],
                                      ps[:, 2 + b, :].rearrange("p (k n) -> p k n", k=4),
                                      xehi[:, 4 * b:4 * b + 4, :].bitcast(F32),
                                      ALU.subtract).then_inc(xelo_done, 1)

            gather_lo(0, None)
            jobs = dve.snap(dve.value_load(jtab[0:1, NCOL:NCOL + 1], min_val=NE, max_val=MAXJOBS))
            split.to(U_MOE + 4)
            with dve.Fori(0, jobs) as j:
                def side(place, u):
                    if place == 3:
                        dve.wait_ge(selT_ready, j + 1)
                        one_hot(bass.ds(j + 1, 1))

                split.j, split.next = j, U_MOE + 4
                u = feed_forward(U_MOE, STEPS, 1, j, side)
                gather_lo(2, j)
                split.to(u + 7)
                dve.wait_ge(unit_used, after(u + 4, JOB, j))
                dve.tensor_copy(ysb[:, CW:D], ps[:, 6, :]).then_inc(y1_done, 1)
                for k in range(4):
                    half, t = k // 2, k % 2
                    dve.wait_ge(sc_ready, 4 * j + k + 1)
                    cols = xres[:, t, half * CW:(half + 1) * CW]
                    dve.tensor_tensor(cols, cols, ps[:, 5 + 2 * t, :], ALU.add).then_inc(sc_done, 1)
                    if k == 0:
                        split.to(U_MOE + JOB + 4)
            split.j, split.next = jobs, U_MOE + 4
            dve.wait_ge(sc_done, jobs * 4)
            dve.sem_inc(x_half, 2)
            square_half(5, 0)
            square_half(5, 1)
            dve.wait_ge(pThi_done, 2)
            dve.tensor_tensor(pTlo[:, :, :], ps[:, 0, :].rearrange("p (k n) -> p k n", k=2),
                              pThi[:, :, :].bitcast(F32), ALU.subtract).then_inc(pTlo_done, 1)
            root(5)
            split.to(U_GATE1 + 4)
            for half in range(2):
                lo_half(7, half, vec(V_PLEG + KT))
            embed_norm(1)
            for c in range(NO):
                split.to(U_END)
                gated_add(1, c, 6)


INPUTS = ["x", "p", "mix_norm_g", "ffn_norm_g", "attn_w_qkv", "attn_w_o", "attn_g_q", "attn_g_k",
          "attn_lam_q1", "attn_lam_k1", "attn_lam_q2", "attn_lam_k2", "attn_g_sub",
          "conv_w_pw1", "conv_b_pw1", "conv_w_dw", "conv_b_dw", "conv_ln_g", "conv_ln_b",
          "conv_w_pw2", "conv_b_pw2", "ffn_w_gate", "ffn_w_up", "ffn_w_down",
          "moe_w_router", "moe_b_router", "moe_w_gate", "moe_w_up", "moe_w_down",
          "ple_w_proj", "ple_norm_g", "ple_gate_norm_g", "ple_w_gate"]


def kernel(**inputs):
    import numpy as np
    import concourse.bacc as bacc
    from concourse.bass_utils import run_bass_kernel_spmd

    nc = bacc.Bacc("TRN2", target_bir_lowering=False, num_devices=1)
    arrays, args = {}, []
    for name in INPUTS:
        a = np.ascontiguousarray(inputs[name])
        arrays[f"in_{name}"] = a
        args.append(nc.dram_tensor(f"in_{name}", a.shape, mybir.dt.from_np(a.dtype), kind="ExternalInput").ap())
    args.append(nc.dram_tensor("out", inputs["x"].shape, F32, kind="ExternalOutput").ap())
    program(nc, *args)
    result = run_bass_kernel_spmd(nc, [arrays], core_ids=[0])
    return result.results[0]["out"]
```

```python
from contextlib import ExitStack

import concourse.bass as bass
from concourse import mybir

F32 = mybir.dt.float32
F32R = mybir.dt.float32r
I32 = mybir.dt.int32
ACT = mybir.ActivationFunctionType
ALU = mybir.AluOpType
AX = mybir.AxisListType.X

P = 128
CW = 512
UNIT = 2 * CW
N_CONSTS = 12
N_LATE = 6
PE_BLOCKS = [0, 1, 2, 3]
DVE_BLOCKS = [4, 5, 6, 7]
RING = 14
SPLIT = 4


def program(nc, x, p, mix_norm_g, ffn_norm_g, attn_w_qkv, attn_w_o, attn_g_q, attn_g_k,
            attn_lam_q1, attn_lam_k1, attn_lam_q2, attn_lam_k2, attn_g_sub,
            conv_w_pw1, conv_b_pw1, conv_w_dw, conv_b_dw, conv_ln_g, conv_ln_b,
            conv_w_pw2, conv_b_pw2, ffn_w_gate, ffn_w_up, ffn_w_down,
            moe_w_router, moe_b_router, moe_w_gate, moe_w_up, moe_w_down,
            ple_w_proj, ple_norm_g, ple_gate_norm_g, ple_w_gate, out):
    _, S, D = x.shape
    T = S // P
    KT = D // P
    FF = ffn_w_gate.shape[2]
    STEPS = FF // CW
    NE = moe_w_router.shape[2]
    H = attn_w_o.shape[1] // P
    HD = P // 2
    TAPS = conv_w_dw.shape[1]
    NQKV = attn_w_qkv.shape[2] // CW
    NO = D // CW
    MAXFULL = (2 * S) // (P + 1)
    MAXJOBS = NE + 1
    NCOL = MAXJOBS + 1
    LAM0 = 0.2
    assert (T, KT, STEPS, NE, H, NQKV, NO) == (2, 8, 7, 8, 8, 6, 2) and 3 * STEPS * 2 % RING == 0
    EPS, LN_EPS = 1e-6, 1e-5
    NEG = -1e30

    U_QKV = 0
    U_WO = U_QKV + 4 * NQKV
    U_FFN = U_WO + 4 * NO
    JOB = 3 * STEPS * 4
    U_PROJ0 = U_FFN + JOB - 4
    U_GATE0 = U_FFN + JOB + 2
    U_PW1 = U_GATE0 + 4 * NO
    U_PW2 = U_PW1 + 16
    U_MOE = U_PW2 + 4 * NO
    U_PROJ1 = U_MOE
    U_GATE1 = U_PROJ1 + 2
    U_END = U_GATE1 + 4 * NO
    C_QKV, C_WO, C_GATE0, C_PW1, C_PW2, C_GATE1 = 0, 6, 8, 10, 14, 16

    wqkv, wo = attn_w_qkv[0], attn_w_o[0]
    wpw1, wpw2 = conv_w_pw1[0], conv_w_pw2[0]

    with ExitStack() as ctx:
        def sb(name, shape, dt=F32, to=ctx):
            return to.enter_context(nc.sbuf_tensor(name, shape, dt))

        def sem(name):
            return ctx.enter_context(nc.semaphore(name))

        ring = sb("weight_ring", [P, RING, 2 * UNIT])
        whi = sb("weight_hi", [P, SPLIT, UNIT], F32R)
        wlo = sb("weight_lo", [P, SPLIT, UNIT], F32R)
        xres = sb("residual", [P, T, D])
        ident = sb("identity", [P, P])
        iota = sb("iota", [P, P])
        upper = sb("strict_upper", [P, P])
        ones = sb("ones", [P, P])
        vecs = sb("column_vectors", [P, 96])
        taps = sb("conv_taps", [P, TAPS * KT])
        mask = sb("causal_mask", [P, P])
        small = sb("small", [P, 160])
        wr = sb("router_raw", [P, KT, NE])
        wr2 = sb("router_hi_lo", [P, KT, 2 * NE], F32R)
        rbias = sb("router_bias", [P, NE])
        jpos = sb("job_positions", [P, T, NCOL])
        jgate = sb("job_gates", [P, T, NCOL])
        jtab = sb("job_table", [1, 16], I32)
        def overlay(*specs):
            with ExitStack() as phase:
                return [sb(name, shape, dt, phase) for name, shape, dt in specs]

        hhi, = overlay(("h_rows_hi", [P, T, D], F32R))
        xn = sb("normed", [P, T, D])
        ahi, alo = overlay(("act_hi", [P, KT, S], F32R), ("act_lo", [P, KT, S], F32R))
        prob, amix, amixT, ident_r, mask_r = overlay(("prob", [P, 3, 2, 3 * P], F32), ("mixed_prob", [P, 2, 3 * P], F32),
                                    ("mixed_prob_T", [P, 2, 3 * P], F32),
                                    ("identity_r", [P, P], F32R), ("mask_r", [P, P], F32R))
        xehi, xelo, hlo = overlay(("job_act_hi", [P, KT, P], F32R), ("job_act_lo", [P, KT, P], F32R),
                                  ("h_rows_lo", [P, T, D], F32R))
        sb("act_region", [P, 2 * KT * S])
        v_sb, qT, kT, lamv = overlay(("values", [P, T, D], F32), ("q_T", [P, H, S], F32),
                                     ("k_T", [P, H, S], F32), ("lambda_vectors", [P, 4, HD], F32))
        sg, hid, hThi, hTlo, ysb, sel, selg, selT = overlay(
            ("silu_gate", [P, T, CW], F32), ("hidden", [P, T, CW], F32),
            ("hidden_T_hi", [P, T, CW], F32R), ("hidden_T_lo", [P, T, CW], F32R),
            ("expert_out", [P, D], F32), ("one_hot", [P, T, P], F32R),
            ("one_hot_gated", [P, T, P], F32), ("one_hot_gated_T", [P, S], F32))
        hrow, = overlay(("h_rows", [P, T, D], F32))
        cT, cy, csq = overlay(("conv_in_T", [P, KT, TAPS - 1 + S], F32), ("conv_out_T", [P, KT, S], F32),
                              ("conv_square", [P, KT, S], F32))
        emb, _, sgm, gbc, pThi, pTlo = overlay(
            ("embedding", [P, T, D], F32), ("beside_hidden_T", [P, D], F32), ("gate_sigmoid", [P, T, CW], F32),
            ("norm_row", [P, D], F32), ("p_T_hi", [P, 2, S], F32R), ("p_T_lo", [P, 2, S], F32R))
        _, pnat = overlay(("before_p_rows", [P, 5 * D], F32), ("p_rows", [P, T, 2 * P], F32))
        sb("stage_region", [P, KT * (TAPS - 1 + S) + 2 * KT * S])
        NDIAG = 8

        def diag(n):
            at = CW + n % 4 * P
            return xn[:, n % NDIAG // 4, at:at + P]

        ps = ctx.enter_context(nc.psum_tensor("psum", [P, 8, CW], F32))

        eps, lneps = small[:, 0:1], small[:, 1:2]
        ssum, std, rstd = small[:, 2:4], small[:, 4:6], small[:, 6:8]
        ssq = small[:, 142:146]
        hsq, hstd, hrstd = small[:, 8:24], small[:, 24:40], small[:, 40:56]
        neglam, lamsum, lamexp = small[:, 56:57], small[:, 57:59], small[:, 59:61]
        gsub = small[:, 61:62]
        mx, nmx = small[:, 64:68], small[:, 68:80]
        psum_e, pinv = small[:, 80:92], small[:, 92:96]
        logits = small[:, 96:112].rearrange("p (t e) -> p t e", t=T)

        V_MIX, V_FFN, V_PLEG, V_BPW1, V_BDW, V_LNG, V_LNB, V_GQ, V_GK, V_GSUB = \
            0, 16, 32, 48, 64, 72, 80, 88, 89, 90
        NV = 91
        TAPROWS = TAPS * KT // 2
        stage_v = kT[0:NV, 0, 0:P]
        stage_t = [kT[0:TAPROWS, 1, 0:P], kT[0:TAPROWS, 2, 0:P]]

        piece_in = [sem(f"piece_in{i}") for i in range(RING)]
        hi_done = sem("hi_done")
        lo_done = sem("lo_done")
        unit_used = sem("unit_used")
        consts_in = sem("consts_in")
        late_in = sem("late_in")
        x_in = sem("x_in")
        p_in = sem("p_in")
        g_in = sem("g_in")
        b_in = sem("b_in")
        masks_done = sem("masks_done")
        pool_seq = sem("pool_seq")
        vecsT_ready = sem("vecsT_ready")
        vecs_done = sem("vecs_done")
        wr_done = sem("wr_done")
        lam_part = sem("lam_part")
        first_a = sem("first_a")
        first_d = sem("first_d")
        first_std = sem("first_std")
        xn_done = sem("xn_done")
        x_half = sem("x_half")
        ssq_a = sem("ssq_a")
        ssq_d = sem("ssq_d")
        sum_done = sem("sum_done")
        std_done = sem("std_done")
        rstd_done = sem("rstd_done")
        tp_ready = sem("tp_ready")
        ahi_done = sem("ahi_done")
        alo_done = sem("alo_done")
        chunk_free = sem("chunk_free")
        qk_sq = sem("qk_sq")
        qk_ssq = sem("qk_ssq")
        qk_std = sem("qk_std")
        qk_n = sem("qk_n")
        qkT_ready = sem("qkT_ready")
        qkT_done = sem("qkT_done")
        v_done = sem("v_done")
        s_ready = sem("scores_ready")
        mask_r_done = sem("mask_r_done")
        max_done = sem("max_done")
        exp_done = sem("exp_done")
        am_done = sem("mixed_done")
        amT_ready = sem("mixedT_ready")
        amT_done = sem("mixedT_done")
        o_ready = sem("o_ready")
        o_done = sem("o_done")
        on_step = sem("o_norm_step")
        silu_done = sem("silu_done")
        h_done = sem("h_done")
        hT_ready = sem("hT_ready")
        hThi_done = sem("hThi_done")
        hTlo_done = sem("hTlo_done")
        pT_ready = sem("pT_ready")
        pThi_done = sem("pThi_done")
        pTlo_done = sem("pTlo_done")
        e_sq = sem("e_sq")
        e_std = sem("e_std")
        e_done = sem("e_done")
        sgm_done = sem("sgm_done")
        rdiag_done = sem("rdiag_done")
        rbc_ready = sem("rbc_ready")
        rbc_done = sem("rbc_done")
        glu_in = sem("glu_in")
        glu_sig = sem("glu_sig")
        glu_done = sem("glu_done")
        diag_done = sem("diag_done")
        diag_used = sem("diag_used")
        convp_done = sem("convp_done")
        conv_done = sem("conv_done")
        mean_ready = sem("mean_ready")
        mean_done = sem("mean_done")
        cent_done = sem("centred_done")
        csq_done = sem("csq_done")
        var_ready = sem("var_ready")
        cstd_done = sem("cstd_done")
        cn_done = sem("conv_normed_done")
        cs_done = sem("conv_silu_done")
        log_ready = sem("logits_ready")
        r_step = sem("router_exp")
        rm_done = sem("route_mask_done")
        cnt_ready = sem("counts_ready")
        tab_done = sem("job_table_done")
        hf_done = sem("h_rows_done")
        hhi_done = sem("h_rows_hi_done")
        hlo_done = sem("h_rows_lo_done")
        sel_done = sem("one_hot_done")
        xe_ready = sem("gather_ready")
        xehi_done = sem("gather_hi_done")
        xelo_done = sem("gather_lo_done")
        selT_ready = sem("one_hot_T_ready")
        selT_done = sem("one_hot_T_done")
        y_done = sem("y_done")
        sc_ready = sem("scatter_ready")
        sc_done = sem("scatter_added")
        dve_seq = sem("dve_seq")
        act_seq = sem("act_seq")
        out_ready = sem("out_ready")
        stored = sem("stored")

        def after(n, per, j):
            return n if j is None else j * per + n

        def job_counts(eng):
            return (eng.snap(eng.value_load(jtab[0:1, NCOL:NCOL + 1], min_val=NE - MAXFULL, max_val=NE + 1)),
                    eng.snap(eng.value_load(jtab[0:1, NCOL + 1:NCOL + 2], min_val=NE, max_val=MAXJOBS)))

        class Splitter:

            def __init__(self, one):
                self.next, self.one, self.j = 0, one, None

            def to(self, n):
                while self.next < n:
                    self.one(self.next, self.j)
                    self.next += 1

        class Order:

            def __init__(self, eng, s):
                self.eng, self.s, self.n = eng, s, 0

            def add(self, ins):
                ins.then_inc(self.s, 1)
                self.n += 1
                return self.n

            def wait(self, n):
                self.eng.wait_ge(self.s, n)

            def step(self, ins):
                self.wait(self.add(ins))

        def raw(u):
            return ring[:, (u // 2) % RING, (u % 2) * UNIT:(u % 2 + 1) * UNIT]

        block = ctx.enter_context(nc.Block())

        @block.sync
        def _(sp):
            def load(piece, src, j, kt=4):
                slot = piece % RING
                if piece >= RING:
                    sp.wait_ge(lo_done, after(2 * (piece - RING) + 2, JOB, j))
                dst = ring[:, slot, :].rearrange("p (t n) -> p t n", t=kt)
                sp.dma_start(dst, src).then_inc(piece_in[slot], 16)

            def columns(first, w, chunk, j=None):
                for k in range(2):
                    load(first + k, w[k * 4 * P:(k + 1) * 4 * P, chunk * CW:(chunk + 1) * CW]
                         .rearrange("(t p) n -> p t n", p=P), j)

            def feed_forward(first, wg, wu, wd, j=None, proj=None):
                def rows(at, s):
                    for half in range(2):
                        load(at + half, wd[s * CW:(s + 1) * CW, half * CW:(half + 1) * CW]
                             .rearrange("(t p) n -> p t n", p=P), j)
                at = first
                for s in range(STEPS):
                    columns(at, wg, s, j)
                    at += 2
                    if s:
                        rows(at, s - 1)
                        at += 2
                    columns(at, wu, s, j)
                    at += 2
                if proj is not None:
                    load(at, proj.rearrange("(t p) n -> p t n", p=P), None, 2)
                    at += 1
                rows(at, STEPS - 1)

            for t in range(T):
                sp.dma_start(xres[:, t, :], x[0, t * P:(t + 1) * P, :]).then_inc(x_in, 16)
            tap_rows = conv_w_dw[0].rearrange("k (c n) -> (k c) n", n=P)
            for i in range(2):
                sp.dma_start(stage_t[i], tap_rows[i * TAPROWS:(i + 1) * TAPROWS, :]).then_inc(consts_in, 16)
            sp.wait_ge(consts_in, 16 * N_CONSTS)
            for c in range(NQKV):
                columns((U_QKV + 4 * c) // 2, wqkv, c)
            for c in range(NO):
                columns((U_WO + 4 * c) // 2, wo, c)
            feed_forward(U_FFN // 2, ffn_w_gate[0], ffn_w_up[0], ffn_w_down[0],
                         proj=ple_w_proj[0])
            for c in range(NO):
                columns((U_GATE0 + 4 * c) // 2, ple_w_gate[0], c)
            for i, c in enumerate((0, 2, 1, 3)):
                columns((U_PW1 + 4 * i) // 2, wpw1, c)
            for c in range(NO):
                columns((U_PW2 + 4 * c) // 2, wpw2, c)
            feed_forward(U_MOE // 2, moe_w_gate[0, 0], moe_w_up[0, 0], moe_w_down[0, 0])
            sp.wait_ge(tab_done, 1)
            _, jobs = job_counts(sp)
            with sp.Fori(1, jobs) as j:
                e = sp.snap(sp.value_load(jtab[0:1, bass.ds(j, 1)], min_val=0, max_val=NE - 1))
                feed_forward(U_MOE // 2, *(w[0, bass.ds(e, 1), :, :].rearrange("a k n -> (a k) n")
                                           for w in (moe_w_gate, moe_w_up, moe_w_down)), j)
            load(U_PROJ1 // 2, ple_w_proj[1].rearrange("(t p) n -> p t n", p=P), jobs, 2)
            for c in range(NO):
                columns((U_GATE1 + 4 * c) // 2, ple_w_gate[1], c, jobs)
            for c in range(NO):
                for t in range(T):
                    sp.wait_ge(out_ready, T * c + t + 1)
                    sp.dma_start(out[0, t * P:(t + 1) * P, c * CW:(c + 1) * CW],
                                 xres[:, t, c * CW:(c + 1) * CW]).then_inc(stored, 16)
            sp.wait_ge(stored, 16 * NO * T)

        @block.gpsimd
        def _(pool):
            pool.memset(ident[:, :], 0.0).then_inc(pool_seq, 1)
            pool.memset(mask[:, :], 0.0).then_inc(pool_seq, 1)
            pool.memset(ones[:, :], 1.0).then_inc(pool_seq, 1)
            pool.wait_ge(pool_seq, 3)
            pool.affine_select(out=ident[:, :], in_=ident[:, :], compare_op=ALU.not_equal, fill=1.0,
                               base=0, pattern=[[-1, P]], channel_multiplier=1).then_inc(masks_done, 1)
            pool.affine_select(out=mask[:, :], in_=mask[:, :], compare_op=ALU.is_ge, fill=NEG,
                               base=0, pattern=[[-1, P]], channel_multiplier=1).then_inc(masks_done, 1)
            pool.affine_select(out=upper[:, :], in_=ones[:, :], compare_op=ALU.is_gt, fill=0.0,
                               base=0, pattern=[[1, P]], channel_multiplier=-1).then_inc(masks_done, 1)
            pool.iota(iota[:, :], pattern=[[1, P]], base=0, channel_multiplier=0,
                      allow_small_or_imprecise_dtypes=True).then_inc(masks_done, 1)
            for i, src in enumerate((attn_lam_q1, attn_lam_k1, attn_lam_q2, attn_lam_k2)):
                pool.dma_start(lamv[:, i, :], src.broadcast_to([P, HD])).then_inc(late_in, 16)
            pool.dma_start(wr[:, :, :], moe_w_router[0].rearrange("(t p) e -> p t e", p=P)).then_inc(late_in, 16)
            pool.dma_start(rbias[:, :], moe_b_router.broadcast_to([P, NE])).then_inc(late_in, 16)

            def embedding_inputs(i):
                pool.dma_start(pnat[:, :, :], p[i, 0].rearrange("(t p) d -> p t d", p=P)).then_inc(p_in, 16)
                pool.dma_start(gbc[:, :], ple_norm_g[i:i + 1, :].broadcast_to([P, D])).then_inc(p_in, 16)

            pool.wait_ge(x_half, 1)
            embedding_inputs(0)
            pool.wait_ge(cn_done, 1)
            pool.dma_start(cT[:, 0:4, 0:2 * P], conv_b_pw2[0:1, :].rearrange("a (c n) -> a c n", c=4)
                           .broadcast_to([P, 4, 2 * P])).then_inc(b_in, 16)
            pool.wait_ge(alo_done, 24)
            pool.dma_start(ysb[:, :], ffn_norm_g[1:2, :].broadcast_to([P, D])).then_inc(g_in, 16)
            pool.wait_ge(hf_done, 2 * T)
            embedding_inputs(1)

        @block.tensor
        def _(pe):
            def wait_unit(u, j):
                pe.wait_ge(lo_done, after(u + 1, JOB, j))

            def three(dst, ahi_, alo_, bhi_, blo_, first, last, **kw):
                pe.matmul(dst, ahi_, bhi_, start=first, stop=False, **kw)
                pe.matmul(dst, ahi_, blo_, start=False, stop=False, **kw)
                return pe.matmul(dst, alo_, bhi_, start=False, stop=last, **kw)

            def linear_unit(u, i, banks, tiles, j=None, ah=ahi, al=alo):
                wait_unit(u, j)
                s = u % SPLIT
                for k in range(2):
                    kt = 2 * i + k
                    cols = slice(k * CW, (k + 1) * CW)
                    for t in range(tiles):
                        rows = slice(t * P, (t + 1) * P)
                        last = three(ps[:, banks + t, :], ah[:, kt, rows], al[:, kt, rows],
                                     whi[:, s, cols], wlo[:, s, cols], kt == 0, kt == KT - 1)
                last.then_inc(unit_used, 1)

            def transpose_half(src, half, banks=4):
                for b in range(2):
                    bank = banks + 2 * half + b
                    for k in range(2):
                        for t in range(T):
                            kt = 4 * half + 2 * b + k
                            at = k * S + t * P
                            last = pe.transpose(ps[:, bank, at:at + P], src[:, t, kt * P:(kt + 1) * P],
                                                ident[:, :])
                    last.then_inc(tp_ready, 1)

            def x_transpose(update, half):
                pe.wait_ge(x_half, 2 * (update - 1) + half + 1)
                transpose_half(xres, half)

            def linear(u0, c0, chunks, stage, update=None):
                for c in range(chunks):
                    if c0 + c >= 2:
                        pe.wait_ge(chunk_free, c0 + c - 1)
                    for i in range(4):
                        if c == 0:
                            pe.wait_ge(alo_done, 4 * stage + i + 1)
                        linear_unit(u0 + 4 * c + i, i, 2 * ((c0 + c) % 2), T)
                        if update is not None and c == 1 and i == 1:
                            x_transpose(update, 0)

            def hidden_transpose(n, tiles, j):
                pe.wait_ge(h_done, after(n, STEPS, j))
                for t in range(tiles):
                    for k in range(4):
                        last = pe.transpose(ps[:, 2 // (3 - tiles) + t, k * P:(k + 1) * P],
                                            hid[:, t, k * P:(k + 1) * P], ident[:, :])
                last.then_inc(hT_ready, 1)

            def down(u, n, s, tiles, j, side=lambda place: None):
                pe.wait_ge(hTlo_done, after(n, STEPS, j))
                for i in range(4):
                    half = i // 2
                    wait_unit(u + i, j)
                    for k in range(2):
                        kt = 2 * (i % 2) + k
                        cols = slice(k * CW, (k + 1) * CW)
                        for t in range(tiles):
                            last = three(ps[:, 4 + 2 * half + t, :], hThi[:, t, kt * P:(kt + 1) * P],
                                         hTlo[:, t, kt * P:(kt + 1) * P], whi[:, (u + i) % SPLIT, cols],
                                         wlo[:, (u + i) % SPLIT, cols], s == 0 and kt == 0,
                                         s == STEPS - 1 and kt == 3)
                    last.then_inc(unit_used, 1)
                    if s == STEPS - 1:
                        side(STEPS + 2 + i)

            def feed_forward(u0, n0, tiles, j, side, ah=ahi, al=alo, gap=0):
                u, up = u0, 2 // (3 - tiles)
                for s in range(STEPS):
                    n = n0 + s
                    if n:
                        pe.wait_ge(silu_done, after(n, STEPS, j))
                    for i in range(4):
                        if j is None and s == 0:
                            pe.wait_ge(alo_done, 8 + i + 1)
                        linear_unit(u + i, i, 0, tiles, j, ah, al)
                        if i == 1 and s:
                            hidden_transpose(n, tiles, j)
                        if i == 1 and not s:
                            side(-1)
                    u += 4
                    if s:
                        down(u, n, s - 1, tiles, j)
                        u += 4
                    side(s)
                    if s == 0 and n:
                        pe.wait_ge(hTlo_done, after(n, STEPS, j))
                    for i in range(4):
                        linear_unit(u + i, i, up, tiles, j, ah, al)
                    u += 4
                side(STEPS)
                hidden_transpose(n0 + STEPS, tiles, j)
                side(STEPS + 1)
                down(u + gap, n0 + STEPS, STEPS - 1, tiles, j, side)

            pe.wait_ge(consts_in, 16 * N_CONSTS)
            pe.wait_ge(masks_done, 4)
            pe.transpose(ps[:, 0, 0:NV], stage_v, ident[0:NV, 0:NV])
            pe.transpose(ps[:, 0, P:P + TAPROWS], stage_t[0], ident[0:TAPROWS, 0:TAPROWS])
            pe.transpose(ps[:, 0, 2 * P:2 * P + TAPROWS], stage_t[1],
                         ident[0:TAPROWS, 0:TAPROWS]).then_inc(vecsT_ready, 1)

            pe.wait_ge(vecs_done, 1)
            pe.wait_ge(xn_done, 2)
            for half in range(2):
                transpose_half(xn, half)
            for c in range(NQKV):
                if c >= 2:
                    pe.wait_ge(chunk_free, c - 1)
                for i in range(4):
                    if c == 0:
                        pe.wait_ge(alo_done, i + 1)
                    linear_unit(U_QKV + 4 * c + i, i, 2 * (c % 2), T)
                    if i == 1 and 1 <= c <= 4:
                        pe.wait_ge(qk_n, c)
                        if c >= 2:
                            pe.wait_ge(qkT_done, c - 1)
                        for t in range(T):
                            for h in range(4):
                                last = pe.transpose(ps[:, 4 + t, h * P:(h + 1) * P],
                                                    xn[:, t, h * P:(h + 1) * P], ident[:, :])
                        last.then_inc(qkT_ready, 1)

            def scores(h):
                if h >= 2:
                    pe.wait_ge(exp_done, h - 1)
                for c in range(2):
                    rows = slice(c * HD, (c + 1) * HD)
                    b = 2 * (h % 2) + c
                    if h + c == 0:
                        pe.wait_ge(mask_r_done, 1)
                    pe.matmul(ps[:, b, 0:P], qT[rows, h, 0:P], kT[rows, h, 0:P], start=True, stop=False)
                    pe.matmul(ps[:, b, 0:P], ident_r[:, :], mask_r[:, :], start=False, stop=True)
                    pe.matmul(ps[:, b, P:3 * P], qT[rows, h, P:S], kT[rows, h, 0:S], start=True, stop=False)
                    last = pe.matmul(ps[:, b, 2 * P:3 * P], ident_r[:, :], mask_r[:, :],
                                     start=False, stop=True)
                last.then_inc(s_ready, 1)

            def head_out(h):
                pe.wait_ge(amT_done, h + 1)
                if h >= 2:
                    pe.wait_ge(o_done, h - 1)
                b, e = 6 + h % 2, slice(h * P, (h + 1) * P)
                pe.matmul(ps[:, b, 0:P], amixT[:, h % 2, 0:P], v_sb[:, 0, e], start=True, stop=True)
                pe.matmul(ps[:, b, P:S], amixT[:, h % 2, P:2 * P], v_sb[:, 0, e], start=True, stop=False)
                pe.matmul(ps[:, b, P:S], amixT[:, h % 2, 2 * P:3 * P], v_sb[:, 1, e],
                          start=False, stop=True).then_inc(o_ready, 1)

            pe.wait_ge(qkT_done, 4)
            pe.wait_ge(v_done, 2)
            scores(0)
            scores(1)
            for h in range(H):
                if h + 2 < H:
                    scores(h + 2)
                pe.wait_ge(am_done, h + 1)
                if h >= 2:
                    pe.wait_ge(amT_done, h - 1)
                for k in range(3):
                    last = pe.transpose(ps[:, 4 + h % 2, k * P:(k + 1) * P],
                                        amix[:, h % 2, k * P:(k + 1) * P], ident[:, :])
                last.then_inc(amT_ready, 1)
                if h:
                    head_out(h - 1)
            head_out(H - 1)
            for half in range(2):
                pe.wait_ge(on_step, 2 + half)
                transpose_half(xn, half)
            linear(U_WO, C_WO, NO, 1, update=1)

            def p_transpose(i, bank):
                pe.wait_ge(p_in, 32 * (i + 1))
                for k in range(2):
                    for t in range(T):
                        last = pe.transpose(ps[:, bank, k * S + t * P:k * S + (t + 1) * P],
                                            pnat[:, t, k * P:(k + 1) * P], ident[:, :])
                last.then_inc(pT_ready, 1)

            def p_project(u, j, i):
                pe.wait_ge(pTlo_done, i + 1)
                for k in range(2):
                    wait_unit(u + k, j)
                    s = (u + k) % SPLIT
                    for t in range(T):
                        if j is None and k == 0 and t == 1:
                            pe.wait_ge(hTlo_done, STEPS)
                        for half in range(2):
                            rows, cols = slice(t * P, (t + 1) * P), slice(half * CW, (half + 1) * CW)
                            last = three(ps[:, 2 * t + half, :], pThi[:, k, rows], pTlo[:, k, rows],
                                         whi[:, s, cols], wlo[:, s, cols], k == 0, k == 1)
                    last.then_inc(unit_used, 1)

            def dense_side(place):
                if place == -1:
                    x_transpose(1, 1)
                    pe.wait_ge(alo_done, 8 + 2)
                    p_transpose(0, 4)
                if place == STEPS + 1:
                    pe.wait_ge(silu_done, STEPS)
                    p_project(U_PROJ0, None, 0)
                if place == STEPS + 4:
                    x_transpose(2, 0)

            feed_forward(U_FFN, 0, T, None, dense_side, gap=2)

            def gate(u_gate, stage, j, late):
                for c in range(NO):
                    for n in range(4):
                        if c == 0:
                            pe.wait_ge(alo_done, 4 * stage + max(n, 1) + 1)
                        linear_unit(u_gate + 4 * c + n, n, 4 + 2 * c, T, j)
                        if n == 1:
                            late(c)

            gate(U_GATE0, 3, None, lambda c: x_transpose(2 + c, 1 - c))

            pe.wait_ge(e_done, 1)
            for c in range(4):
                pe.wait_ge(chunk_free, C_PW1 + c - 1)
                for i in range(4):
                    u = U_PW1 + 4 * c + i
                    if c == 0:
                        pe.wait_ge(alo_done, 16 + i + 1)
                    wait_unit(u, None)
                    for k in range(2):
                        kt = 2 * i + k
                        for b in range(4):
                            cols = slice(k * CW + b * P, k * CW + (b + 1) * P)
                            bank, at = 2 * (c % 2) + b // 2, (b % 2) * S
                            last = three(ps[:, bank, at:at + S], whi[:, u % SPLIT, cols],
                                         wlo[:, u % SPLIT, cols], ahi[:, kt, :], alo[:, kt, :],
                                         kt == 0 and b % 2 == 0, kt == KT - 1, skip_group_check=True)
                    last.then_inc(unit_used, 1)
                    if c == 0 and i == 1:
                        x_transpose(3, 1)
                if c == 0:
                    pe.wait_ge(rdiag_done, 1)
                    for t in range(T):
                        last = pe.matmul(ps[:, 4, t * P:(t + 1) * P], ones[:, :],
                                         xn[:, 0, S + t * P:S + (t + 1) * P], start=True, stop=True)
                    last.then_inc(rbc_ready, 1)
            n = 0
            pe.wait_ge(glu_done, 1)
            for ch in PE_BLOCKS:
                for k in range(TAPS):
                    pe.wait_ge(diag_done, n + 1)
                    pe.matmul(ps[:, 4 + ch, 0:S], diag(n), cT[:, ch, k:k + S],
                              start=k == 0, stop=k == TAPS - 1).then_inc(diag_used, 1)
                    n += 1
            pe.wait_ge(glu_done, 2)
            for n, ch in enumerate(PE_BLOCKS + DVE_BLOCKS):
                if ch in PE_BLOCKS:
                    pe.wait_ge(convp_done, PE_BLOCKS.index(ch) + 1)
                else:
                    pe.wait_ge(conv_done, DVE_BLOCKS.index(ch) + 1)
                last = pe.matmul(ps[:, 0, 0:S], ones[:, :], cy[:, ch, :], start=n == 0, stop=n == KT - 1)
            last.then_inc(mean_ready, 1)
            for b in range(KT):
                pe.wait_ge(csq_done, b // 4 + 1)
                last = pe.matmul(ps[:, 3, 0:S], ones[:, :], csq[:, b, :], start=b == 0, stop=b == KT - 1)
            last.then_inc(var_ready, 1)
            linear(U_PW2, C_PW2, NO, 5, update=4)
            x_transpose(4, 1)

            for t in range(T):
                rows = slice(t * P, (t + 1) * P)
                for kt in range(KT):
                    pe.wait_ge(alo_done, 24 + kt // 2 + 1)
                    for a in (ahi, alo):
                        last = pe.matmul(ps[:, 0, 2 * t * NE:2 * (t + 1) * NE], a[:, kt, rows], wr2[:, kt, :],
                                         start=kt == 0 and a is ahi, stop=kt == KT - 1 and a is alo)
            last.then_inc(log_ready, 1)
            pe.wait_ge(rm_done, 1)
            m = small[:, 112:128].rearrange("p (t e) -> p t e", t=T)
            pe.matmul(ps[:, 1, 0:NE], upper[:, :], m[:, 0, :], start=True, stop=True)
            pe.matmul(ps[:, 1, NE:2 * NE], ones[:, :], m[:, 0, :], start=True, stop=False)
            pe.matmul(ps[:, 1, NE:2 * NE], upper[:, :], m[:, 1, :], start=False, stop=True)
            pe.matmul(ps[:, 1, 2 * NE:3 * NE], ones[:, :], m[:, 0, :], start=True, stop=False)
            pe.matmul(ps[:, 1, 2 * NE:3 * NE], ones[:, :], m[:, 1, :], start=False,
                      stop=True).then_inc(cnt_ready, 1)

            def gather(bank):
                for k in range(4):
                    kt = 4 * (bank - 2) + k
                    cols = slice(kt * P, (kt + 1) * P)
                    for t in range(T):
                        pe.matmul(ps[:, bank, k * P:(k + 1) * P], hhi[:, t, cols], sel[:, t, :],
                                  start=t == 0, stop=False)
                        last = pe.matmul(ps[:, bank, k * P:(k + 1) * P], hlo[:, t, cols], sel[:, t, :],
                                         start=False, stop=t == T - 1)
                last.then_inc(xe_ready, 1)

            pe.wait_ge(hlo_done, T)
            pe.wait_ge(sel_done, 1)
            gather(2)
            gather(3)
            pe.wait_ge(tab_done, 1)
            small_jobs, jobs = job_counts(pe)
            with pe.Fori(0, small_jobs) as j:
                def side(place):
                    if place == 2:
                        for t in range(T):
                            last = pe.transpose(ps[:, 3, t * P:(t + 1) * P], selg[:, t, :], ident[:, :])
                        last.then_inc(selT_ready, 1)
                    if place == STEPS:
                        pe.wait_ge(selT_done, j + 1)
                        pe.wait_ge(sel_done, j + 2)
                        gather(2)
                    if place == STEPS + 1:
                        gather(3)
                    if place == STEPS + 4:
                        scatter(0)

                def scatter(half):
                    pe.wait_ge(y_done, 2 * j + (half + 1))
                    for t in range(T):
                        if half:
                            pe.wait_ge(sc_done, 4 * j + (t + 1))
                        pe.matmul(ps[:, 5 + 2 * t, :], selT[:, t * P:(t + 1) * P],
                                  ysb[:, half * CW:(half + 1) * CW], start=True, stop=True).then_inc(sc_ready, 1)

                pe.wait_ge(xelo_done, 2 * j + 2)
                feed_forward(U_MOE, STEPS, 1, j, side, xehi, xelo)
                scatter(1)
            pe.wait_ge(hf_done, 2 * T)
            pe.wait_ge(xelo_done, 2 * small_jobs + 2)
            for half in range(2):
                transpose_half(xn, half, 0)
            pe.wait_ge(alo_done, 4 * 7 + 4)
            with pe.If(small_jobs < jobs):
                with pe.Fori(small_jobs, jobs) as j:
                    def full_side(place):
                        if place == 0:
                            pe.wait_ge(sc_done, 4 * j)
                    feed_forward(U_MOE, STEPS, T, j, full_side)
            p_transpose(1, 0)
            x_transpose(5, 0)
            x_transpose(5, 1)
            p_project(U_PROJ1, jobs, 1)
            gate(U_GATE1, 8, jobs, lambda c: None)

        @block.scalar
        def _(act):
            def split_hi(u, j):
                act.wait_ge(piece_in[(u // 2) % RING],
                            after(16 * (u // 2 // RING + 1), 16 * (JOB // 2 // RING), j))
                if u >= SPLIT:
                    act.wait_ge(unit_used, after(u - SPLIT + 1, JOB, j))
                act.activation(whi[:, u % SPLIT, :], raw(u), ACT.Copy).then_inc(hi_done, 1)

            split = Splitter(split_hi)
            own = Order(act, act_seq)

            rows = [(V_MIX, mix_norm_g, 16), (V_FFN, ffn_norm_g, 16), (V_PLEG, ple_gate_norm_g, 16),
                    (V_BPW1, conv_b_pw1, 16), (V_BDW, conv_b_dw, 8), (V_LNG, conv_ln_g, 8),
                    (V_LNB, conv_ln_b, 8)]
            for at, src, n in rows:
                act.dma_start(kT[at:at + n, 0, 0:P], src.rearrange("l (c n) -> (l c) n", n=P)
                              ).then_inc(consts_in, 16)
            for at, src in ((V_GQ, attn_g_q), (V_GK, attn_g_k)):
                act.dma_start(kT[at:at + 1, 0, 0:P], src.rearrange("l c n -> l (c n)")).then_inc(consts_in, 16)
            act.dma_start(kT[V_GSUB:V_GSUB + 1, 0, 0:P], attn_g_sub).then_inc(consts_in, 16)

            def square_half(r, half):
                act.wait_ge(x_half, 2 * (r - 1) + half + 1)
                cols = slice(half * CW, (half + 1) * CW)
                act.activation(xn[:, 0, cols], xres[:, 0, cols], ACT.Square,
                               accum_out=ssq[:, 2 * half:2 * half + 1]).then_inc(ssq_a, 1)

            def root(r):
                act.wait_ge(sum_done, r)
                act.activation(std, ssum, ACT.Sqrt, bias=eps, scale=1.0 / D).then_inc(std_done, 1)

            def hi_half(tp, half, gain, banks=4):
                for b in range(2):
                    act.wait_ge(tp_ready, tp + 2 * half + b + 1)
                    for k in range(2):
                        kt = 4 * half + 2 * b + k
                        ins = act.activation(ahi[:, kt, :], ps[:, banks + 2 * half + b, k * S:(k + 1) * S],
                                             ACT.Copy, scale=gain(kt))
                    ins.then_inc(ahi_done, 1)

            def vec(at):
                return lambda kt: vecs[:, at + kt:at + kt + 1]


            act.wait_ge(x_in, 16 * T)
            act.activation(xn[:, 0, :], xres[:, 0, :], ACT.Square, accum_out=ssum[:, 0:1]).then_inc(first_a, 1)
            act.wait_ge(first_a, 1)
            act.wait_ge(first_d, 1)
            act.activation(std, ssum, ACT.Sqrt, bias=eps, scale=1.0 / D).then_inc(first_std, 1)
            act.wait_ge(vecs_done, 1)
            for half in range(2):
                hi_half(0, half, vec(V_MIX))

            def qk_transposed(c):
                act.wait_ge(qkT_ready, c + 1)
                dst, gain = (qT, V_GQ) if c < 2 else (kT, V_GK)
                for t in range(T):
                    ins = act.activation(dst[:, 4 * (c % 2):4 * (c % 2) + 4, t * P:(t + 1) * P],
                                         ps[:, 4 + t, :].rearrange("p (h n) -> p h n", h=4), ACT.Copy,
                                         scale=vecs[:, gain:gain + 1])
                ins.then_inc(qkT_done, 1)

            for c in range(NQKV):
                q = U_QKV + 4 * c + 3
                pair = ps[:, 2 * (c % 2):2 * (c % 2) + 2, :]
                if c < 4:
                    split.to(q + 4)
                    act.wait_ge(unit_used, q + 1)
                    if c:
                        act.wait_ge(qk_ssq, c)
                    act.activation(xn[:, :, CW:D], pair, ACT.Square).then_inc(qk_sq, 1)
                    act.wait_ge(qk_ssq, c + 1)
                    act.activation(hstd, hsq, ACT.Sqrt, bias=eps, scale=1.0 / HD).then_inc(qk_std, 1)
                    split.to(q + 6)
                    qk_transposed(c)
                else:
                    split.to(q + 4)
                    act.wait_ge(unit_used, q + 1)
                    act.activation(v_sb[:, :, (c - 4) * CW:(c - 3) * CW], pair, ACT.Copy).then_inc(v_done, 1)

            act.activation(ident_r[:, :], ident[:, :], ACT.Copy)
            act.activation(mask_r[:, :], mask[:, :], ACT.Copy).then_inc(mask_r_done, 1)
            act.wait_ge(late_in, 16 * N_LATE)
            act.activation(wr2[:, :, 0:NE], wr[:, :, :], ACT.Copy).then_inc(wr_done, 1)
            act.wait_ge(lam_part, 1)
            act.activation(lamexp, lamsum, ACT.Exp).then_inc(lam_part, 1)

            def exps(h):
                act.wait_ge(max_done, h + 1)
                if h >= 3:
                    act.wait_ge(am_done, h - 2)
                for t in range(T):
                    for c in range(2):
                        i = 4 * (h % 3) + 2 * t + c
                        keys = slice(0, P) if t == 0 else slice(P, 3 * P)
                        ins = act.activation(prob[:, h % 3, c, keys], ps[:, 2 * (h % 2) + c, keys], ACT.Exp,
                                             scale=HD ** -0.5, bias=nmx[:, i:i + 1],
                                             accum_out=psum_e[:, i:i + 1])
                ins.then_inc(exp_done, 1)

            def head_out(h):
                act.wait_ge(o_ready, h + 1)
                for t in range(T):
                    n = own.add(act.activation(xn[:, t, h * P:(h + 1) * P], ps[:, 6 + h % 2, t * P:(t + 1) * P],
                                               ACT.Square, accum_out=hsq[:, t * H + h:t * H + h + 1]))
                own.wait(n)
                act.activation(xn[:, :, h * P:(h + 1) * P],
                               ps[:, 6 + h % 2, 0:S].rearrange("p (t n) -> p t n", t=T),
                               ACT.Copy).then_inc(o_done, 1)

            split.to(U_WO + 4)
            exps(0)
            for h in range(H):
                if h + 1 < H:
                    exps(h + 1)
                act.wait_ge(amT_ready, h + 1)
                if h >= 2:
                    act.wait_ge(o_ready, h - 1)
                act.activation(amixT[:, h % 2, :], ps[:, 4 + h % 2, 0:3 * P], ACT.Copy).then_inc(amT_done, 1)
                if h:
                    head_out(h - 1)
            head_out(H - 1)
            act.activation(hstd, hsq, ACT.Sqrt, bias=eps, scale=1.0 / P).then_inc(on_step, 1)
            for half in range(2):
                hi_half(4, half, lambda kt: gsub)

            def feed_forward(u0, n0, tiles, j, side):
                u, up = u0, 2 // (3 - tiles)

                def hidden_hi(n):
                    act.wait_ge(hT_ready, after(n, STEPS, j))
                    act.activation(hThi[:, 0:tiles, :], ps[:, up:up + tiles, :], ACT.Copy).then_inc(hThi_done, 1)

                for s in range(STEPS):
                    n = n0 + s
                    if s:
                        split.to(u + 5)
                        hidden_hi(n)
                    split.to(u + 7)
                    act.wait_ge(unit_used, after(u + 4, JOB, j))
                    if n:
                        act.wait_ge(h_done, after(n, STEPS, j))
                    if j is not None:
                        ins = act.activation(sg[:, 0:tiles, :], ps[:, 0:tiles, :], ACT.Silu)
                    else:
                        for t in range(tiles):
                            ins = act.activation(sg[:, t, :], ps[:, t, :], ACT.Silu, scale=rstd[:, t:t + 1])
                    ins.then_inc(silu_done, 1)
                    side(s, u + 4)
                    u += 12 if s else 8
                side(STEPS, u)
                split.to(u + 4)
                hidden_hi(n0 + STEPS)
                return u

            q = U_WO + 7
            split.to(q + 2)
            square_half(1, 0)
            hi_half(8, 0, vec(V_FFN))
            split.to(q + 4)
            square_half(1, 1)
            split.to(q + 6)
            hi_half(8, 1, vec(V_FFN))
            act.wait_ge(pT_ready, 1)
            act.activation(pThi[:, :, :], ps[:, 4, :].rearrange("p (k n) -> p k n", k=2),
                           ACT.Copy).then_inc(pThi_done, 1)
            root(1)
            act.wait_ge(rstd_done, 1)
            feed_forward(U_FFN, 0, T, None, lambda place, u: None)

            def embed_root(i, u_proj, j):
                act.wait_ge(unit_used, after(u_proj + 2, JOB, j))
                for t in range(T):
                    ins = act.activation(emb[:, t, :], ps[:, 2 * t:2 * t + 2, :].rearrange("p b n -> p (b n)"),
                                         ACT.Square, accum_out=hsq[:, t:t + 1])
                own.step(ins)
                act.activation(hstd[:, 0:2], hsq[:, 0:2], ACT.Sqrt, bias=eps, scale=1.0 / D).then_inc(e_std, 1)

            def gate_sigmoid(i, c, q, j):
                act.wait_ge(unit_used, after(q + 1, JOB, j))
                if c:
                    act.wait_ge(chunk_free, (C_GATE1 if i else C_GATE0) + 1)
                for t in range(T):
                    act.activation(sgm[:, t, :], ps[:, 4 + 2 * c + t, :], ACT.Sigmoid,
                                   scale=rstd[:, t:t + 1]).then_inc(sgm_done, 1)

            split.to(U_PROJ0 + 5)
            embed_root(0, U_PROJ0, None)
            q = U_GATE0 - 1
            split.to(q + 3)
            square_half(2, 0)
            hi_half(12, 0, vec(V_PLEG))
            split.to(q + 4)
            square_half(2, 1)
            split.to(q + 6)
            hi_half(12, 1, vec(V_PLEG))
            root(2)
            act.wait_ge(rstd_done, 2)
            q = U_GATE0 + 3
            split.to(q + 4)
            gate_sigmoid(0, 0, q, None)
            split.to(q + 6)
            square_half(3, 0)
            hi_half(16, 0, vec(V_MIX + KT))
            q += 4
            split.to(q + 4)
            gate_sigmoid(0, 1, q, None)

            split.to(q + 5)
            square_half(3, 1)
            split.to(q + 6)
            hi_half(16, 1, vec(V_MIX + KT))
            root(3)
            split.to(q + 8)
            act.wait_ge(rbc_ready, 1)
            act.activation(xn[:, 1, S:2 * S], ps[:, 4, 0:S], ACT.Copy).then_inc(rbc_done, 1)

            def sigmoids(cc):
                act.wait_ge(glu_in, cc + 1)
                for b in range(4):
                    ch = 4 * cc + b
                    ins = act.activation(csq[:, b, :], csq[:, b, :], ACT.Sigmoid,
                                         bias=vecs[:, V_BPW1 + KT + ch:V_BPW1 + KT + ch + 1])
                ins.then_inc(glu_sig, 1)

            def diagonals(first, n):
                for m in range(first, n):
                    i, k = m // TAPS, m % TAPS
                    if m >= NDIAG:
                        act.wait_ge(diag_used, m - NDIAG + 1)
                    at = k * KT + PE_BLOCKS[i]
                    act.activation(diag(m), ident[:, :], ACT.Copy, scale=taps[:, at:at + 1]).then_inc(diag_done, 1)
                    if i and k == 4:
                        conv_out(i - 1)

            def conv_out(i):
                ch = PE_BLOCKS[i]
                act.wait_ge(diag_used, TAPS * (i + 1))
                act.activation(cy[:, ch, :], ps[:, 4 + ch, 0:S], ACT.Identity,
                               bias=vecs[:, V_BDW + ch:V_BDW + ch + 1]).then_inc(convp_done, 1)

            split.to(U_PW1 + 7 + 4)
            sigmoids(0)
            diagonals(0, NDIAG)
            split.to(U_PW1 + 15 + 4)
            diagonals(NDIAG, NDIAG + 4)
            sigmoids(1)
            split.to(U_PW2 + 4)
            diagonals(NDIAG + 4, TAPS * len(PE_BLOCKS))
            conv_out(len(PE_BLOCKS) - 1)
            act.wait_ge(mean_ready, 1)
            act.activation(xn[:, 0, 0:S], ps[:, 0, 0:S], ACT.Copy, scale=1.0 / D).then_inc(mean_done, 1)
            for b in range(2):
                act.wait_ge(cent_done, b + 1)
                act.activation(csq[:, 4 * b:4 * b + 4, :], cy[:, 4 * b:4 * b + 4, :],
                               ACT.Square).then_inc(csq_done, 1)
            act.wait_ge(var_ready, 1)
            act.activation(xn[:, 0, CW:CW + S], ps[:, 3, 0:S], ACT.Sqrt, bias=lneps,
                           scale=1.0 / D).then_inc(cstd_done, 1)
            for b in range(KT):
                act.wait_ge(cn_done, b // 2 + 1)
                act.activation(csq[:, b, :], cy[:, b, :], ACT.Silu, bias=vecs[:, V_LNB + b:V_LNB + b + 1],
                               scale=vecs[:, V_LNG + b:V_LNG + b + 1]).then_inc(cs_done, 1)
                if b % 2:
                    act.wait_ge(cs_done, b + 1)
                    act.activation(ahi[:, b - 1:b + 1, :], csq[:, b - 1:b + 1, :], ACT.Copy).then_inc(ahi_done, 1)

            q = U_PW2 + 7
            split.to(q + 2)
            square_half(4, 0)
            hi_half(20, 0, vec(V_FFN + KT))
            split.to(q + 4)
            square_half(4, 1)
            hi_half(20, 1, vec(V_FFN + KT))
            root(4)
            for t in range(T):
                act.wait_ge(hf_done, t + 1)
                act.activation(hhi[:, t, :], hrow[:, t, :], ACT.Copy).then_inc(hhi_done, 1)
            act.wait_ge(r_step, 1)
            act.activation(small[:, 140:142], small[:, 138:140], ACT.Exp).then_inc(r_step, 1)

            def gather_hi(n, j):
                for b in range(2):
                    act.wait_ge(xe_ready, after(n + b + 1, 2, j))
                    act.activation(xehi[:, 4 * b:4 * b + 4, :],
                                   ps[:, 2 + b, :].rearrange("p (k n) -> p k n", k=4),
                                   ACT.Copy).then_inc(xehi_done, 1)

            gather_hi(0, None)
            split.to(U_MOE + 4)
            act.wait_ge(tab_done, 1)
            small_jobs, jobs = job_counts(act)
            with act.Fori(0, small_jobs) as j:
                def side(place, u):
                    if place == 2:
                        split.to(u + 8)
                        act.wait_ge(selT_ready, j + 1)
                        act.activation(selT[:, :], ps[:, 3, 0:S], ACT.Copy).then_inc(selT_done, 1)

                split.j, split.next = j, U_MOE + 4
                u = feed_forward(U_MOE, STEPS, 1, j, side)
                gather_hi(2, j)
                for half in range(2):
                    split.to(u + 6 + half)
                    act.wait_ge(unit_used, after(u + 2 * half + 2, JOB, j))
                    act.activation(ysb[:, half * CW:(half + 1) * CW], ps[:, 4 + 2 * half, :],
                                   ACT.Copy).then_inc(y_done, 1)
                split.to(U_MOE + JOB + 4)
            for half in range(2):
                hi_half(24, half, lambda kt: 1.0, 0)
            with act.If(small_jobs < jobs):
                with act.Fori(small_jobs, jobs) as j:
                    split.j, split.next = j, U_MOE + 4
                    feed_forward(U_MOE, STEPS, T, j, lambda place, u: None)
                    split.to(U_MOE + JOB + 4)
            split.j, split.next = jobs, U_MOE + 4
            act.wait_ge(pT_ready, 2)
            act.activation(pThi[:, :, :], ps[:, 0, :].rearrange("p (k n) -> p k n", k=2),
                           ACT.Copy).then_inc(pThi_done, 1)
            for half in range(2):
                hi_half(28, half, vec(V_PLEG + KT))
            for half in range(2):
                square_half(5, half)
            split.to(U_GATE1 + 4)
            root(5)
            embed_root(1, U_PROJ1, jobs)
            act.wait_ge(rstd_done, 5)
            for c in range(NO):
                split.to(U_END)
                gate_sigmoid(1, c, U_GATE1 + 4 * c + 3, jobs)

        @block.vector
        def _(dve):
            def split_lo(u, j):
                dve.wait_ge(hi_done, after(u + 1, JOB, j))
                dve.tensor_tensor(wlo[:, u % SPLIT, :], raw(u), whi[:, u % SPLIT, :].bitcast(F32),
                                  ALU.subtract).then_inc(lo_done, 1)

            split = Splitter(split_lo)
            own = Order(dve, dve_seq)

            def square_half(r, half):
                cols = slice(half * CW, (half + 1) * CW)
                dve.tensor_tensor_reduce(out=xn[:, 1, cols], in0=xres[:, 1, cols], in1=xres[:, 1, cols],
                                         scale=1.0, scalar=0.0, op0=ALU.mult, op1=ALU.add,
                                         accum_out=ssq[:, 2 * half + 1:2 * half + 2]).then_inc(ssq_d, 1)

            def root(r):
                dve.wait_ge(ssq_a, 2 * r)
                dve.wait_ge(ssq_d, 2 * r)
                dve.tensor_tensor(ssum, ssq[:, 0:2], ssq[:, 2:4], ALU.add).then_inc(sum_done, 1)
                dve.wait_ge(std_done, r)
                dve.reciprocal(rstd, std).then_inc(rstd_done, 1)
                dve.wait_ge(rstd_done, r)

            def lo_half(m, half, gain, banks=4):
                for b in range(2):
                    dve.wait_ge(ahi_done, 4 * m + 2 * half + b + 1)
                    for k in range(2):
                        kt = 4 * half + 2 * b + k
                        src = ps[:, banks + 2 * half + b, k * S:(k + 1) * S]
                        if gain is None:
                            ins = dve.tensor_tensor(alo[:, kt, :], src, ahi[:, kt, :].bitcast(F32), ALU.subtract)
                        else:
                            ins = dve.scalar_tensor_tensor(alo[:, kt, :], src, gain(kt),
                                                           ahi[:, kt, :].bitcast(F32), ALU.mult, ALU.subtract)
                    ins.then_inc(alo_done, 1)

            def add_half(half, q, banks, r):
                dve.wait_ge(unit_used, q + 1)
                cols = xres[:, :, half * CW:(half + 1) * CW]
                dve.tensor_tensor(cols, cols, ps[:, banks:banks + 2, :], ALU.add).then_inc(x_half, 1)
                dve.wait_ge(x_half, 2 * (r - 1) + half + 1)

            def vec(at):
                return lambda kt: vecs[:, at + kt:at + kt + 1]

            dve.memset(eps, EPS)
            own.step(dve.memset(lneps, LN_EPS))
            dve.wait_ge(x_in, 16 * T)
            dve.tensor_tensor_reduce(out=xn[:, 1, :], in0=xres[:, 1, :], in1=xres[:, 1, :], scale=1.0,
                                     scalar=0.0, op0=ALU.mult, op1=ALU.add,
                                     accum_out=ssum[:, 1:2]).then_inc(first_d, 1)
            dve.wait_ge(first_std, 1)
            own.step(dve.reciprocal(rstd, std))
            for t in range(T):
                dve.tensor_scalar(xn[:, t, :], xres[:, t, :], rstd[:, t:t + 1], None,
                                  ALU.mult).then_inc(xn_done, 1)
            dve.wait_ge(vecsT_ready, 1)
            dve.tensor_copy(vecs[:, 0:NV], ps[:, 0, 0:NV])
            own.step(dve.tensor_copy(taps[:, :].rearrange("p (a n) -> p a n", a=2),
                                     ps[:, 0, P:3 * P].rearrange("p (a n) -> p a n", a=2)[:, :, 0:TAPROWS]))
            own.step(dve.tensor_scalar(gsub, vecs[:, V_GSUB:V_GSUB + 1], 1.0 - LAM0, None, ALU.mult))
            dve.sem_inc(vecs_done, 1)

            for half in range(2):
                lo_half(0, half, vec(V_MIX))
            dve.wait_ge(late_in, 16 * N_LATE)
            own.step(dve.tensor_tensor(lamv[:, 0:4:2, :], lamv[:, 0:4:2, :], lamv[:, 1:4:2, :], ALU.mult))
            dve.reduce_sum(lamsum, lamv[:, 0:4:2, :], AX).then_inc(lam_part, 1)
            for c in range(NQKV):
                q = U_QKV + 4 * c + 3
                pair = ps[:, 2 * (c % 2):2 * (c % 2) + 2, :]
                split.to(q + 4)
                if c < 4:
                    groups = "p t (g n) -> p t g n"
                    h16 = hsq.rearrange("p (t g) -> p t g", t=T)
                    dve.wait_ge(qk_sq, c + 1)
                    dve.tensor_reduce(h16, xn[:, :, CW:D].rearrange(groups, n=HD), AX,
                                      ALU.add).then_inc(qk_ssq, 1)
                    dve.wait_ge(qk_std, c + 1)
                    own.step(dve.reciprocal(hrstd, hstd))
                    if c:
                        dve.wait_ge(qkT_ready, c)
                    for t in range(T):
                        ins = dve.tensor_tensor(
                            xn[:, t, 0:CW].rearrange("p (g n) -> p g n", n=HD),
                            pair[:, t, :].rearrange("p (g n) -> p g n", n=HD),
                            hrstd[:, 8 * t:8 * t + 8].unsqueeze(2).broadcast_to([P, 8, HD]), ALU.mult)
                        own.step(ins)
                    dve.sem_inc(qk_n, 1)
                    dve.sem_inc(chunk_free, 1)
                else:
                    dve.wait_ge(v_done, c - 3)
                    dve.sem_inc(chunk_free, 1)

            def maxima(h):
                dve.wait_ge(s_ready, h + 1)
                b = h % 3
                if h:
                    dve.wait_ge(max_done, h)
                scores = ps[:, 2 * (h % 2):2 * (h % 2) + 2, :]
                dve.reduce_max(mx[:, 0:2], scores[:, :, 0:P], AX)
                own.step(dve.reduce_max(mx[:, 2:4], scores[:, :, P:3 * P], AX))
                dve.tensor_scalar(nmx[:, 4 * b:4 * b + 4], mx, -HD ** -0.5, None, ALU.mult).then_inc(max_done, 1)

            maxima(0)
            maxima(1)
            dve.wait_ge(wr_done, 1)
            own.step(dve.tensor_tensor(wr2[:, :, NE:2 * NE], wr[:, :, :], wr2[:, :, 0:NE].bitcast(F32), ALU.subtract))
            dve.wait_ge(lam_part, 2)
            own.step(dve.tensor_tensor(neglam, lamexp[:, 1:2], lamexp[:, 0:1], ALU.subtract))
            own.step(dve.tensor_scalar(neglam, neglam, -LAM0, None, ALU.add))
            for h in range(H):
                b, b3 = h % 2, h % 3
                dve.wait_ge(exp_done, h + 1)
                if h:
                    dve.wait_ge(am_done, h)
                own.step(dve.reciprocal(pinv, psum_e[:, 4 * b3:4 * b3 + 4]))
                own.step(dve.tensor_scalar(pinv[:, 1:4:2], pinv[:, 1:4:2], neglam, None, ALU.mult))
                if h >= 2:
                    dve.wait_ge(amT_ready, h - 1)
                parts = (slice(0, P), slice(P, 3 * P))
                for t in range(T):
                    n = own.add(dve.tensor_scalar(amix[:, b, parts[t]], prob[:, b3, 0, parts[t]],
                                                  pinv[:, 2 * t:2 * t + 1], None, ALU.mult))
                own.wait(n)
                for t in range(T):
                    ins = dve.scalar_tensor_tensor(amix[:, b, parts[t]], prob[:, b3, 1, parts[t]],
                                                   pinv[:, 2 * t + 1:2 * t + 2],
                                                   amix[:, b, parts[t]], ALU.mult, ALU.add)
                ins.then_inc(am_done, 1)
                if h + 2 < H:
                    maxima(h + 2)
            split.to(U_WO + 4)
            dve.wait_ge(on_step, 1)
            own.step(dve.reciprocal(hrstd, hstd))
            for half in range(2):
                for t in range(T):
                    o4 = xn[:, t, half * CW:(half + 1) * CW].rearrange("p (h n) -> p h n", n=P)
                    at = t * H + 4 * half
                    ins = dve.tensor_tensor(o4, o4, hrstd[:, at:at + 4].unsqueeze(2).broadcast_to([P, 4, P]),
                                            ALU.mult)
                ins.then_inc(on_step, 1)
            for half in range(2):
                lo_half(1, half, lambda kt: gsub)
            q = U_WO + 3
            split.to(q + 4)
            add_half(0, q, 0, 1)
            dve.sem_inc(chunk_free, 1)
            square_half(1, 0)
            q += 4
            split.to(q + 2)
            lo_half(2, 0, vec(V_FFN))
            split.to(q + 4)
            add_half(1, q, 2, 1)
            dve.sem_inc(chunk_free, 1)
            square_half(1, 1)
            split.to(q + 6)
            lo_half(2, 1, vec(V_FFN))

            def feed_forward(u0, n0, tiles, j, side):
                u, up = u0, 2 // (3 - tiles)

                def hidden(n):
                    dve.wait_ge(silu_done, after(n, STEPS, j))
                    if n > 1:
                        dve.wait_ge(hT_ready, after(n - 1, STEPS, j))
                    if j is not None:
                        ins = dve.tensor_tensor(hid[:, 0:tiles, :], sg[:, 0:tiles, :], ps[:, up:up + tiles, :],
                                                ALU.mult)
                    else:
                        for t in range(tiles):
                            ins = dve.scalar_tensor_tensor(hid[:, t, :], ps[:, up + t, :], rstd[:, t:t + 1],
                                                           sg[:, t, :], ALU.mult, ALU.mult)
                    ins.then_inc(h_done, 1)

                def hidden_lo(n):
                    dve.wait_ge(hThi_done, after(n, STEPS, j))
                    dve.tensor_tensor(hTlo[:, 0:tiles, :], ps[:, up:up + tiles, :],
                                      hThi[:, 0:tiles, :].bitcast(F32), ALU.subtract).then_inc(hTlo_done, 1)

                for s in range(STEPS):
                    n = n0 + s
                    if s:
                        split.to(u + 3)
                        dve.wait_ge(unit_used, after(u, JOB, j))
                        hidden(n)
                        split.to(u + 5)
                        hidden_lo(n)
                    side(s, u + 4)
                    u += 12 if s else 8
                split.to(u + 3)
                dve.wait_ge(unit_used, after(u, JOB, j))
                hidden(n0 + STEPS)
                split.to(u + 4)
                hidden_lo(n0 + STEPS)
                return u

            dve.wait_ge(pThi_done, 1)
            dve.tensor_tensor(pTlo[:, :, :], ps[:, 4, :].rearrange("p (k n) -> p k n", k=2),
                              pThi[:, :, :].bitcast(F32), ALU.subtract).then_inc(pTlo_done, 1)
            root(1)
            feed_forward(U_FFN, 0, T, None, lambda place, u: None)

            def embed_norm(i):
                dve.wait_ge(e_std, i + 1)
                own.step(dve.reciprocal(hrstd[:, 0:2], hstd[:, 0:2]))
                for t in range(T):
                    n = own.add(dve.scalar_tensor_tensor(
                        emb[:, t, :], ps[:, 2 * t:2 * t + 2, :].rearrange("p b n -> p (b n)"),
                        hrstd[:, t:t + 1], gbc[:, :], ALU.mult, ALU.mult))
                own.wait(n)
                dve.sem_inc(e_done, 1)

            def gated_add(i, c, r):
                cols = slice(c * CW, (c + 1) * CW)
                for t in range(T):
                    dve.wait_ge(sgm_done, 4 * i + 2 * c + t + 1)
                    own.step(dve.tensor_tensor(emb[:, t, cols], emb[:, t, cols], sgm[:, t, :], ALU.mult))
                    if t == T - 1:
                        dve.sem_inc(chunk_free, 1)
                    ins = dve.tensor_tensor(xres[:, t, cols], xres[:, t, cols], emb[:, t, cols], ALU.add)
                    if i:
                        ins.then_inc(out_ready, 1)
                    else:
                        n = own.add(ins)
                if not i:
                    own.wait(n)
                    dve.sem_inc(x_half, 1)
                    dve.wait_ge(x_half, 2 * (r - 1) + c + 1)

            split.to(U_PROJ0 + 5)
            embed_norm(0)
            q = U_GATE0 - 1
            split.to(q + 2)
            add_half(0, q - 2, 4, 2)
            square_half(2, 0)
            split.to(q + 3)
            lo_half(3, 0, vec(V_PLEG))
            split.to(q + 4)
            add_half(1, q, 6, 2)
            square_half(2, 1)
            split.to(q + 6)
            lo_half(3, 1, vec(V_PLEG))
            root(2)
            q = U_GATE0 + 3
            split.to(q + 4)
            gated_add(0, 0, 3)
            square_half(3, 0)
            split.to(q + 6)
            lo_half(4, 0, vec(V_MIX + KT))
            q += 4
            split.to(q + 4)
            gated_add(0, 1, 3)
            square_half(3, 1)

            split.to(q + 6)
            lo_half(4, 1, vec(V_MIX + KT))
            root(3)
            for t in range(T):
                n = own.add(dve.tensor_scalar(xn[:, 0, S + t * P:S + (t + 1) * P], ident[:, :], rstd[:, t:t + 1],
                                              None, ALU.mult))
            own.wait(n)
            dve.sem_inc(rdiag_done, 1)
            own.step(dve.memset(cT[:, :, 0:TAPS - 1], 0.0))

            def glu_scale(cc):
                dve.wait_ge(unit_used, U_PW1 + 8 * cc + 8)
                rbc = xn[:, 1:2, S:2 * S].broadcast_to([P, 4, S])
                dve.tensor_tensor(csq[:, 0:4, :], ps[:, 2:4, :].rearrange("p b (a n) -> p (b a) n", n=S), rbc,
                                  ALU.mult).then_inc(glu_in, 1)
                own.step(dve.tensor_tensor(csq[:, 4:8, :], ps[:, 0:2, :].rearrange("p b (a n) -> p (b a) n", n=S),
                                           rbc, ALU.mult))
                dve.wait_ge(glu_in, cc + 1)
                dve.sem_inc(chunk_free, 2)

            def glu(cc):
                dve.wait_ge(glu_sig, cc + 1)
                for b in range(4):
                    ch = 4 * cc + b
                    n = own.add(dve.scalar_tensor_tensor(
                        cT[:, ch, TAPS - 1:TAPS - 1 + S], csq[:, 4 + b, :],
                        vecs[:, V_BPW1 + ch:V_BPW1 + ch + 1], csq[:, b, :], ALU.add, ALU.mult))
                own.wait(n)
                dve.sem_inc(glu_done, 1)

            split.to(U_PW1 + 7 + 4)
            dve.wait_ge(rbc_done, 1)
            glu_scale(0)
            glu(0)
            split.to(U_PW1 + 15 + 4)
            glu_scale(1)
            split.to(U_PW2 + 4)
            glu(1)
            last_of = {}
            for k in range(TAPS):
                for ch in DVE_BLOCKS:
                    src, w = cT[:, ch, k:k + S], taps[:, k * KT + ch:k * KT + ch + 1]
                    if k == 0:
                        last_of[ch] = own.add(dve.tensor_scalar(
                            cy[:, ch, :], src, w, vecs[:, V_BDW + ch:V_BDW + ch + 1], ALU.mult, ALU.add))
                        continue
                    own.wait(last_of[ch])
                    ins = dve.scalar_tensor_tensor(cy[:, ch, :], src, w, cy[:, ch, :], ALU.mult, ALU.add)
                    if k < TAPS - 1:
                        last_of[ch] = own.add(ins)
                    else:
                        ins.then_inc(conv_done, 1)
            dve.wait_ge(mean_done, 1)
            for b in range(2):
                dve.tensor_tensor(cy[:, 4 * b:4 * b + 4, :], cy[:, 4 * b:4 * b + 4, :],
                                  xn[:, 0:1, 0:S].broadcast_to([P, 4, S]), ALU.subtract).then_inc(cent_done, 1)
            dve.wait_ge(cstd_done, 1)
            own.step(dve.reciprocal(xn[:, 1, 0:S], xn[:, 0, CW:CW + S]))
            for b in range(4):
                dve.tensor_tensor(cy[:, 2 * b:2 * b + 2, :], cy[:, 2 * b:2 * b + 2, :],
                                  xn[:, 1:2, 0:S].broadcast_to([P, 2, S]), ALU.mult).then_inc(cn_done, 1)
            for b in range(4):
                dve.wait_ge(ahi_done, 20 + b + 1)
                dve.tensor_tensor(alo[:, 2 * b:2 * b + 2, :], csq[:, 2 * b:2 * b + 2, :],
                                  ahi[:, 2 * b:2 * b + 2, :].bitcast(F32), ALU.subtract).then_inc(alo_done, 1)
            dve.wait_ge(b_in, 16)
            for t in range(T):
                row4 = xres[:, t, :].rearrange("p (a n) -> p a n", a=4)
                n = own.add(dve.tensor_tensor(row4, row4, cT[:, 0:4, 0:2 * P], ALU.add))
            own.wait(n)
            q = U_PW2 + 3
            split.to(q + 4)
            add_half(0, q, 0, 4)
            dve.sem_inc(chunk_free, 1)
            square_half(4, 0)
            q += 4
            split.to(q + 2)
            lo_half(6, 0, vec(V_FFN + KT))
            split.to(q + 4)
            add_half(1, q, 2, 4)
            dve.sem_inc(chunk_free, 1)
            square_half(4, 1)
            lo_half(6, 1, vec(V_FFN + KT))
            root(4)
            dve.wait_ge(g_in, 16)
            for t in range(T):
                dve.scalar_tensor_tensor(hrow[:, t, :], xres[:, t, :], rstd[:, t:t + 1], ysb[:, :],
                                         ALU.mult, ALU.mult).then_inc(hf_done, 1)

            m12, g12 = small[:, 128:132], small[:, 132:136]
            pick = small[:, 112:128].rearrange("p (t e) -> p t e", t=T)
            tmp = selT[:, :].rearrange("p (i n) -> p i n", n=16)
            e3 = lambda i: tmp[:, i, :].rearrange("p (t e) -> p t e", t=T)
            back, oh1, oh2, cand, l2 = e3(0), e3(1), e3(2), e3(3), e3(4)
            row = lambda v: v.unsqueeze(2).broadcast_to([P, T, NE])
            iota8 = iota[:, 0:NE].unsqueeze(1).broadcast_to([P, T, NE])
            dve.wait_ge(log_ready, 1)
            own.step(dve.tensor_scalar(back, iota8, -1.0, float(NE), ALU.mult, ALU.add))
            for part in range(2):
                for t in range(T):
                    at = (2 * t + part) * NE
                    n = own.add(dve.scalar_tensor_tensor(logits[:, t, :], ps[:, 0, at:at + NE], rstd[:, t:t + 1],
                                                         logits[:, t, :] if part else rbias[:, :],
                                                         ALU.mult, ALU.add))
                own.wait(n)

            def top(src, mval, hot):
                own.step(dve.reduce_max(mval, src, AX))
                own.step(dve.tensor_tensor(cand, src, row(mval), ALU.is_equal))
                own.step(dve.tensor_tensor(cand, cand, back, ALU.mult))
                own.step(dve.reduce_max(g12[:, 0:2], cand, AX))
                own.step(dve.tensor_tensor(hot, back, row(g12[:, 0:2]), ALU.is_equal))

            top(logits, m12[:, 0:2], oh1)
            own.step(dve.scalar_tensor_tensor(l2, oh1, -3e38, logits, ALU.mult, ALU.add))
            top(l2, m12[:, 2:4], oh2)
            own.step(dve.tensor_tensor(pick, oh1, oh2, ALU.add))
            dve.sem_inc(rm_done, 1)
            dve.tensor_tensor(small[:, 138:140], m12[:, 2:4], m12[:, 0:2], ALU.subtract).then_inc(r_step, 1)
            for t in range(T):
                dve.wait_ge(hhi_done, t + 1)
                dve.tensor_tensor(hlo[:, t, :], hrow[:, t, :], hhi[:, t, :].bitcast(F32),
                                  ALU.subtract).then_inc(hlo_done, 1)
            dve.wait_ge(r_step, 2)
            own.step(dve.tensor_scalar(g12[:, 0:2], small[:, 140:142], 1.0, None, ALU.add))
            own.step(dve.reciprocal(g12[:, 0:2], g12[:, 0:2]))
            own.step(dve.tensor_tensor(g12[:, 2:4], g12[:, 0:2], small[:, 140:142], ALU.mult))
            own.step(dve.tensor_tensor(oh1, oh1, row(g12[:, 0:2]), ALU.mult))
            own.step(dve.tensor_tensor(oh2, oh2, row(g12[:, 2:4]), ALU.mult))
            pos8, gate8 = e3(10), e3(11)
            own.step(dve.tensor_tensor(gate8, oh1, oh2, ALU.add))
            FAR = 10000.0
            dve.wait_ge(cnt_ready, 1)
            own.step(dve.tensor_scalar(pos8, ps[:, 1, 0:2 * NE].rearrange("p (t e) -> p t e", t=T), FAR, None, ALU.add))
            own.step(dve.tensor_tensor(pos8, pos8, pick, ALU.mult))
            own.step(dve.tensor_scalar(pos8, pos8, -FAR, None, ALU.add))
            dve.tensor_copy(jgate[:, :, 0:1], gate8[:, :, 0:1])
            own.step(dve.tensor_copy(jpos[:, :, 0:1], pos8[:, :, 0:1]))

            def one_hot(col):
                for t in range(T):
                    dve.tensor_scalar(sel[:, t, :], iota[:, :], jpos[:, t, col], None, ALU.is_equal)
                    ins = dve.tensor_scalar(selg[:, t, :], iota[:, :], jpos[:, t, col], jgate[:, t, col],
                                            ALU.is_equal, ALU.mult)
                ins.then_inc(sel_done, 1)

            one_hot(slice(0, 1))
            over, full, upto, shift, before, column = (tmp[:, 5 + i, 0:NE] for i in (0, 1, 2, 3, 7, 8))
            trow = tmp[:, 14, :]
            iota_e, over0, n_small = iota[:, 0:NE], over[:, 0:1], trow[:, NCOL:NCOL + 1]
            rest = tmp[:, 15, 0:1]
            own.step(dve.tensor_scalar(over, ps[:, 1, 2 * NE:3 * NE], P + 0.5, None, ALU.is_gt))
            own.step(dve.memset(trow, 0.0))
            own.step(dve.tensor_copy(full, over))
            own.step(dve.memset(full[:, 0:1], 0.0))
            own.step(dve.tensor_copy(upto, full))
            for d in (1, 2, 4):
                own.step(dve.tensor_copy(shift, upto))
                own.step(dve.tensor_tensor(upto[:, d:NE], shift[:, d:NE], shift[:, 0:NE - d], ALU.add))
            own.step(dve.tensor_tensor(before, upto, full, ALU.subtract))
            own.step(dve.tensor_scalar(rest, upto[:, NE - 1:NE], -1.0, float(NE), ALU.mult, ALU.add))
            own.step(dve.tensor_tensor(n_small, rest, over0, ALU.add))
            own.step(dve.tensor_scalar(trow[:, NCOL + 1:NCOL + 2], over0, float(NE), None, ALU.add))
            own.step(dve.scalar_tensor_tensor(rest, rest, 1.0, over0, ALU.add, ALU.mult))
            own.step(dve.tensor_scalar(rest, rest, -1.0, None, ALU.add))
            own.step(dve.scalar_tensor_tensor(column, before, 2.0, iota_e, ALU.mult, ALU.subtract))
            own.step(dve.scalar_tensor_tensor(column, column, n_small, full, ALU.add, ALU.mult))
            own.step(dve.tensor_tensor(column, column, before, ALU.subtract))
            own.step(dve.tensor_tensor(column, column, iota_e, ALU.add))
            dve.wait_ge(hf_done, T)
            NJ = NCOL - 1
            grid = lambda i: ysb[:, i * P:i * P + NJ * NE].rearrange("p (c e) -> p c e", e=NE)
            by_expert = lambda v: v.unsqueeze(1).broadcast_to([P, NJ, NE])
            hot, is_rest = grid(0), ysb[:, P - NJ:P]
            own.step(dve.tensor_tensor(hot, iota[:, 1:NCOL].unsqueeze(2).broadcast_to([P, NJ, NE]),
                                       by_expert(column), ALU.is_equal))
            own.step(dve.tensor_scalar(is_rest, iota[:, 1:NCOL], rest, None, ALU.is_equal))
            rows_of = [(iota_e, trow[:, 1:NCOL])]
            for t in range(T):
                rows_of += [(pos8[:, t, :], jpos[:, t, 1:NCOL]), (gate8[:, t, :], jgate[:, t, 1:NCOL])]
            for i, (v, _) in enumerate(rows_of):
                n = own.add(dve.tensor_tensor(grid(1 + i), hot, by_expert(v), ALU.mult))
            own.wait(n)
            for i, (_, dst) in enumerate(rows_of):
                n = own.add(dve.reduce_sum(dst, grid(1 + i), AX))
            own.wait(n)
            for t in range(T):
                own.step(dve.tensor_scalar(rest, pos8[:, t, 0:1], -float(P), None, ALU.add))
                own.step(dve.scalar_tensor_tensor(jpos[:, t, 1:NCOL], is_rest, rest, jpos[:, t, 1:NCOL],
                                                  ALU.mult, ALU.add))
                own.step(dve.scalar_tensor_tensor(jgate[:, t, 1:NCOL], is_rest, gate8[:, t, 0:1],
                                                  jgate[:, t, 1:NCOL], ALU.mult, ALU.add))
            own.step(dve.tensor_copy(jtab[0:1, :], trow[0:1, :]))
            dve.sem_inc(tab_done, 1)

            def gather_lo(n, j):
                for b in range(2):
                    dve.wait_ge(xehi_done, after(n + b + 1, 2, j))
                    dve.tensor_tensor(xelo[:, 4 * b:4 * b + 4, :],
                                      ps[:, 2 + b, :].rearrange("p (k n) -> p k n", k=4),
                                      xehi[:, 4 * b:4 * b + 4, :].bitcast(F32),
                                      ALU.subtract).then_inc(xelo_done, 1)

            gather_lo(0, None)
            small_jobs, jobs = job_counts(dve)
            split.to(U_MOE + 4)
            with dve.Fori(0, small_jobs) as j:
                def side(place, u):
                    if place == 3:
                        dve.wait_ge(selT_ready, j + 1)
                        one_hot(bass.ds(j + 1, 1))

                split.j, split.next = j, U_MOE + 4
                u = feed_forward(U_MOE, STEPS, 1, j, side)
                gather_lo(2, j)
                for k in range(4):
                    half, t = k // 2, k % 2
                    if k != 1:
                        split.to(u + (6, 6, 7, 8)[k])
                    dve.wait_ge(sc_ready, 4 * j + k + 1)
                    cols = xres[:, t, half * CW:(half + 1) * CW]
                    dve.tensor_tensor(cols, cols, ps[:, 5 + 2 * t, :], ALU.add).then_inc(sc_done, 1)
            dve.wait_ge(xe_ready, 2 * small_jobs + 2)
            for t in range(T):
                dve.tensor_tensor(xn[:, t, :], hhi[:, t, :].bitcast(F32), hlo[:, t, :].bitcast(F32),
                                  ALU.add).then_inc(hf_done, 1)
            dve.wait_ge(hf_done, 2 * T)
            for half in range(2):
                lo_half(7, half, None, 0)
            with dve.If(small_jobs < jobs):
                with dve.Fori(small_jobs, jobs) as j:
                    split.j, split.next = j, U_MOE + 4
                    u = feed_forward(U_MOE, STEPS, T, j, lambda place, u: None)
                    for half in range(2):
                        split.to(u + 2 * half + 5)
                        dve.wait_ge(unit_used, after(u + 2 * half + 2, JOB, j))
                        for t in range(T):
                            cols = xres[:, t, half * CW:(half + 1) * CW]
                            dve.scalar_tensor_tensor(cols, ps[:, 4 + 2 * half + t, :], jgate[:, t, bass.ds(j, 1)],
                                                     cols, ALU.mult, ALU.add).then_inc(sc_done, 1)
                    split.to(U_MOE + JOB + 4)
            split.j, split.next = jobs, U_MOE + 4
            dve.wait_ge(sc_done, jobs * 4)
            dve.sem_inc(x_half, 2)
            dve.wait_ge(pThi_done, 2)
            dve.tensor_tensor(pTlo[:, :, :], ps[:, 0, :].rearrange("p (k n) -> p k n", k=2),
                              pThi[:, :, :].bitcast(F32), ALU.subtract).then_inc(pTlo_done, 1)
            for half in range(2):
                lo_half(8, half, vec(V_PLEG + KT))
            for half in range(2):
                square_half(5, half)
            split.to(U_GATE1 + 4)
            root(5)
            embed_norm(1)
            for c in range(NO):
                split.to(U_END)
                gated_add(1, c, 6)


INPUTS = ["x", "p", "mix_norm_g", "ffn_norm_g", "attn_w_qkv", "attn_w_o", "attn_g_q", "attn_g_k",
          "attn_lam_q1", "attn_lam_k1", "attn_lam_q2", "attn_lam_k2", "attn_g_sub",
          "conv_w_pw1", "conv_b_pw1", "conv_w_dw", "conv_b_dw", "conv_ln_g", "conv_ln_b",
          "conv_w_pw2", "conv_b_pw2", "ffn_w_gate", "ffn_w_up", "ffn_w_down",
          "moe_w_router", "moe_b_router", "moe_w_gate", "moe_w_up", "moe_w_down",
          "ple_w_proj", "ple_norm_g", "ple_gate_norm_g", "ple_w_gate"]


def kernel(**inputs):
    import numpy as np
    import concourse.bacc as bacc
    from concourse.bass_utils import run_bass_kernel_spmd

    nc = bacc.Bacc("TRN2", target_bir_lowering=False, num_devices=1)
    arrays, args = {}, []
    for name in INPUTS:
        a = np.ascontiguousarray(inputs[name])
        arrays[f"in_{name}"] = a
        args.append(nc.dram_tensor(f"in_{name}", a.shape, mybir.dt.from_np(a.dtype), kind="ExternalInput").ap())
    args.append(nc.dram_tensor("out", inputs["x"].shape, F32, kind="ExternalOutput").ap())
    program(nc, *args)
    result = run_bass_kernel_spmd(nc, [arrays], core_ids=[0])
    return result.results[0]["out"]
```
